# Optimizing a Trainium2 kernel written in Bass

```python
import math
import jax, jax.numpy as jnp
from jax import lax
import numpy as np

D_MODEL = 1024
BATCH = 1
SEQ = 1024
DEPTH = 2

NORM_EPS = 1e-6
D_FF = 4 * D_MODEL
QBLK = 128
NEG_INF = -1e30
FORCE_SCORE = 1e4

NUM_BUCKETS = 32
MAX_DISTANCE = 1024

LRU_WIDTH = D_MODEL // 2
LRU_BLOCKS = 8
LRU_BLOCK_DIM = LRU_WIDTH // LRU_BLOCKS
CONV_WIDTH = 4
LRU_C = 8.0

MLA_HEADS = 8
MLA_NOPE = 64
MLA_ROPE = 32
MLA_QK = MLA_NOPE + MLA_ROPE
MLA_V = 64
MLA_Q_RANK = 384
MLA_KV_RANK = 256
ROPE_THETA = 10000.0

HY_SPLITS = (LRU_WIDTH, LRU_WIDTH, MLA_Q_RANK, MLA_KV_RANK, MLA_ROPE)
HY_IN = sum(HY_SPLITS)
HY_OUT = LRU_WIDTH + MLA_HEADS * MLA_V

NSA_HEADS = 16
NSA_GROUPS = 2
NSA_HPG = NSA_HEADS // NSA_GROUPS
NSA_DK = 64
NSA_DV = 64
NSA_KV = NSA_GROUPS * NSA_DK
CMP_BLOCK = 32
CMP_STRIDE = 16
CMP_HIDDEN = 256
SLC_BLOCK = 64
SLC_TOPN = 8
WINDOW = 512
NSA_SPLITS = (NSA_HEADS * NSA_DK,) + (NSA_KV,) * 6 + (3 * NSA_HEADS,)
NSA_IN = sum(NSA_SPLITS)
NSA_OUT = NSA_HEADS * NSA_DV

N_EVEN = (DEPTH + 1) // 2
N_ODD = DEPTH // 2

kernel_name = 'hybrid_rglru_mla_nsa_trunk'

def rms_norm(x, g):
    xf = x.astype(jnp.float32)
    y = xf * lax.rsqrt(jnp.mean(xf * xf, axis=-1, keepdims=True) + NORM_EPS)
    return (y * g.astype(jnp.float32)).astype(x.dtype)

def split_cols(z, sizes):
    out, off = [], 0
    for s in sizes:
        out.append(z[..., off:off + s])
        off += s
    return out

def t5_bucket(dist):
    n = jnp.maximum(dist, 0)
    max_exact = NUM_BUCKETS // 2
    nf = jnp.maximum(n, 1).astype(jnp.float32)
    large = max_exact + (jnp.log(nf / max_exact) / math.log(MAX_DISTANCE / max_exact)
                         * (NUM_BUCKETS - max_exact)).astype(jnp.int32)
    large = jnp.minimum(large, NUM_BUCKETS - 1)
    return jnp.where(n < max_exact, n, large)

def apply_rope(x, pos):
    half = x.shape[-1] // 2
    freqs = ROPE_THETA ** (-jnp.arange(half, dtype=jnp.float32) / half)
    ang = pos.astype(jnp.float32)[:, None] * freqs[None, :]
    cos = jnp.cos(ang)[None, :, None, :]
    sin = jnp.sin(ang)[None, :, None, :]
    xf = x.astype(jnp.float32)
    x1, x2 = xf[..., :half], xf[..., half:]
    return jnp.concatenate([x1 * cos - x2 * sin, x2 * cos + x1 * sin], axis=-1).astype(x.dtype)

def causal_depthwise_conv(x, w, b):
    S = x.shape[1]
    xp = jnp.pad(x, ((0, 0), (CONV_WIDTH - 1, 0), (0, 0)))
    y = xp[:, 0:S] * w[0]
    for k in range(1, CONV_WIDTH):
        y = y + xp[:, k:k + S] * w[k]
    return y + b

def rg_lru(x, wa, ba, wx, bx, lam):
    B, S, C = x.shape
    xb = x.reshape(B, S, LRU_BLOCKS, LRU_BLOCK_DIM)
    r = jax.nn.sigmoid(jnp.einsum('bsnd,nde->bsne', xb, wa) + ba).reshape(B, S, C)
    i = jax.nn.sigmoid(jnp.einsum('bsnd,nde->bsne', xb, wx) + bx).reshape(B, S, C)
    log_a = -LRU_C * r.astype(jnp.float32) * jax.nn.softplus(-lam.astype(jnp.float32))
    a = jnp.exp(log_a)
    mult = jnp.sqrt(-jnp.expm1(2.0 * log_a))
    mult = mult.at[:, 0].set(1.0)
    b_in = mult * (i * x).astype(jnp.float32)

    def combine(lhs, rhs):
        a1, b1 = lhs
        a2, b2 = rhs
        return a1 * a2, a2 * b1 + b2

    _, h = lax.associative_scan(combine, (a, b_in), axis=1)
    return h.astype(x.dtype)

def causal_block_attention(q, k, v):
    B, H, S, dk = q.shape
    dv = v.shape[-1]
    nb = S // QBLK
    scale = dk ** -0.5
    qb = q.reshape(B, H, nb, QBLK, dk).transpose(2, 0, 1, 3, 4)
    kpos = jnp.arange(S)

    def body(args):
        qi, blk = args
        qpos = blk * QBLK + jnp.arange(QBLK)
        s = jnp.einsum('bhqd,bhkd->bhqk', qi, k).astype(jnp.float32) * scale
        s = jnp.where(kpos[None, :] <= qpos[:, None], s, NEG_INF)
        p = jax.nn.softmax(s, axis=-1).astype(v.dtype)
        return jnp.einsum('bhqk,bhkd->bhqd', p, v)

    o = lax.map(body, (qb, jnp.arange(nb)))
    return o.transpose(1, 0, 3, 2, 4).reshape(B, S, H * dv)

def hybrid_mixer(u, w_in, conv_w, conv_b, wa, ba, wx, bx, lam,
                 q_norm, kv_norm, w_uq, w_ukv, qn_q, qn_k, w_out):
    B, S, _ = u.shape
    pos = jnp.arange(S)
    z = u @ w_in
    xr, xg, q_lat, kv_lat, k_rope = split_cols(z, HY_SPLITS)
    lru = rg_lru(causal_depthwise_conv(xr, conv_w, conv_b), wa, ba, wx, bx, lam)
    lru = lru * jax.nn.gelu(xg)
    q = (rms_norm(q_lat, q_norm) @ w_uq).reshape(B, S, MLA_HEADS, MLA_QK)
    kv = (rms_norm(kv_lat, kv_norm) @ w_ukv).reshape(B, S, MLA_HEADS, MLA_NOPE + MLA_V)
    k_nope, v = kv[..., :MLA_NOPE], kv[..., MLA_NOPE:]
    k_r = jnp.broadcast_to(k_rope[:, :, None, :], (B, S, MLA_HEADS, MLA_ROPE))
    k = jnp.concatenate([k_nope, k_r], axis=-1)
    q = rms_norm(q, qn_q)
    k = rms_norm(k, qn_k)
    q = jnp.concatenate([q[..., :MLA_NOPE], apply_rope(q[..., MLA_NOPE:], pos)], axis=-1)
    k = jnp.concatenate([k[..., :MLA_NOPE], apply_rope(k[..., MLA_NOPE:], pos)], axis=-1)
    mla = causal_block_attention(q.transpose(0, 2, 1, 3), k.transpose(0, 2, 1, 3),
                                 v.transpose(0, 2, 1, 3))
    return jnp.concatenate([lru, mla], axis=-1) @ w_out

def nsa_mixer(u, w_in, pos_k, w1_k, w2_k, pos_v, w1_v, w2_v, q_norm, k_norm, rel_bias, w_out):
    B, S, _ = u.shape
    G, HPG, DK, DV = NSA_GROUPS, NSA_HPG, NSA_DK, NSA_DV
    z = u @ w_in
    q, kc, vc, ks, vs, kw, vw, gate = split_cols(z, NSA_SPLITS)
    q = rms_norm(q.reshape(B, S, NSA_HEADS, DK), q_norm).reshape(B, S, G, HPG, DK)
    gate = jax.nn.sigmoid(gate).reshape(B, S, NSA_HEADS, 3)

    nc = (S - CMP_BLOCK) // CMP_STRIDE + 1
    cstart = jnp.arange(nc) * CMP_STRIDE
    cend = cstart + CMP_BLOCK - 1
    cidx = cstart[:, None] + jnp.arange(CMP_BLOCK)[None, :]

    def compress(t, pos_emb, w1, w2):
        t = t.reshape(B, S, G, DK)[:, cidx]
        t = t + pos_emb[None, None, :, None, :]
        t = t.transpose(0, 1, 3, 2, 4).reshape(B, nc, G, CMP_BLOCK * DK)
        return jax.nn.gelu(t @ w1) @ w2

    ck = rms_norm(compress(kc, pos_k, w1_k, w2_k), k_norm[0])
    cv = compress(vc, pos_v, w1_v, w2_v)

    nsel = S // SLC_BLOCK
    n_top = min(SLC_TOPN, nsel)
    kb = rms_norm(ks.reshape(B, S, G, DK), k_norm[1]).reshape(B, nsel, SLC_BLOCK, G, DK).transpose(0, 3, 1, 2, 4)
    vb = vs.reshape(B, nsel, SLC_BLOCK, G, DV).transpose(0, 3, 1, 2, 4)
    sstart = jnp.arange(nsel) * SLC_BLOCK
    ov = jnp.clip(jnp.minimum(cstart[:, None] + CMP_BLOCK, sstart[None, :] + SLC_BLOCK)
                  - jnp.maximum(cstart[:, None], sstart[None, :]), 0, None).astype(jnp.float32) / CMP_BLOCK

    kw_pad = jnp.pad(rms_norm(kw.reshape(B, S, G, DK), k_norm[2]), ((0, 0), (WINDOW, 0), (0, 0), (0, 0)))
    vw_pad = jnp.pad(vw.reshape(B, S, G, DV), ((0, 0), (WINDOW, 0), (0, 0), (0, 0)))

    tab = rel_bias.reshape(NUM_BUCKETS, G, HPG)
    tab_g = tab.transpose(1, 0, 2)
    scale = DK ** -0.5
    nb = S // QBLK
    qb = q.reshape(B, nb, QBLK, G, HPG, DK).transpose(1, 0, 2, 3, 4, 5)
    bi = jnp.arange(B)[:, None, None, None]
    gi = jnp.arange(G)[None, :, None, None]
    blk_id = jnp.arange(nsel)

    def block(args):
        qi, blk = args
        q0 = blk * QBLK
        qpos = q0 + jnp.arange(QBLK)
        s = jnp.einsum('bqghd,bngd->bghqn', qi, ck).astype(jnp.float32) * scale
        s = s + tab[t5_bucket(qpos[:, None] - cend[None, :])].transpose(2, 3, 0, 1)
        valid_c = cend[None, :] <= qpos[:, None]
        s = jnp.where(valid_c, s, NEG_INF)
        p_c = jax.nn.softmax(s, axis=-1) * jnp.any(valid_c, axis=-1)[:, None]
        o_c = jnp.einsum('bghqn,bngd->bqghd', p_c.astype(cv.dtype), cv)
        imp = jnp.einsum('bghqn,nm->bgqm', p_c, ov)
        cur = qpos // SLC_BLOCK
        valid_s = sstart[None, :] <= qpos[:, None]
        forced = (blk_id[None, :] == 0) | (blk_id[None, :] == cur[:, None]) | (blk_id[None, :] == cur[:, None] - 1)
        score = jnp.where(valid_s & forced, FORCE_SCORE, jnp.where(valid_s, imp, -1.0))
        _, idx = lax.top_k(score, n_top)
        k_sel = kb[bi, gi, idx].reshape(B, G, QBLK, n_top * SLC_BLOCK, DK)
        v_sel = vb[bi, gi, idx].reshape(B, G, QBLK, n_top * SLC_BLOCK, DV)
        kpos = (idx[..., None] * SLC_BLOCK + jnp.arange(SLC_BLOCK)).reshape(B, G, QBLK, n_top * SLC_BLOCK)
        dist = qpos[None, None, :, None] - kpos
        s = jnp.einsum('bqghd,bgqkd->bghqk', qi, k_sel).astype(jnp.float32) * scale
        s = s + tab_g[gi, t5_bucket(dist)].transpose(0, 1, 4, 2, 3)
        s = jnp.where((dist >= 0)[:, :, None], s, NEG_INF)
        p_s = jax.nn.softmax(s, axis=-1).astype(v_sel.dtype)
        o_s = jnp.einsum('bghqk,bgqkd->bqghd', p_s, v_sel)
        k_win = lax.dynamic_slice_in_dim(kw_pad, q0, WINDOW + QBLK, axis=1)
        v_win = lax.dynamic_slice_in_dim(vw_pad, q0, WINDOW + QBLK, axis=1)
        wpos = q0 - WINDOW + jnp.arange(WINDOW + QBLK)
        wdist = qpos[:, None] - wpos[None, :]
        wmask = (wdist >= 0) & (wdist < WINDOW) & (wpos[None, :] >= 0)
        s = jnp.einsum('bqghd,bkgd->bghqk', qi, k_win).astype(jnp.float32) * scale
        s = s + tab[t5_bucket(wdist)].transpose(2, 3, 0, 1)
        s = jnp.where(wmask, s, NEG_INF)
        p_w = jax.nn.softmax(s, axis=-1).astype(v_win.dtype)
        o_w = jnp.einsum('bghqk,bkgd->bqghd', p_w, v_win)
        return o_c, o_s, o_w

    o_c, o_s, o_w = lax.map(block, (qb, jnp.arange(nb)))

    def unblock(o):
        return o.transpose(1, 0, 2, 3, 4, 5).reshape(B, S, NSA_HEADS, DV)

    o = (gate[..., 0:1] * unblock(o_c) + gate[..., 1:2] * unblock(o_s)
         + gate[..., 2:3] * unblock(o_w))
    return o.reshape(B, S, NSA_OUT) @ w_out

def squared_relu_mlp(u, w1, w2):
    return jnp.square(jax.nn.relu(u @ w1)) @ w2

def setup_inputs(seed: int = 0) -> dict:
    key = jax.random.key(seed)
    keys = iter(jax.random.split(key, 40))
    f32 = jnp.float32

    def nrm(shape, fan_in):
        return jax.random.normal(next(keys), shape, f32) * fan_in ** -0.5

    def gain(shape):
        return 1.0 + 0.05 * jax.random.normal(next(keys), shape, f32)

    def small(shape, s=0.1):
        return s * jax.random.normal(next(keys), shape, f32)

    x = jax.random.normal(next(keys), (BATCH, SEQ, D_MODEL), f32)
    rel_bias = small((NUM_BUCKETS, NSA_HEADS), 0.5)
    norm_mix = gain((DEPTH, D_MODEL))
    norm_mlp = gain((DEPTH, D_MODEL))
    mlp_w1 = nrm((DEPTH, D_MODEL, D_FF), D_MODEL)
    mlp_w2 = nrm((DEPTH, D_FF, D_MODEL), D_FF)
    hy_w_in = nrm((N_EVEN, D_MODEL, HY_IN), D_MODEL)
    lru_conv_w = nrm((N_EVEN, CONV_WIDTH, LRU_WIDTH), CONV_WIDTH)
    lru_conv_b = small((N_EVEN, LRU_WIDTH))
    lru_wa = nrm((N_EVEN, LRU_BLOCKS, LRU_BLOCK_DIM, LRU_BLOCK_DIM), LRU_BLOCK_DIM)
    lru_ba = small((N_EVEN, LRU_BLOCKS, LRU_BLOCK_DIM))
    lru_wx = nrm((N_EVEN, LRU_BLOCKS, LRU_BLOCK_DIM, LRU_BLOCK_DIM), LRU_BLOCK_DIM)
    lru_bx = small((N_EVEN, LRU_BLOCKS, LRU_BLOCK_DIM))
    a_c = jax.random.uniform(next(keys), (N_EVEN, LRU_WIDTH), f32, minval=0.9, maxval=0.999)
    a0 = a_c ** (1.0 / LRU_C)
    lru_lambda = jnp.log(a0 / (1.0 - a0))
    mla_q_norm = gain((N_EVEN, MLA_Q_RANK))
    mla_kv_norm = gain((N_EVEN, MLA_KV_RANK))
    mla_w_uq = nrm((N_EVEN, MLA_Q_RANK, MLA_HEADS * MLA_QK), MLA_Q_RANK)
    mla_w_ukv = nrm((N_EVEN, MLA_KV_RANK, MLA_HEADS * (MLA_NOPE + MLA_V)), MLA_KV_RANK)
    mla_qn_q = gain((N_EVEN, MLA_QK))
    mla_qn_k = gain((N_EVEN, MLA_QK))
    hy_w_out = nrm((N_EVEN, HY_OUT, D_MODEL), HY_OUT)
    nsa_w_in = nrm((N_ODD, D_MODEL, NSA_IN), D_MODEL)
    nsa_cmp_pos_k = small((N_ODD, CMP_BLOCK, NSA_DK))
    nsa_cmp_w1_k = nrm((N_ODD, CMP_BLOCK * NSA_DK, CMP_HIDDEN), CMP_BLOCK * NSA_DK)
    nsa_cmp_w2_k = nrm((N_ODD, CMP_HIDDEN, NSA_DK), CMP_HIDDEN)
    nsa_cmp_pos_v = small((N_ODD, CMP_BLOCK, NSA_DV))
    nsa_cmp_w1_v = nrm((N_ODD, CMP_BLOCK * NSA_DV, CMP_HIDDEN), CMP_BLOCK * NSA_DV)
    nsa_cmp_w2_v = nrm((N_ODD, CMP_HIDDEN, NSA_DV), CMP_HIDDEN)
    nsa_q_norm = gain((N_ODD, NSA_DK))
    nsa_k_norm = gain((N_ODD, 3, NSA_DK))
    nsa_w_out = nrm((N_ODD, NSA_OUT, D_MODEL), NSA_OUT)
    return {'x': x, 'rel_bias': rel_bias, 'norm_mix': norm_mix, 'norm_mlp': norm_mlp,
            'mlp_w1': mlp_w1, 'mlp_w2': mlp_w2, 'hy_w_in': hy_w_in,
            'lru_conv_w': lru_conv_w, 'lru_conv_b': lru_conv_b, 'lru_wa': lru_wa, 'lru_ba': lru_ba,
            'lru_wx': lru_wx, 'lru_bx': lru_bx, 'lru_lambda': lru_lambda,
            'mla_q_norm': mla_q_norm, 'mla_kv_norm': mla_kv_norm, 'mla_w_uq': mla_w_uq,
            'mla_w_ukv': mla_w_ukv, 'mla_qn_q': mla_qn_q, 'mla_qn_k': mla_qn_k, 'hy_w_out': hy_w_out,
            'nsa_w_in': nsa_w_in, 'nsa_cmp_pos_k': nsa_cmp_pos_k, 'nsa_cmp_w1_k': nsa_cmp_w1_k,
            'nsa_cmp_w2_k': nsa_cmp_w2_k, 'nsa_cmp_pos_v': nsa_cmp_pos_v, 'nsa_cmp_w1_v': nsa_cmp_w1_v,
            'nsa_cmp_w2_v': nsa_cmp_w2_v, 'nsa_q_norm': nsa_q_norm, 'nsa_k_norm': nsa_k_norm,
            'nsa_w_out': nsa_w_out}

def reference(x, rel_bias, norm_mix, norm_mlp, mlp_w1, mlp_w2, hy_w_in,
              lru_conv_w, lru_conv_b, lru_wa, lru_ba, lru_wx, lru_bx, lru_lambda,
              mla_q_norm, mla_kv_norm, mla_w_uq, mla_w_ukv, mla_qn_q, mla_qn_k, hy_w_out,
              nsa_w_in, nsa_cmp_pos_k, nsa_cmp_w1_k, nsa_cmp_w2_k, nsa_cmp_pos_v, nsa_cmp_w1_v,
              nsa_cmp_w2_v, nsa_q_norm, nsa_k_norm, nsa_w_out):
    h = x
    for layer in range(DEPTH):
        u = rms_norm(h, norm_mix[layer])
        if layer % 2 == 0:
            e = layer // 2
            mix = hybrid_mixer(u, hy_w_in[e], lru_conv_w[e], lru_conv_b[e], lru_wa[e], lru_ba[e],
                               lru_wx[e], lru_bx[e], lru_lambda[e], mla_q_norm[e], mla_kv_norm[e],
                               mla_w_uq[e], mla_w_ukv[e], mla_qn_q[e], mla_qn_k[e], hy_w_out[e])
        else:
            o = layer // 2
            mix = nsa_mixer(u, nsa_w_in[o], nsa_cmp_pos_k[o], nsa_cmp_w1_k[o], nsa_cmp_w2_k[o],
                            nsa_cmp_pos_v[o], nsa_cmp_w1_v[o], nsa_cmp_w2_v[o], nsa_q_norm[o],
                            nsa_k_norm[o], rel_bias, nsa_w_out[o])
        h = h + mix
        h = h + squared_relu_mlp(rms_norm(h, norm_mlp[layer]), mlp_w1[layer], mlp_w2[layer])
    return h


_drawn_inputs = setup_inputs


def setup_inputs(seed=0):
    import zlib

    import numpy as np

    out = dict(_drawn_inputs(seed))
    spreads = {}
    factors = {'lru_ba': 19.29,
     'lru_bx': 11.867,
     'mla_q_norm': 8.0,
     'mla_kv_norm': 8.0,
     'mla_qn_q': 8.0,
     'mla_qn_k': 8.0,
     'nsa_cmp_pos_k': 8.0,
     'nsa_cmp_pos_v': 9.129,
     'nsa_q_norm': 8.0,
     'nsa_k_norm': 8.0,
     'rel_bias': 4.648}
    for name, (base, spread) in spreads.items():
        noise = np.random.default_rng([zlib.crc32(name.encode()), seed]).standard_normal(out[name].shape)
        drawn = base * np.exp(spread * noise) if base else spread * noise
        out[name] = __import__('jax').numpy.asarray(drawn.astype(out[name].dtype))
    for name, factor in factors.items():
        out[name] = (out[name] * factor).astype(out[name].dtype)
    return out
```

```python
from contextlib import ExitStack

import concourse.bass as bass
from concourse import mybir

F32 = mybir.dt.float32
F32R = mybir.dt.float32r
ALU = mybir.AluOpType
ACT = mybir.ActivationFunctionType
AX = mybir.AxisListType.X

P = 128
S = 1024
D = 1024
NT = S // P
KC = D // P
HALF = 512
FF = 4096
PIECE = 2048
COLS = PIECE // KC
EPS = 1e-6
NEG = -1e30

LW = 512
LC = LW // P
CONV = 4
QR, KVR, ROPE = 384, 256, 32
QRC, KVC = QR // P, KVR // P
MH, MQK, MNOPE, MV = 8, 96, 64, 64
NH, NG, HPG, DK = 16, 2, 8, 64
NCMP = 63
CMP_HID = 256
NSEL = 16
WB = 4
GATES = 3 * NH
ES_N = S + P - 1
EW_N = WB * P + 2 * P - 1
RW = (WB + 1) * P
CB_N = 119
FILL = -3.0e38

P_IN0 = 0
P_UKV = 7
P_UQ = 8
P_OUT0 = 10
P_MLP0 = 14
P_IN1 = P_MLP0 + 2 * (FF // COLS)
P_KC1 = P_IN1 + 4
P_KV1 = P_IN1 + 5
P_GATE1 = P_IN1 + 7
P_OUT1 = P_IN1 + 8
P_MLP1 = P_OUT1 + 4
N_PIECES = P_MLP1 + 2 * (FF // COLS)

C_ID, C_CAUS, C_ROPE, C_OV, C_V0 = 0, 128, 256, 512, 528
N_CST = 536
C_REV = C_CAUS
G_MIX0, G_MLP0, G_MIX1, G_MLP1 = 0, 8, 16, 24
G_CW, G_CB, G_BA, G_BX, G_LAM = 32, 48, 52, 56, 60
G_QN, G_KVN, G_GQ, G_GK = 64, 67, 69, 165
G_Q1, G_K1, G_POS = 261, 262, 265
N_PRM = 297


def build_program(nc, xT, pieces, cst, sel, prm, gatew, relx, onehot, w1c, w2c, blkind, out, stop=99):
    ctx = ExitStack()
    with ctx:
        base = (nc.sbuf_base + 63) // 64 * 64
        A0, A_W = 0, 14848
        B0 = A0 + A_W
        W0 = B0 + 16384
        G0 = W0 + 16384
        C0 = G0 + 4096

        def at(name, word, shape, dt=F32):
            return nc.alloc_sbuf_tensor_at(name, shape, dt, offset=base + 4 * word)

        def sem(name):
            return ctx.enter_context(nc.semaphore(name))

        def dram(name, shape):
            return nc.dram_tensor(name, shape, F32, kind="Internal").ap()

        ps = ctx.enter_context(nc.psum_tensor("ps", [P, 8, HALF], F32))

        def bank(b, n=1):
            return ps[:, b:b + n, :].rearrange("p b n -> p (b n)")

        top = [C0]

        def small(name, n, dt=F32):
            t = at(name, top[0], [P, n], dt)
            top[0] += (n + 7) // 8 * 8
            return t

        cs = small("cs", N_CST)
        pr = small("pr", N_PRM)
        ones = small("ones", P)
        msq = small("msq", 16)
        rsd = small("rsd", 16)
        ss = small("ss", 128)
        rs = small("rs", 128)
        ssk = small("ssk", 32)
        rsk = small("rsk", 32)
        nmx = small("nmx", 8)
        sums = small("sums", 8)
        rinv = small("rinv", 8)
        coef = small("coef", 8)
        cmx = small("cmx", 8)
        sm = small("sm", 32)
        assert (top[0]) * 4 + base <= nc.sbuf_usable_end, (top[0] * 4 + base, nc.sbuf_usable_end)
        ident = cs[:, C_ID:C_ID + P]
        causal = cs[:, C_CAUS:C_CAUS + P]
        reverse = cs[:, C_REV:C_REV + P]

        H = at("H", A0, [P, KC, S])
        hid_hi = at("hid_hi", A0 + 8192, [P, 2, 2, HALF], F32R)
        hid_lo = at("hid_lo", A0 + 10240, [P, 2, 2, HALF], F32R)
        relu = at("relu", A0 + 12288, [P, 2, HALF])
        sqr = at("sqr", A0 + 13312, [P, 2, HALF])
        nacc = at("nacc", A0 + 8192, [P, S])
        ndiag = at("ndiag", A0 + 9216, [P, NT, P])
        nuf = at("nuf", A0 + 10240, [P, 2, S])
        nsq = at("nsq", A0 + 12288, [P, 2, S])
        U_hi = at("U_hi", B0, [P, KC, S], F32R)
        U_lo = at("U_lo", B0 + 8192, [P, KC, S], F32R)
        W_hi = at("W_hi", W0, [P, 4, PIECE], F32R)
        W_lo = at("W_lo", W0 + 8192, [P, 4, PIECE], F32R)
        stage = at("stage", G0, [P, 2, PIECE])
        oh = at("oh", B0, [33, ES_N + EW_N + 1120])
        esb = at("esb", B0 + 3200, [NH, ES_N + EW_N])
        cbs = at("cbs", B0 + 5400, [P, NH, CB_N])
        rel = at("rel", B0 + 7400, [33, NH])
        lr = at("lr", A0, [P, LC, S])
        xg = at("xg", A0 + 4096, [P, LC, S])
        krope = at("krope", A0 + 8192, [32, S])
        kvlat = at("kvlat", A0 + 9216, [P, KVC, S])
        qlat = at("qlat", A0 + 11264, [P, QRC, S])
        xc = at("xc", B0, [P, LC, S])
        lra = at("lra", B0 + 4096, [P, LC, S])
        lri = at("lri", B0 + 8192, [P, LC, S])
        lrt = at("lrt", B0 + 12288, [P, 2, S])
        gw = at("gw", B0 + 14336, [P, 2, LC, P])
        lsq = at("lsq", A0 + 4096, [P, 2, S])
        lacc = at("lacc", A0 + 6144, [P, 2, S])
        Q = at("Q", A0 + 4096, [P, NT, MH, MQK])
        mla_out = Q[:].rearrange("p t h d -> p t (h d)")
        K = at("K", B0, [P, NT, MH, MQK])
        V = at("V", B0 + 6144, [P, NT, MH * MV])
        kvl_hi = at("kvl_hi", B0 + 10240, [P, KVC, S], F32R)
        kvl_lo = at("kvl_lo", B0 + 12288, [P, KVC, S], F32R)
        ql_hi = at("ql_hi", B0 + 10240, [P, QRC, S], F32R)
        ql_lo = at("ql_lo", B0 + 13312, [P, QRC, S], F32R)
        hsq = at("hsq", B0 + 10240, [P, NT, MH, MQK])
        ropet = at("ropet", B0 + 10240, [P, 4, NT, MH, 16])
        QT = at("QT", A0 + 10240, [P, 2, S])
        KT = at("KT", A0 + 12288, [P, 2, S])
        stq = at("stq", B0 + 10240, [P, NT, MQK])
        stk = at("stk", B0 + 11008, [P, NT, MQK])
        prob = at("prob", B0 + 11776, [P, 2, S])
        probT = at("probT", B0 + 13824, [P, 2, S])
        ZQ = at("ZQ", A0, [P, NT, NH * DK])
        KV = at("KV", A0 + 8192, [P, NT, 4, NG, DK])
        KCV = at("KCV", A0 + 12288, [P, 2, S])
        GATE = at("GATE", A0 + 14336, [P, NT, GATES])
        T4 = at("T4", B0, [P, 4, S])
        W1C = at("W1C", B0 + 4096, [P, 2, 16, CMP_HID])
        TP = at("TP", B0 + 12288, [P, 2, 16, NCMP])
        HC = at("HC", B0 + 14336, [NCMP, 4, CMP_HID])
        HCT = at("HCT", B0 + 15360, [P, 4, 2, NCMP])
        W2C = at("W2C", B0 + 15872, [P, 2, 2, DK])
        CKN = at("CKN", A0 + 12288, [NCMP, NG, DK])
        CKT = at("CKT", A0 + 12416, [DK, NG, NCMP])
        CV = at("CV", A0 + 12544, [NCMP, NG, DK])
        KST = at("KST", B0, [DK + NSEL, NG, S])
        KWT = at("KWT", B0 + 2048, [DK, NG, S])
        QTG = at("QTG", B0 + 4096, [DK, HPG, S])
        QA = at("QA", W0 + 9216, [DK + NSEL, 2, S])
        PW = at("PW", B0 + 12288, [P, 2, RW])
        PTW = at("PTW", B0 + 13568, [P, 2, RW])
        PTC = at("PTC", B0 + 14848, [NCMP, S])
        MT16 = at("MT16", B0 + 14848, [NSEL, S])
        P1 = at("P1", W0 + 11264, [P, 2, S])
        PT1 = at("PT1", W0 + 13312, [P, 2, S])
        STQ = at("STQ", A0 + 12800, [P, NT, DK])
        TMPO = at("TMPO", A0 + 13312, [P, NT, DK])
        PACC = at("PACC", A0 + 13824, [P, NT, NCMP])
        SW = at("SW", W0, [P, 2, RW])
        RWB = at("RWB", W0 + 1280, [P, 2, RW])
        CB = at("CB", W0 + 2560, [P, HPG, CB_N])
        PC = at("PC", W0 + 3520, [P, NT, NCMP])
        SS1 = at("SS1", W0 + 4096, [P, 2, S])
        RSB = at("RSB", W0 + 6144, [P, 2, S])
        SCO = at("SCO", W0 + 8192, [P, NT, NSEL])
        REP = at("REP", W0 + 8320, [P, NT, NSEL])
        M8 = at("M8", W0 + 8448, [P, NT, 8])
        SQ1 = at("SQ1", W0 + 4096, [P, 2, S])
        CTMP = at("CTMP", W0 + 8704, [NCMP, NG, DK])
        q_gain8 = sm[0:DK, 28:29]

        es_d = dram("es_d", [NH, ES_N])
        ew_d = dram("ew_d", [NH, EW_N])
        cb_d = dram("cb_d", [NG, P, HPG, CB_N])
        h_d = dram("h_d", [P, KC, S])

        loaded = [sem("piece_loaded0"), sem("piece_loaded1")]
        split_hi = sem("piece_hi")
        ready = sem("piece_ready")
        used = sem("piece_used")
        const_in = sem("const_in")
        x_in = sem("x_in")
        gw_in = sem("gw_in")
        oh_in = sem("oh_in")
        ones_ok = sem("ones_ok")
        waited = sem("register_waited")
        b_ready, b_evac, cb_ok, b_out = sem("bias_ready"), sem("bias_evac"), sem("cmp_bias"), sem("bias_out")
        n_sq, n_acc, n_ssq, n_ms, n_sd, n_rs, n_dg, n_bc, n_uf, n_hi, n_lo = (
            sem("norm_" + x) for x in "sq acc ssq ms sd rs dg bc uf hi lo".split())
        z_ready, z_evac = sem("z_ready"), sem("z_evac")
        sp_dve, sp_act = sem("softplus_dve"), sem("softplus_act")
        l_cv, l_conv, l_gate, l_sig, l_tanh, l_exp, l_ix, l_aa, l_t2, l_mult, l_b, l_scan, l_done = (
            sem("lru_" + x) for x in "cv conv gate sig tanh exp ix aa t2 mult b scan done".split())
        m_sq, m_acc, m_ssq, m_ms, m_sd, m_rs, m_g, m_hi, m_lo = (
            sem("lat_" + x) for x in "sq acc ssq ms sd rs gain hi lo".split())
        m_rope, m_krope, m_up, m_upev = sem("krope_T"), sem("krope_in_K"), sem("up_ready"), sem("up_evac")
        h_sq, h_red, h_ms, h_sd, h_rs, q_nrm, k_nrm = (
            sem("head_" + x) for x in "sq red ms sd rs q k".split())
        a_st, a_tr, a_trev, a_qk, a_max, a_exp, a_tp, a_tpev, a_pv, a_ri, a_out = (
            sem("mla_" + x) for x in "staged tr trev qk max exp tp tpev pv rinv out".split())
        a_diag = sem("mla_diag")
        x_tr, x_hi, x_lo = sem("mix_T"), sem("mix_hi"), sem("mix_lo")
        o_ready, o_added = sem("oproj_ready"), sem("oproj_added")
        h_in, h_spill = sem("h_reload"), sem("h_spilled")
        up_ready, up_free, relu_ok, sq_ok, sq_free, hh, hl, dn_ready, dn_free = (
            sem("mlp_" + x) for x in
            "up_ready up_free relu sq sq_free hid_hi hid_lo down_ready down_free".split())
        out_done = sem("out_done")
        w_in, t4_in, ki_in = sem("cmp_w_in"), sem("cmp_T4_in"), sem("block_rows_in")
        c_tp, c_mm, c_gelu, c_hT, c_hTev, c_out, c_sm, c_sd, c_ckT, c_ck, c_gate = (
            sem("cmp_" + x) for x in "TP mm gelu hT hTev out small sd ckT ck gate".split())
        k_sc, k_tr, k_trev = (sem("nsa_k_" + x) for x in "scaled tr trev".split())
        g_in, rw_in, rs_in, mk_in = sem("cb_in"), [sem("rw_in0"), sem("rw_in1")], [sem("rs_in0"), sem("rs_in1")], sem("mask_in")
        t_st, t_tr, t_ev, t_kept, t_back = (sem("q_" + x) for x in "staged T Tev kept back".split())
        e_qk, e_dve, e_exp, e_p, e_acc, e_tp, e_tpev, e_pv, e_o = (
            sem("c_" + x) for x in "qk dve exp p acc tp tpev pv o".split())
        w_qk, w_max, w_exp, w_tp, w_tpev, w_pv, w_ri, w_co, w_tmp, w_o = (
            sem("w_" + x) for x in "qk max exp tp tpev pv ri coef tmp o".split())
        s_qk, s_max, s_exp, s_tp, s_tpev, s_pv, s_ri, s_co, s_tmp, s_o = (
            sem("s_" + x) for x in "qk max exp tp tpev pv ri coef tmp o".split())
        i_tp, i_tpev, i_mm, i_dve, i_mask, i_mtr, i_mtrev = (
            sem("imp_" + x) for x in "tp tpev mm dve mask mtr mtrev".split())
        e_acc_c = sem("c_norm")

        block = ctx.enter_context(nc.Block())

        MLP_UNITS = 2 * (FF // COLS)

        def word(i):
            return i % 4

        def alone(eng):
            eng.sem_inc(waited, 1)

        def rotate(eng, api, X, slot, done, n):
            cos = cs[:, C_ROPE:C_ROPE + 128].rearrange("p (t d) -> p t d", t=NT).unsqueeze(2).to_broadcast([P, NT, MH, 16])
            sin = cs[:, C_ROPE + 128:C_ROPE + 256].rearrange("p (t d) -> p t d", t=NT).unsqueeze(2).to_broadcast([P, NT, MH, 16])
            x1, x2 = X[:, :, :, 64:80], X[:, :, :, 80:96]
            t1, t2 = ropet[:, slot], ropet[:, slot + 1]
            eng.wait_ge(done, n)
            api.tensor_tensor(t1, x1, sin, ALU.mult).then_inc(done, 1)
            api.tensor_tensor(t2, x2, sin, ALU.mult).then_inc(done, 1)
            eng.wait_ge(done, n + 2)
            api.tensor_tensor(x1, x1, cos, ALU.mult).then_inc(done, 1)
            api.tensor_tensor(x2, x2, cos, ALU.mult).then_inc(done, 1)
            eng.wait_ge(done, n + 4)
            api.tensor_tensor(x1, x1, t2, ALU.subtract).then_inc(done, 1)
            api.tensor_tensor(x2, x2, t1, ALU.add).then_inc(done, 1)

        def stqk_pair(t, c):
            return mla_out[:, t, c * P:(c + 1) * P]

        def mlp_pe(pe, mm3, piece_read, piece_read_now, p0, layer):
            u0 = MLP_UNITS * layer

            def up(n, q):
                s, g = q % 2, q // 2
                if s == 0:
                    pe.wait_ge(ready, n_piece(n, q) + 1)
                for j in range(2):
                    pe.wait_ge(up_free, (n + u0) * 2 + j + 1)
                    b = 2 * s + j
                    for kc in range(KC):
                        w = slice(kc * COLS + j * P, kc * COLS + (j + 1) * P)
                        m = mm3(ps[:, b, :], W_hi[:, word(p0 + 2 * g), w], W_lo[:, word(p0 + 2 * g), w],
                                U_hi[:, kc, s * HALF:(s + 1) * HALF], U_lo[:, kc, s * HALF:(s + 1) * HALF],
                                kc == 0, kc == KC - 1)
                    m.then_inc(up_ready, 1)
                if s == 1:
                    piece_read()

            def n_piece(n, q):
                return p0 + (n - q) + 2 * (q // 2)

            def down(n, q):
                s, g = q % 2, q // 2
                if s == 0:
                    pe.wait_ge(ready, n_piece(n, q) + 2)
                pe.wait_ge(hl, (n + u0) * 2 + 2)
                for dc in range(KC):
                    pe.wait_ge(dn_free, (n + u0) * 8 + dc + 1)
                    for j in range(2):
                        w = slice(j * 1024 + dc * P, j * 1024 + (dc + 1) * P)
                        m = mm3(ps[:, 4 + dc % 4, :], W_hi[:, word(p0 + 2 * g + 1), w], W_lo[:, word(p0 + 2 * g + 1), w],
                                hid_hi[:, s, j, :], hid_lo[:, s, j, :], j == 0, j == 1)
                    m.then_inc(dn_ready, 1)
                if s == 1 and q == 1:
                    piece_read()
                elif s == 1:
                    piece_read_now(dn_ready, (n + u0) * 8 + 8)

            up(0, 0)
            n_it = MLP_UNITS // 4
            with pe.Fori(0, n_it - 1) as t:
                for q in range(4):
                    up(t * 4 + (q + 1), (q + 1) % 4)
                    down(t * 4 + q, q)
            for q in range(4):
                n = (n_it - 1) * 4 + q
                if q < 3:
                    up(n + 1, q + 1)
                down(n, q)

        def norm_first_wait(act):
            act.wait_ge(cb_ok, 2)
            for g in range(NG):
                act.dma_start(cb_d[g], cbs[:, HPG * g:HPG * (g + 1), :]).then_inc(b_out, 16)
            act.wait_ge(b_out, 64)

        def mlp_act(act, layer):
            A = nc.scalar.activation
            u0 = MLP_UNITS * layer

            def hidden(n, q):
                for j in range(2):
                    act.wait_ge(up_ready, (n + u0) * 2 + j + 1)
                    A(relu[:, j, :], ps[:, 2 * (q % 2) + j, :], ACT.Relu).then_inc(up_free, 1)
                    act.wait_ge(sq_free, (n + u0) * 2 + j + 1)
                    act.wait_ge(up_free, (n + u0) * 2 + j + 5)
                    A(sqr[:, j, :], relu[:, j, :], ACT.Square).then_inc(sq_ok, 1)

            if layer == 0:
                act.sem_inc(up_free, 4)
            hidden(0, 0)
            n_it = MLP_UNITS // 4
            with act.Fori(0, n_it - 1) as t:
                for q in range(4):
                    hidden(t * 4 + (q + 1), (q + 1) % 4)
            for q in range(3):
                hidden((n_it - 1) * 4 + q + 1, q + 1)

        def mlp_dve(dve, layer):
            V_ = nc.vector
            u0 = MLP_UNITS * layer

            def hidden(n, q, first=False):
                for j in range(2):
                    dve.wait_ge(sq_ok, (n + u0) * 2 + j + 1)
                    if not first:
                        dve.wait_ge(dn_ready, (n + u0) * 8 - 8)
                    V_.tensor_copy(hid_hi[:, q % 2, j, :], sqr[:, j, :]).then_inc(hh, 1)
                    dve.wait_ge(hh, (n + u0) * 2 + j + 1)
                    V_.tensor_tensor(hid_lo[:, q % 2, j, :], sqr[:, j, :], hid_hi[:, q % 2, j, :].bitcast(F32),
                                     ALU.subtract).then_inc(hl, 1)
                dve.wait_ge(hl, (n + u0) * 2 + 2)
                dve.sem_inc(sq_free, 2)

            def add(n, q):
                cols = slice((q % 2) * HALF, (q % 2 + 1) * HALF)
                for dc in range(KC):
                    dve.wait_ge(dn_ready, (n + u0) * 8 + dc + 1)
                    dve.wait_ge(dn_free, (n + u0) * 8 + dc + 4)
                    V_.tensor_tensor(H[:, dc, cols], H[:, dc, cols], ps[:, 4 + dc % 4, :], ALU.add
                                     ).then_inc(dn_free, 1)

            hidden(0, 0, True)
            n_it = MLP_UNITS // 4
            with dve.Fori(0, n_it - 1) as t:
                for q in range(4):
                    hidden(t * 4 + (q + 1), (q + 1) % 4)
                    add(t * 4 + q, q)
            for q in range(4):
                n = (n_it - 1) * 4 + q
                if q < 3:
                    hidden(n + 1, q + 1)
                add(n, q)


        SP_COUNT = 27
        Z0 = 28
        Z1_UNITS = 60
        X0, XL0 = 8, 12
        HD0 = 2 * NT

        @block.sync
        def _(sp):
            def load(p, k):
                nc.sync.dma_start(stage[:, k % 2, :], pieces[p, :, :]).then_inc(loaded[k % 2], 16)

            load(0, 0)
            load(1, 1)
            with sp.Fori(0, (P_MLP0 - 2) // 4) as t:
                for j in range(4):
                    sp.wait_ge(ready, t * 4 + (j + 1))
                    load(t * 4 + (j + 2), j)
            with sp.Fori(0, ((P_OUT1 if stop > 1 else P_IN1) - P_MLP0) // 4) as t:
                for j in range(4):
                    sp.wait_ge(ready, t * 4 + (P_MLP0 + j - 1))
                    load(t * 4 + (P_MLP0 + j), j)
            if stop == 1:
                return
            nc.sync.dma_start(cs[:, C_REV:C_ROPE + 256], sel[:, :]).then_inc(const_in, 16)
            for p in range(P_OUT1, P_OUT1 + 2):
                sp.wait_ge(ready, p - 1)
                load(p, p)
            sp.wait_ge(z_evac, Z1_UNITS + Z0)
            nc.sync.dma_start(W1C[:], w1c[:, :, :, :]).then_inc(w_in, 16)
            nc.sync.dma_start(W2C[:], w2c[:, :, :, :]).then_inc(w_in, 16)
            for kv in range(2):
                for g in range(NG):
                    rows = slice(DK * g, DK * (g + 1))
                    nc.sync.dma_start(T4[0:DK, 2 * kv + g, :], KCV[rows, kv, :]).then_inc(t4_in, 16)
                    nc.sync.dma_start(T4[DK:P, 2 * kv + g, 0:S - 1], KCV[rows, kv, 1:S]).then_inc(t4_in, 16)
            sp.wait_ge(c_tp, 4)
            nc.sync.dma_start(KST[DK:DK + NSEL, :, :], blkind[:, :, :]).then_inc(ki_in, 16)
            sp.wait_ge(h_red, NT + 2 + HD0)
            for g in range(NG):
                if g:
                    sp.wait_ge(e_dve, g * 24)
                nc.sync.dma_start(CB[:], cb_d[g]).then_inc(g_in, 16)
                for h in range(HPG):
                    if g * HPG + h >= 2:
                        sp.wait_ge(w_max, g * 64 + 8 * (h - 1))
                    src = ew_d[g * HPG + h:g * HPG + h + 1, :]
                    src = bass.AP(src.tensor, src.offset, [[1, P], [1, RW]])
                    nc.sync.dma_start(RWB[:, h % 2, :], src).then_inc(rw_in[h % 2], 16)
                sp.wait_ge(i_mtrev, g + 1)
                for k in range(2):
                    nc.sync.dma_start(QA[DK:DK + NSEL, k, :], MT16[:]).then_inc(mk_in, 16)
                for h in range(HPG):
                    if g * HPG + h >= 2:
                        sp.wait_ge(s_max, g * 64 + 8 * (h - 1))
                    src = es_d[g * HPG + h:g * HPG + h + 1, :]
                    src = bass.AP(src.tensor, src.offset, [[1, P], [1, S]])
                    nc.sync.dma_start(RSB[:, h % 2, :], src).then_inc(rs_in[h % 2], 16)
            for p in range(P_OUT1 + 2, P_MLP1):
                sp.wait_ge(ready, p - 1)
                load(p, p)
            with sp.Fori(0, (N_PIECES - P_MLP1) // 4) as t:
                for j in range(4):
                    sp.wait_ge(ready, t * 4 + (P_MLP1 + j - 1))
                    load(t * 4 + (P_MLP1 + j), j)

        @block.gpsimd
        def _(pool):
            nc.gpsimd.memset(ones[:], 1.0).then_inc(ones_ok, 1)

            def split(t, p0, j):
                k = p0 + j
                pool.wait_ge(loaded[k % 2], (t * 4 + k - k % 2) * 8 + 16)
                if not (isinstance(t, int) and 4 * t + k < 4):
                    pool.wait_ge(used, t * 4 + (k - 3))
                alone(pool)
                nc.gpsimd.tensor_copy(W_hi[:, k % 4, :], stage[:, k % 2, :]).then_inc(split_hi, 1)
                pool.wait_ge(split_hi, t * 4 + (k + 1))
                nc.gpsimd.tensor_tensor(W_lo[:, k % 4, :], stage[:, k % 2, :],
                                        W_hi[:, k % 4, :].bitcast(F32), ALU.subtract).then_inc(ready, 1)

            for j in range(4):
                split(0, 0, j)
            with pool.Fori(1, P_MLP0 // 4) as t:
                for j in range(4):
                    split(t, 0, j)
            for j in range(P_MLP0 % 4):
                split(0, P_MLP0 // 4 * 4, j)

            pool.wait_ge(h_rs, 2)
            for t in range(NT):
                nc.gpsimd.tensor_tensor(K[:, t], K[:, t],
                                        rs[:, 64 + 8 * t:72 + 8 * t].unsqueeze(2).to_broadcast([P, MH, MQK]),
                                        ALU.mult).then_inc(k_nrm, 1)
            for t in range(NT):
                pool.wait_ge(k_nrm, t + 1)
                nc.gpsimd.tensor_tensor(K[:, t], K[:, t],
                                        pr[:, G_GK:G_GK + MQK].unsqueeze(1).to_broadcast([P, MH, MQK]),
                                        ALU.mult).then_inc(k_nrm, 1)
            rotate(pool, nc.gpsimd, K, 2, k_nrm, 2 * NT)

            pool.wait_ge(q_nrm, 2 * NT + 6)
            pool.wait_ge(k_nrm, 2 * NT + 6)
            with pool.Fori(0, MH // 2) as t:
                for hh_ in range(2):
                    pool.wait_ge(a_tr, t * 8 + 4 * hh_)
                    head = t * 2 + hh_
                    alone(pool)
                    nc.gpsimd.tensor_copy(stq[:], Q[:, :, bass.ds(head, 1), :].rearrange("p t o d -> p t (o d)")
                                          ).then_inc(a_st, 1)
                    nc.gpsimd.tensor_copy(stk[:], K[:, :, bass.ds(head, 1), :].rearrange("p t o d -> p t (o d)")
                                          ).then_inc(a_st, 1)

            with pool.Fori(0, ((P_OUT1 if stop > 1 else P_IN1) - P_MLP0) // 4) as t:
                for j in range(4):
                    split(t, P_MLP0, j)
            if stop == 1:
                return
            pool.wait_ge(h_rs, 2 + 2)
            rs_t = rs[:].rearrange("p (t h) -> p t h", t=NT)
            with pool.Fori(0, NG) as g:
                def stage_q(h):
                    pool.wait_ge(t_tr, g * 16 + h * 2)
                    head = g * HPG + h
                    nc.gpsimd.tensor_tensor(STQ[:], ZQ[:, :, bass.ds(head * DK, DK)],
                                            rs_t[:, :, bass.ds(head, 1)].to_broadcast([P, NT, DK]), ALU.mult
                                            ).then_inc(t_st, 1)

                def keep_q(h, par):
                    pool.wait_ge(t_ev, g * 16 + h * 2 + 2)
                    alone(pool)
                    nc.gpsimd.tensor_copy(QTG[:, bass.ds(h, 1), :].rearrange("p o n -> p (o n)"), QA[0:DK, par, :]
                                          ).then_inc(t_kept, 1)

                stage_q(0)
                with pool.Fori(0, HPG // 2 - 1) as t:
                    stage_q(t * 2 + 1)
                    keep_q(t * 2, 0)
                    stage_q(t * 2 + 2)
                    keep_q(t * 2 + 1, 1)
                stage_q(HPG - 1)
                keep_q(HPG - 2, 0)
                keep_q(HPG - 1, 1)

                def return_q(h, par):
                    alone(pool)
                    nc.gpsimd.tensor_copy(QA[0:DK, par, :], QTG[:, bass.ds(h, 1), :].rearrange("p o n -> p (o n)")
                                          ).then_inc(t_back, 1)

                pool.wait_ge(w_qk, g * 64 + 64)
                pool.wait_ge(t_kept, g * 8 + 8)
                return_q(0, 0)
                return_q(1, 1)
                with pool.Fori(1, HPG // 2) as t:
                    for k in range(2):
                        pool.wait_ge(s_qk, g * 64 + (t * 2 + (k - 1)) * 8)
                        return_q(t * 2 + k, k)
            pool.wait_ge(s_o, NH)
            pool.wait_ge(s_qk, 8 * NH)
            pool.wait_ge(s_pv, 8 * NH)
            with pool.Fori(0, (N_PIECES - P_OUT1) // 4) as t:
                for j in range(4):
                    split(t, P_OUT1, j)

        @block.tensor
        def _(pe):
            mm = nc.tensor.matmul

            owed = [0]

            def piece_read():
                assert not owed[0]
                owed[0] = 1

            def piece_read_now(last, value):
                pe.wait_ge(last, value)
                pe.sem_inc(used, 1)

            def mm3(o, a_hi, a_lo, b_hi, b_lo, first, last):
                m = mm(o, a_hi, b_hi, start=first, stop=False)
                if owed[0]:
                    m.then_inc(used, 1)
                    owed[0] = 0
                mm(o, a_hi, b_lo, start=False, stop=False)
                return mm(o, a_lo, b_hi, start=False, stop=last)

            def norm(k):
                pe.wait_ge(n_acc, 7 * (k + 1))
                if k == 0:
                    pe.wait_ge(ones_ok, 1)
                    pe.wait_ge(b_evac, 4)
                    pe.wait_ge(cb_ok, 2)
                for t in range(NT):
                    m = mm(ps[:, 0, t:t + 1], nacc[:, t * P:(t + 1) * P], ones[:, 0:1], start=True, stop=True)
                m.then_inc(n_ssq, 1)
                pe.wait_ge(n_dg, NT * (k + 1))
                for t in range(NT):
                    m = mm(ps[:, 1 + t // 4, t % 4 * P:t % 4 * P + P], ones[:], ndiag[:, t, :], start=True, stop=True)
                m.then_inc(n_bc, 1)

            def project_cols(k, p, c, b, m=P):
                for half in range(2):
                    yield half, b(half), [
                        (W_hi[:, word(p), kc * COLS + c * P:kc * COLS + c * P + m],
                         W_lo[:, word(p), kc * COLS + c * P:kc * COLS + c * P + m],
                         U_hi[:, kc, half * HALF:(half + 1) * HALF],
                         U_lo[:, kc, half * HALF:(half + 1) * HALF]) for kc in range(KC)]

            pe.wait_ge(oh_in, 32)
            n_tab = ES_N + EW_N
            for j in range(4):
                c1 = min(n_tab, (j + 1) * HALF)
                mm(ps[0:NH, j, 0:c1 - j * HALF], rel[:], oh[:, j * HALF:c1], start=True, stop=True).then_inc(b_ready, 1)
            for r in range(63):
                m = mm(ps[:, 4 + r // 32, (r % 32) * NH:(r % 32 + 1) * NH],
                       oh[:, n_tab + 16 * r:n_tab + 16 * r + P], rel[:], start=True, stop=True)
                if r in (31, 62):
                    m.then_inc(b_ready, 1)

            norm(0)
            pe.wait_ge(n_lo, KC)
            for c in range(14):
                p = P_IN0 + c // 2
                if c % 2 == 0:
                    pe.wait_ge(ready, p + 1)
                m_ = P if c < 13 else ROPE
                for half, b, ks in project_cols(0, p, c % 2, lambda h: (2 * c + h) % 8, m_):
                    if 2 * c + half >= 8:
                        pe.wait_ge(z_evac, 2 * c + half - 7)
                    for kc, (wh, wl, uh, ul) in enumerate(ks):
                        m = mm3(ps[0:m_, b, :], wh, wl, uh, ul, kc == 0, kc == KC - 1)
                    m.then_inc(z_ready, 1)
                if c % 2 == 1 and c < 13:
                    piece_read()
            piece_read_now(z_ready, 28)

            pe.wait_ge(gw_in, 16)
            pe.wait_ge(z_evac, 28)
            for c in range(LC):
                pe.wait_ge(l_conv, c + 1)
                if c >= 2:
                    pe.wait_ge(l_sig, 2 * (c - 1))
                for g in range(2):
                    for half in range(2):
                        m = mm(ps[:, 4 * (c % 2) + 2 * g + half, :], gw[:, g, c, :],
                               xc[:, c, half * HALF:(half + 1) * HALF], start=True, stop=True)
                    m.then_inc(l_gate, 1)

            pe.wait_ge(m_acc, 3)
            pe.wait_ge(l_sig, 2 * LC)
            for j in range(2):
                for t in range(NT):
                    m = mm(ps[:, 0, 8 * j + t:8 * j + t + 1], lacc[:, j, t * P:(t + 1) * P], ones[:, 0:1],
                           start=True, stop=True)
            m.then_inc(m_ssq, 1)
            for t in range(NT):
                m = nc.tensor.transpose(ps[:, 1, t * ROPE:(t + 1) * ROPE], krope[:, t * P:(t + 1) * P],
                                        ident[0:ROPE, 0:ROPE])
            m.then_inc(m_rope, 1)
            pe.wait_ge(ready, P_UKV + 1)
            pe.wait_ge(m_lo, KVC)
            pe.wait_ge(m_krope, 1)
            pe.wait_ge(m_ms, 1)
            for t in range(NT):
                for j in range(2):
                    n = 2 * t + j
                    if n >= 8:
                        pe.wait_ge(m_upev, n - 7)
                    for kc in range(KVC):
                        cols = slice(kc * 1024 + j * HALF, kc * 1024 + (j + 1) * HALF)
                        m = mm3(bank(n % 8), kvl_hi[:, kc, t * P:(t + 1) * P], kvl_lo[:, kc, t * P:(t + 1) * P],
                                W_hi[:, word(P_UKV), cols], W_lo[:, word(P_UKV), cols], kc == 0, kc == KVC - 1)
                    m.then_inc(m_up, 1)
            piece_read_now(m_up, 2 * NT)
            pe.wait_ge(m_lo, KVC + QRC)
            for j in range(2):
                pe.wait_ge(ready, P_UQ + j + 1)
                for t in range(NT):
                    n = 2 * NT + NT * j + t
                    pe.wait_ge(m_upev, n - 7)
                    for kc in range(QRC):
                        cols = slice(kc * 384, (kc + 1) * 384)
                        m = mm3(ps[:, n % 8, 0:384], ql_hi[:, kc, t * P:(t + 1) * P], ql_lo[:, kc, t * P:(t + 1) * P],
                                W_hi[:, word(P_UQ + j), cols], W_lo[:, word(P_UQ + j), cols],
                                kc == 0, kc == QRC - 1)
                    m.then_inc(m_up, 1)
                piece_read_now(m_up, 2 * NT + NT * (j + 1))

            pe.wait_ge(m_upev, 4 * NT)
            with pe.Fori(0, MH // 2) as it:
                for hh_ in range(2):
                    pe.wait_ge(a_st, it * 4 + 2 * hh_ + 2)
                    for j in range(4):
                        pe.wait_ge(a_trev, it * 8 + 4 * hh_ + j)
                        src = stq if j < 2 else stk
                        for t in range(4):
                            m = nc.tensor.transpose(ps[0:MQK, 7, t * P:(t + 1) * P], src[:, 4 * (j % 2) + t, :], ident)
                        m.then_inc(a_tr, 1)

                def scores(u):
                    h_, i = u // 8, u % 8
                    if u >= 2:
                        pe.wait_ge(a_exp, it * 16 + (u - 1))
                    else:
                        pe.wait_ge(a_exp, it * 16)
                    if i == 0:
                        pe.wait_ge(a_trev, it * 8 + 4 * h_ + 4)
                    n = (i + 1) * P
                    for c in range(0, n, HALF):
                        w = min(HALF, n - c)
                        m = mm(ps[:, 2 * (u % 2) + c // HALF, 0:w], QT[0:MQK, h_, i * P:(i + 1) * P],
                               KT[0:MQK, h_, c:c + w], start=True, stop=True)
                    m.then_inc(a_qk, 1)

                scores(0)
                scores(1)
                for u in range(16):
                    h_, i = u // 8, u % 8
                    pe.wait_ge(a_exp, it * 16 + u + 1)
                    pe.wait_ge(a_tpev, it * 16 + u)
                    for kb in range(i + 1):
                        m = nc.tensor.transpose(ps[:, 4 + kb // 4, kb % 4 * P:kb % 4 * P + P],
                                                prob[:, u % 2, kb * P:(kb + 1) * P], ident)
                    m.then_inc(a_tp, 1)
                    if u + 2 < 16:
                        scores(u + 2)
                    pe.wait_ge(a_tpev, it * 16 + u + 1)
                    if i == 0:
                        pe.wait_ge(a_out, it * 2 + h_)
                    for kb in range(i + 1):
                        m = mm(ps[:, 6, i * MV:(i + 1) * MV], probT[:, u % 2, kb * P:(kb + 1) * P],
                               V[:, kb, bass.ds((it * 2 + h_) * MV, MV)], start=(kb == 0), stop=(kb == i))
                    m.then_inc(a_pv, 1)

            pe.wait_ge(a_out, MH)
            for c in range(4):
                for half in range(2):
                    n = 2 * c + half
                    if n >= 4:
                        pe.wait_ge(x_lo, 4 + n - 3)
                    for t in range(4):
                        m = nc.tensor.transpose(ps[:, n % 4, t * P:(t + 1) * P],
                                                stqk_pair(4 * half + t, c), ident)
                    m.then_inc(x_tr, 1)

            def out_proj(p0, k):
                for c in range(KC):
                    p = p0 + c // 2
                    if c % 2 == 0:
                        pe.wait_ge(ready, p + 1)
                    for half, b, ks in project_cols(0, p, c % 2, lambda h: (2 * c + h) % 4 + 4):
                        n = 16 * k + 2 * c + half
                        if n >= 4:
                            pe.wait_ge(o_added, n - 3)
                        for kc, (wh, wl, uh, ul) in enumerate(ks):
                            m = mm3(ps[:, b, :], wh, wl, uh, ul, kc == 0, kc == KC - 1)
                        m.then_inc(o_ready, 1)
                    if c % 2 == 1 and c < KC - 1:
                        piece_read()
                piece_read_now(o_ready, 16 * (k + 1))

            pe.wait_ge(x_lo, 12)
            out_proj(P_OUT0, 0)
            norm(1)
            pe.wait_ge(n_lo, 2 * KC)
            mlp_pe(pe, mm3, piece_read, piece_read_now, P_MLP0, 0)
            if stop == 1:
                return

            norm(2)
            pe.wait_ge(n_lo, 3 * KC)
            n = 0
            for p in range(P_IN1, P_OUT1):
                pe.wait_ge(ready, p + 1)
                if p == P_KC1:
                    for c in range(2):
                        for half, b, ks in project_cols(0, p, c, lambda h: (n + h) % 8):
                            pe.wait_ge(z_evac, n + half - 7 + Z0)
                            for kc, (wh, wl, uh, ul) in enumerate(ks):
                                m = mm3(ps[:, b, :], wh, wl, uh, ul, kc == 0, kc == KC - 1)
                            m.then_inc(z_ready, 1)
                        n += 2
                else:
                    w = GATES if p == P_GATE1 else COLS
                    for t in range(NT):
                        if n >= 8:
                            pe.wait_ge(z_evac, n - 7 + Z0)
                        for kc in range(KC):
                            m = mm3(ps[:, n % 8, 0:w], U_hi[:, kc, t * P:(t + 1) * P], U_lo[:, kc, t * P:(t + 1) * P],
                                    W_hi[:, word(p), kc * COLS:kc * COLS + w], W_lo[:, word(p), kc * COLS:kc * COLS + w],
                                    kc == 0, kc == KC - 1)
                        m.then_inc(z_ready, 1)
                        n += 1
                if p < P_OUT1 - 1:
                    piece_read()
            assert n == Z1_UNITS
            piece_read_now(z_ready, Z0 + n)

            pe.wait_ge(w_in, 32)
            pe.wait_ge(z_evac, Z1_UNITS + Z0)
            for u in range(4):
                pe.wait_ge(c_tp, u + 1)
                for c in range(16):
                    m = mm(ps[0:NCMP, u, 0:CMP_HID], TP[:, u % 2, c, :], W1C[:, u // 2, c, :], start=c == 0, stop=c == 15)
                m.then_inc(c_mm, 1)
            for u in range(4):
                pe.wait_ge(c_gelu, u + 1)
                for k in range(2):
                    j = 2 * u + k
                    m = nc.tensor.transpose(ps[:, 4, j * NCMP:(j + 1) * NCMP], HC[:, u, k * P:(k + 1) * P],
                                            ident[0:NCMP, 0:NCMP])
            m.then_inc(c_hT, 1)
            pe.wait_ge(c_hTev, 1)
            for u in range(4):
                for k in range(2):
                    m = mm(ps[0:NCMP, 5, u * DK:(u + 1) * DK], HCT[:, u, k, :], W2C[:, u // 2, k, :],
                           start=k == 0, stop=k == 1)
            m.then_inc(c_out, 1)
            pe.wait_ge(const_in, 48)
            mm(ps[:, 7, 0:NT * GATES], reverse, GATE[:].rearrange("p t n -> p (t n)"), start=True, stop=True
               ).then_inc(c_gate, 1)
            for n in range(8):
                j, g, half = n // 4, n // 2 % 2, n % 2
                pe.wait_ge(k_sc, j + 1)
                if n >= 4:
                    pe.wait_ge(k_trev, n - 3)
                for t in range(4):
                    m = nc.tensor.transpose(ps[0:DK, n % 4, t * P:(t + 1) * P], KV[:, 4 * half + t, 2 * j, g, :], ident)
                m.then_inc(k_tr, 1)
            pe.wait_ge(c_sm, 6)
            for g in range(NG):
                m = nc.tensor.transpose(ps[0:DK, 6, g * NCMP:(g + 1) * NCMP], CKN[:, g, :], ident[0:NCMP, 0:NCMP])
            m.then_inc(c_ckT, 1)

            pe.wait_ge(c_ck, 1)
            pe.wait_ge(k_trev, 8)
            pe.wait_ge(ki_in, 16)
            pe.wait_ge(c_sm, 8)
            with pe.Fori(0, NG) as g:
                pe.wait_ge(s_o, g * 8)

                def turn_q(h, half):
                    if half == 0:
                        pe.wait_ge(t_st, g * 8 + h + 1)
                        pe.wait_ge(e_o, g * 8 + h)
                    pe.wait_ge(t_ev, g * 16 + h * 2 + half)
                    for t in range(4):
                        m = mm(ps[0:DK, 7, t * P:(t + 1) * P], STQ[:, 4 * half + t, :], reverse, start=True, stop=True)
                    m.then_inc(t_tr, 1)

                def turn_p(i, src, nb, exp, tp, tpev, value):
                    pe.wait_ge(exp, value + 1)
                    pe.wait_ge(tpev, value)
                    for kb in range(nb):
                        m = nc.tensor.transpose(ps[:, 4 + kb // 4, kb % 4 * P:kb % 4 * P + P],
                                                src[:, i % 2, kb * P:(kb + 1) * P], ident)
                    m.then_inc(tp, 1)

                def head_scores(h, par, last):
                    pe.wait_ge(t_ev, g * 16 + h * 2 + 2)
                    alone(pe)
                    for i in range(NT):
                        j = NT - 1 - i
                        m = mm(ps[:, 7, j * NCMP:(j + 1) * NCMP], QA[0:DK, par, i * P:(i + 1) * P],
                               CKT[:, bass.ds(g, 1), :].rearrange("p o n -> p (o n)"), start=True, stop=True)
                    m.then_inc(e_qk, 1)

                    def window(i):
                        u = g * 64 + h * 8 + i
                        pe.wait_ge(w_max, u if i == 0 else u - 1)
                        alone(pe)
                        k0, nk = max(i - WB, 0) * P, (min(i, WB) + 1) * P
                        for c in range(0, nk, HALF):
                            w = min(HALF, nk - c)
                            m = mm(ps[:, 2 * (i % 2) + c // HALF, 0:w], QA[0:DK, par, i * P:(i + 1) * P],
                                   KWT[:, bass.ds(g, 1), k0 + c:k0 + c + w].rearrange("p o n -> p (o n)"),
                                   start=True, stop=True)
                        m.then_inc(w_qk, 1)

                    window(0)
                    window(1)
                    for i in range(NT):
                        nb, k0 = min(i, WB) + 1, max(i - WB, 0)
                        if i == 5:
                            pe.wait_ge(e_tpev, g * 8 + h + 1)
                        turn_p(i, PW, nb, w_exp, w_tp, w_tpev, g * 64 + h * 8 + i)
                        if i + 2 < NT:
                            window(i + 2)
                        pe.wait_ge(w_tpev, g * 64 + h * 8 + i + 1)
                        if i == 0:
                            pe.wait_ge(w_o, g * 8 + h)
                        for kb in range(nb):
                            m = mm(ps[:, 6, i * DK:(i + 1) * DK], PTW[:, i % 2, kb * P:(kb + 1) * P],
                                   KV[:, k0 + kb, 3, bass.ds(g, 1), :].rearrange("p o n -> p (o n)"),
                                   start=kb == 0, stop=kb == nb - 1)
                        m.then_inc(w_pv, 1)
                        if i == 4:
                            pe.wait_ge(e_p, g * 8 + h + 1)
                            alone(pe)
                            for t in range(NT):
                                m = nc.tensor.transpose(ps[0:NCMP, 4 + t // 4, t % 4 * P:t % 4 * P + P], PC[:, NT - 1 - t, :], ident)
                            m.then_inc(e_tp, 1)
                        if i == 5:
                            alone(pe)
                            for t in range(NT):
                                m = mm(ps[:, 7, t * DK:(t + 1) * DK], PTC[:, t * P:(t + 1) * P],
                                       CV[:, bass.ds(g, 1), :].rearrange("p o n -> p (o n)"), start=True, stop=True)
                            m.then_inc(e_pv, 1)
                        if i >= 6 and not last:
                            turn_q(h + 1, i - 6)

                turn_q(0, 0)
                turn_q(0, 1)
                with pe.Fori(0, HPG // 2 - 1) as t:
                    head_scores(t * 2, 0, False)
                    head_scores(t * 2 + 1, 1, False)
                head_scores(HPG - 2, 0, False)
                head_scores(HPG - 1, 1, True)

                pe.wait_ge(e_acc, g * 9 + 9)
                pe.wait_ge(w_tpev, g * 64 + 64)
                alone(pe)
                for t in range(NT):
                    m = nc.tensor.transpose(ps[0:NCMP, 4 + t // 4, t % 4 * P:t % 4 * P + P], PACC[:, NT - 1 - t, :], ident)
                m.then_inc(i_tp, 1)
                pe.wait_ge(i_tpev, g + 1)
                pe.wait_ge(e_o, g * 8 + 8)
                for t in range(NT):
                    m = mm(ps[:, 7, t * NSEL:(t + 1) * NSEL], PTC[:, t * P:(t + 1) * P], cs[0:NCMP, C_OV:C_OV + NSEL],
                           start=True, stop=True)
                m.then_inc(i_mm, 1)
                pe.wait_ge(i_mask, g + 1)
                for t in range(NT):
                    m = nc.tensor.transpose(ps[0:NSEL, 4 + t // 4, t % 4 * P:t % 4 * P + P], REP[:, t, :], ident)
                m.then_inc(i_mtr, 1)

                pe.wait_ge(mk_in, g * 32 + 32)

                def selected(h, par, i, first=False):
                    if i == 0:
                        pe.wait_ge(t_back, g * 8 + h + 1)
                    pe.wait_ge(s_max, g * 64 if first else g * 64 + h * 8 + i - 1)
                    alone(pe)
                    nk = (i + 1) * P
                    for c in range(0, nk, HALF):
                        w = min(HALF, nk - c)
                        m = mm(ps[:, 2 * (i % 2) + c // HALF, 0:w], QA[:, par, i * P:(i + 1) * P],
                               KST[:, bass.ds(g, 1), c:c + w].rearrange("p o n -> p (o n)"), start=True, stop=True)
                    m.then_inc(s_qk, 1)

                def head_selected(h, par, first=False, last=False):
                    for i in range(NT):
                        turn_p(i, P1, i + 1, s_exp, s_tp, s_tpev, g * 64 + h * 8 + i)
                        if i + 2 < NT:
                            selected(h, par, i + 2)
                        elif not last:
                            selected(h + 1, 1 - par, i + 2 - NT)
                        pe.wait_ge(s_tpev, g * 64 + h * 8 + i + 1)
                        if i == 0 and first:
                            pe.wait_ge(w_o, g * 8 + 8)
                        elif i == 0:
                            pe.wait_ge(s_o, g * 8 + h)
                        for kb in range(i + 1):
                            m = mm(ps[:, 6, i * DK:(i + 1) * DK], PT1[:, i % 2, kb * P:(kb + 1) * P],
                                   KV[:, kb, 1, bass.ds(g, 1), :].rearrange("p o n -> p (o n)"), start=kb == 0,
                                   stop=kb == i)
                        m.then_inc(s_pv, 1)

                selected(0, 0, 0, True)
                selected(0, 0, 1, True)
                pe.wait_ge(i_mtrev, g + 1)
                head_selected(0, 0, first=True)
                with pe.Fori(0, HPG // 2 - 1) as t:
                    head_selected(t * 2 + 1, 1)
                    head_selected(t * 2 + 2, 0)
                head_selected(HPG - 1, 1, last=True)

            pe.wait_ge(s_o, NH)
            for n in range(2 * KC):
                if n >= 4:
                    pe.wait_ge(x_lo, n - 3 + XL0)
                for t in range(4):
                    m = mm(ps[:, n % 4, t * P:(t + 1) * P],
                           ZQ[:, 4 * (n % 2) + t, n // 2 * P:(n // 2 + 1) * P], reverse, start=True, stop=True)
                m.then_inc(x_tr, 1)
            pe.wait_ge(x_lo, 2 * KC + XL0)
            out_proj(P_OUT1, 1)
            norm(3)
            pe.wait_ge(n_lo, 4 * KC)
            mlp_pe(pe, mm3, piece_read, piece_read_now, P_MLP1, 1)

        @block.scalar
        def _(act):
            A = nc.scalar.activation
            act.dma_start(cs[:], cst[:, :]).then_inc(const_in, 16)
            act.dma_start(pr[:], prm[:, :]).then_inc(const_in, 16)
            act.dma_start(oh[:], onehot[:, :]).then_inc(oh_in, 16)
            act.dma_start(rel[:], relx[:, :]).then_inc(oh_in, 16)
            act.dma_start(H[:], xT[:, :, :]).then_inc(x_in, 16)

            def norm(k):
                for c in range(KC):
                    if k == 0 and c == 0:
                        act.wait_ge(x_in, 16)
                    if c >= 2:
                        act.wait_ge(n_acc, 7 * k + c - 1)
                    A(nsq[:, c % 2, :], H[:, c, :], ACT.Square).then_inc(n_sq, 1)
                act.wait_ge(n_ms, k + 1)
                A(msq[:, 8:16], msq[:, 0:8], ACT.Sqrt).then_inc(n_sd, 1)
                for c in range(KC):
                    act.wait_ge(n_uf, KC * k + c + 1)
                    A(U_hi[:, c, :], nuf[:, c % 2, :], ACT.Copy).then_inc(n_hi, 1)

            for j in range(4):
                act.wait_ge(b_ready, j + 1)
                c1 = min(ES_N + EW_N, (j + 1) * HALF)
                A(esb[:, j * HALF:c1], ps[0:NH, j, 0:c1 - j * HALF], ACT.Copy).then_inc(b_evac, 1)
            act.wait_ge(b_evac, 4)
            act.dma_start(es_d[:, :], esb[:, 0:ES_N]).then_inc(b_out, 16)
            act.dma_start(ew_d[:, :], esb[:, ES_N:ES_N + EW_N]).then_inc(b_out, 16)
            norm_first_wait(act)
            norm(0)

            for c in range(14):
                for half in range(2):
                    n = 2 * c + half
                    act.wait_ge(z_ready, n + 1)
                    cols = slice(half * HALF, (half + 1) * HALF)
                    src = ps[:, n % 8, :]
                    if c < 4:
                        A(lr[:, c, cols], src, ACT.Copy).then_inc(z_evac, 1)
                    elif c < 8:
                        A(xg[:, c - 4, cols], src, ACT.Gelu_apprx_tanh).then_inc(z_evac, 1)
                    elif c < 11:
                        A(qlat[:, c - 8, cols], src, ACT.Copy).then_inc(z_evac, 1)
                    elif c < 13:
                        A(kvlat[:, c - 11, cols], src, ACT.Copy).then_inc(z_evac, 1)
                    else:
                        A(krope[:, cols], ps[0:ROPE, n % 8, :], ACT.Copy).then_inc(z_evac, 1)
            act.wait_ge(z_evac, 28)
            act.dma_start(gw[:], gatew[:, :, :, :]).then_inc(gw_in, 16)
            act.wait_ge(sp_dve, 1)
            A(sm[:, 4:8], sm[:, 0:4], ACT.Exp, scale=-1.0).then_inc(sp_act, 1)
            for c in range(LC):
                for g, dst in ((0, lra), (1, lri)):
                    act.wait_ge(l_gate, 2 * c + g + 1)
                    o = G_BA if g == 0 else G_BX
                    A(dst[:, c, :], bank(4 * (c % 2) + 2 * g, 2), ACT.Sigmoid, bias=pr[:, o + c:o + c + 1]
                      ).then_inc(l_sig, 1)
            act.wait_ge(sp_dve, SP_COUNT)
            for c in range(LC):
                act.wait_ge(l_sig, 2 * c + 1)
                if c >= 2:
                    act.wait_ge(l_t2, c - 1)
                A(lrt[:, c % 2, :], lra[:, c, :], ACT.Tanh, scale=sm[:, 20 + c:21 + c]).then_inc(l_tanh, 1)
                act.wait_ge(l_tanh, c + 1)
                A(lra[:, c, :], lra[:, c, :], ACT.Exp, scale=sm[:, 24 + c:25 + c]).then_inc(l_exp, 1)
            for c in range(LC):
                act.wait_ge(l_t2, c + 1)
                A(xc[:, c, :], xc[:, c, :], ACT.Sqrt).then_inc(l_mult, 1)
            act.wait_ge(l_done, LC)
            for n, src in enumerate([qlat[:, 0], qlat[:, 1], qlat[:, 2], kvlat[:, 0], kvlat[:, 1]]):
                if n == 2:
                    act.wait_ge(m_acc, 1)
                if n == 4:
                    act.wait_ge(m_acc, 2)
                A(lsq[:, n % 2, :], src, ACT.Square).then_inc(m_sq, 1)
            act.wait_ge(m_ms, 1)
            A(rsd[:], msq[:], ACT.Sqrt).then_inc(m_sd, 1)
            for c in range(KVC):
                act.wait_ge(m_g, c + 1)
                A(kvl_hi[:, c, :], kvlat[:, c, :], ACT.Copy).then_inc(m_hi, 1)
            act.wait_ge(m_rs, 1)
            for t in range(NT):
                for j in range(2):
                    act.wait_ge(m_up, 2 * t + j + 1)
                    b = (2 * t + j) % 8
                    if j == 0:
                        A(K[:, t, :, 0:MNOPE], bank(b).rearrange("p (h d) -> p h d", h=MH), ACT.Copy,
                          scale=rsd[:, 8 + t:9 + t]).then_inc(m_upev, 1)
                    else:
                        A(V[:, t, :], bank(b), ACT.Copy, scale=rsd[:, 8 + t:9 + t]).then_inc(m_upev, 1)
            for c in range(QRC):
                act.wait_ge(m_g, KVC + c + 1)
                A(ql_hi[:, c, :], qlat[:, c, :], ACT.Copy).then_inc(m_hi, 1)
            for j in range(2):
                for t in range(NT):
                    n = 2 * NT + NT * j + t
                    act.wait_ge(m_up, n + 1)
                    A(Q[:, t, 4 * j:4 * j + 4, :], ps[:, n % 8, 0:384].rearrange("p (h d) -> p h d", h=4), ACT.Copy,
                      scale=rsd[:, t:t + 1]).then_inc(m_upev, 1)
            act.wait_ge(m_upev, 4 * NT)
            act.wait_ge(m_krope, 1)
            for n in range(2 * NT):
                if n >= NT:
                    act.wait_ge(h_red, n - NT + 1)
                X = Q if n < NT else K
                A(hsq[:, n % NT], X[:, n % NT], ACT.Square).then_inc(h_sq, 1)
            act.wait_ge(h_ms, 1)
            A(rs[:], ss[:], ACT.Sqrt).then_inc(h_sd, 1)

            with act.Fori(0, MH // 2) as it:
                for hh_ in range(2):
                    for j in range(4):
                        act.wait_ge(a_tr, it * 8 + 4 * hh_ + j + 1)
                        if j == 0:
                            act.wait_ge(a_pv, it * 16)
                        dst = QT if j < 2 else KT
                        A(dst[0:MQK, hh_, (j % 2) * HALF:(j % 2 + 1) * HALF], ps[0:MQK, 7, :], ACT.Copy
                          ).then_inc(a_trev, 1)

                def turned(u):
                    n = (u % 8 + 1) * P
                    act.wait_ge(a_tp, it * 16 + u + 1)
                    if u >= 2:
                        act.wait_ge(a_pv, it * 16 + (u - 1))
                    A(probT[:, u % 2, 0:n], bank(4, 2)[:, 0:n], ACT.Copy).then_inc(a_tpev, 1)

                for u in range(16):
                    n = (u % 8 + 1) * P
                    act.wait_ge(a_max, it * 16 + u + 1)
                    if u >= 2:
                        act.wait_ge(a_tp, it * 16 + (u - 1))
                    if u == 8:
                        act.wait_ge(a_ri, it * 2 + 1)
                    if u == 0:
                        act.wait_ge(a_ri, it * 2)
                    A(prob[:, u % 2, 0:n], bank(2 * (u % 2), 2)[:, 0:n], ACT.Exp, bias=nmx[:, u % 8:u % 8 + 1],
                      accum_out=sums[:, u % 8:u % 8 + 1]).then_inc(a_exp, 1)
                    if u >= 1:
                        turned(u - 1)
                turned(15)

            act.wait_ge(a_pv, 8 * MH)
            for c in range(4):
                A(U_hi[:, c, :], lr[:, c, :], ACT.Copy).then_inc(x_hi, 1)
            for n in range(8):
                act.wait_ge(x_tr, n + 1)
                A(U_hi[:, 4 + n // 2, (n % 2) * HALF:(n % 2 + 1) * HALF], ps[:, n % 4, :], ACT.Copy).then_inc(x_hi, 1)
            act.wait_ge(x_lo, 12)
            act.wait_ge(x_tr, 8)
            act.dma_start(H[:], xT[:, :, :]).then_inc(h_in, 16)
            act.wait_ge(o_added, 16)
            norm(1)
            mlp_act(act, 0)
            if stop == 1:
                act.wait_ge(out_done, 1)
                act.dma_start(out[:, :, :], H[:]).then_inc(h_in, 16)
                act.wait_ge(h_in, 32)
                return

            act.wait_ge(dn_free, 4 + 8 * MLP_UNITS)
            act.dma_start(h_d[:, :, :], H[:]).then_inc(h_spill, 16)
            norm(2)
            act.wait_ge(h_spill, 16)
            n = 0
            for p in range(P_IN1, P_OUT1):
                for t in range(4 if p == P_KC1 else NT):
                    act.wait_ge(z_ready, n + 1 + Z0)
                    src = ps[:, n % 8, 0:COLS]
                    if p < P_KC1:
                        A(ZQ[:, t, (p - P_IN1) * COLS:(p - P_IN1 + 1) * COLS], src, ACT.Copy).then_inc(z_evac, 1)
                    elif p == P_KC1:
                        A(KCV[:, t // 2, t % 2 * HALF:(t % 2 + 1) * HALF], ps[:, n % 8, :], ACT.Copy).then_inc(z_evac, 1)
                    elif p < P_GATE1:
                        j = 2 * (p - P_KV1)
                        A(KV[:, t, j:j + 2].rearrange("p j g d -> p (j g d)"), src, ACT.Copy).then_inc(z_evac, 1)
                    else:
                        A(GATE[:, t, :], ps[:, n % 8, 0:GATES], ACT.Sigmoid).then_inc(z_evac, 1)
                    n += 1
            act.wait_ge(z_evac, Z1_UNITS + Z0)
            for t in range(NT):
                if t >= 2:
                    act.wait_ge(h_red, t - 1 + HD0)
                A(SQ1[:, t % 2, :], ZQ[:, t, :], ACT.Square).then_inc(h_sq, 1)
            for j in range(2):
                act.wait_ge(h_red, NT + j - 1 + HD0)
                A(SQ1[:, j, :].rearrange("p (t n) -> p t n", t=NT), KV[:, :, 2 * j].rearrange("p t g d -> p t (g d)"),
                  ACT.Square).then_inc(h_sq, 1)
            act.wait_ge(h_ms, 2 + 1)
            A(rs[:], ss[:], ACT.Sqrt).then_inc(h_sd, 1)
            A(rsk[:], ssk[:], ACT.Sqrt).then_inc(h_sd, 1)
            for u in range(4):
                act.wait_ge(c_mm, u + 1)
                A(HC[:, u, :], ps[0:NCMP, u, 0:CMP_HID], ACT.Gelu_apprx_tanh).then_inc(c_gelu, 1)
            act.wait_ge(c_sm, 4)
            A(cmx[0:NCMP, 4:6], cmx[0:NCMP, 2:4], ACT.Sqrt).then_inc(c_sd, 1)
            act.wait_ge(c_tp, 4)
            for n in range(8):
                j, g, half = n // 4, n // 2 % 2, n % 2
                act.wait_ge(k_tr, n + 1)
                dst = KST if j == 0 else KWT
                A(dst[0:DK, g, half * HALF:(half + 1) * HALF], ps[0:DK, n % 4, :], ACT.Copy,
                  scale=pr[0:DK, G_K1 + 1 + j:G_K1 + 2 + j]).then_inc(k_trev, 1)
            act.wait_ge(c_ckT, 1)
            A(CKT[:], ps[0:DK, 6, 0:NG * NCMP].rearrange("p (g n) -> p g n", g=NG), ACT.Copy,
              scale=pr[0:DK, G_K1:G_K1 + 1]).then_inc(c_ck, 1)

            with act.Fori(0, NG) as g:
                def turn_q(h, par, half):
                    act.wait_ge(t_tr, g * 16 + h * 2 + half + 1)
                    act.wait_ge(t_kept, g * 8 + (h if isinstance(h, int) and h < 1 else h - 1))
                    A(QA[0:DK, par, half * HALF:(half + 1) * HALF], ps[0:DK, 7, :], ACT.Copy, scale=q_gain8
                      ).then_inc(t_ev, 1)

                turn_q(0, 0, 0)
                turn_q(0, 0, 1)

                def head_scores(h, par, last):
                    act.wait_ge(e_dve, g * 24 + h * 3 + 3)
                    A(PC[:], PC[:], ACT.Exp).then_inc(e_exp, 1)

                    def expo(i):
                        u = g * 64 + h * 8 + i
                        nk = (min(i, WB) + 1) * P
                        act.wait_ge(w_max, u + 1)
                        if i == 0:
                            act.wait_ge(w_ri, g * 8 + h)
                        else:
                            act.wait_ge(w_tp, u - 1)
                        A(PW[:, i % 2, 0:nk], SW[:, i % 2, 0:nk], ACT.Exp, bias=nmx[:, i:i + 1], scale=-1.0,
                          accum_out=sums[:, i:i + 1]).then_inc(w_exp, 1)

                    expo(0)
                    for i in range(NT):
                        if i + 1 < NT:
                            expo(i + 1)
                        nk = (min(i, WB) + 1) * P
                        act.wait_ge(w_tp, g * 64 + h * 8 + i + 1)
                        act.wait_ge(w_pv, g * 64 + h * 8 + i)
                        A(PTW[:, i % 2, 0:nk], bank(4, 2)[:, 0:nk], ACT.Copy).then_inc(w_tpev, 1)
                        if i == 4:
                            act.wait_ge(e_tp, g * 8 + h + 1)
                            act.wait_ge(e_pv, g * 8 + h)
                            A(PTC[:], bank(4, 2)[0:NCMP, :], ACT.Copy).then_inc(e_tpev, 1)
                        if i >= 6 and not last:
                            turn_q(h + 1, 1 - par, i - 6)

                with act.Fori(0, HPG // 2 - 1) as t:
                    head_scores(t * 2, 0, False)
                    head_scores(t * 2 + 1, 1, False)
                head_scores(HPG - 2, 0, False)
                head_scores(HPG - 1, 1, True)
                act.wait_ge(i_tp, g + 1)
                act.wait_ge(e_pv, g * 8 + 8)
                A(PTC[:], bank(4, 2)[0:NCMP, :], ACT.Copy).then_inc(i_tpev, 1)
                act.wait_ge(i_mtr, g + 1)
                A(MT16[:], bank(4, 2)[0:NSEL, :], ACT.Copy).then_inc(i_mtrev, 1)

                def expo_s(h, i, first=False):
                    nk = (i + 1) * P
                    act.wait_ge(s_max, g * 64 + h * 8 + i + 1)
                    if first:
                        act.wait_ge(w_ri, g * 8 + 8)
                    else:
                        act.wait_ge(s_tp, g * 64 + h * 8 + i - 1)
                        if i == 0:
                            act.wait_ge(s_ri, g * 8 + h)
                    A(P1[:, i % 2, 0:nk], SS1[:, i % 2, 0:nk], ACT.Exp, bias=nmx[:, i:i + 1], scale=-1.0,
                      accum_out=sums[:, i:i + 1]).then_inc(s_exp, 1)

                def head_selected(h, last):
                    for i in range(NT):
                        if i + 1 < NT:
                            expo_s(h, i + 1)
                        elif not last:
                            expo_s(h + 1, 0)
                        nk = (i + 1) * P
                        act.wait_ge(s_tp, g * 64 + h * 8 + i + 1)
                        act.wait_ge(s_pv, g * 64 + h * 8 + i)
                        A(PT1[:, i % 2, 0:nk], bank(4, 2)[:, 0:nk], ACT.Copy).then_inc(s_tpev, 1)

                act.wait_ge(mk_in, g * 32 + 32)
                expo_s(0, 0, True)
                with act.Fori(0, HPG - 1) as h:
                    head_selected(h, False)
                head_selected(HPG - 1, True)

            act.wait_ge(s_pv, 128)
            for n in range(2 * KC):
                act.wait_ge(x_tr, n + 1 + X0)
                A(U_hi[:, n // 2, (n % 2) * HALF:(n % 2 + 1) * HALF], ps[:, n % 4, :], ACT.Copy).then_inc(x_hi, 1)
            act.dma_start(H[:], h_d[:, :, :]).then_inc(h_in, 16)
            act.wait_ge(o_added, 32)
            norm(3)
            mlp_act(act, 1)
            act.wait_ge(out_done, 1)
            act.dma_start(out[:, :, :], H[:]).then_inc(h_in, 16)
            act.wait_ge(h_in, 48)


        @block.vector
        def _(dve):
            V_ = nc.vector

            dve.sem_inc(sq_free, 2)
            dve.sem_inc(dn_free, 4)

            def norm(k, g0):
                for c in range(1, KC):
                    dve.wait_ge(n_sq, KC * k + c + 1)
                    if c == 1:
                        V_.tensor_tensor(nacc[:], nsq[:, 0, :], nsq[:, 1, :], ALU.add).then_inc(n_acc, 1)
                    else:
                        dve.wait_ge(n_acc, 7 * k + c - 1)
                        V_.tensor_tensor(nacc[:], nacc[:], nsq[:, c % 2, :], ALU.add).then_inc(n_acc, 1)
                dve.wait_ge(n_ssq, k + 1)
                V_.tensor_scalar(msq[:, 0:8], ps[:, 0, 0:8], 1.0 / D, EPS, ALU.mult, ALU.add).then_inc(n_ms, 1)
                dve.wait_ge(n_sd, k + 1)
                V_.reciprocal(rsd[:, 0:8], msq[:, 8:16]).then_inc(n_rs, 1)
                dve.wait_ge(n_rs, k + 1)
                for t in range(NT):
                    V_.tensor_scalar(ndiag[:, t, :], ident, rsd[:, t:t + 1], None, ALU.mult).then_inc(n_dg, 1)
                dve.wait_ge(n_bc, k + 1)

                def low(c):
                    dve.wait_ge(n_hi, KC * k + c + 1)
                    V_.tensor_tensor(U_lo[:, c, :], nuf[:, c % 2, :], U_hi[:, c, :].bitcast(F32), ALU.subtract
                                     ).then_inc(n_lo, 1)

                for c in range(KC):
                    if c >= 2:
                        dve.wait_ge(n_lo, KC * k + c - 1)
                    V_.scalar_tensor_tensor(nuf[:, c % 2, :], H[:, c, :], pr[:, g0 + c:g0 + c + 1], bank(1, 2),
                                            ALU.mult, ALU.mult).then_inc(n_uf, 1)
                    if c >= 1:
                        low(c - 1)
                low(KC - 1)

            V_.memset(cbs[:, :, 63:CB_N], NEG).then_inc(cb_ok, 1)
            dve.wait_ge(b_ready, 6)
            cb_v = cbs[:, :, 0:63].rearrange("p h r -> p r h")
            V_.tensor_copy(cb_v, bank(4, 2)[:, 0:63 * NH].rearrange("p (r h) -> p r h", h=NH)).then_inc(cb_ok, 1)
            dve.wait_ge(const_in, 32)
            dve.wait_ge(b_out, 64)
            norm(0, G_MIX0)

            n_sp = [0]

            def chain(ins):
                ins.then_inc(sp_dve, 1)
                n_sp[0] += 1
                dve.wait_ge(sp_dve, n_sp[0])

            lam = pr[:, G_LAM:G_LAM + 4]
            chain(V_.scalar_tensor_tensor(sm[:, 0:4], lam, -1.0, lam, ALU.mult, ALU.max))
            dve.wait_ge(sp_act, 1)
            e = sm[:, 4:8]
            chain(V_.tensor_scalar(sm[:, 8:12], e, 2.0, None, ALU.add))
            chain(V_.reciprocal(sm[:, 12:16], sm[:, 8:12]))
            chain(V_.tensor_tensor(sm[:, 8:12], e, sm[:, 12:16], ALU.mult))
            chain(V_.tensor_tensor(sm[:, 12:16], sm[:, 8:12], sm[:, 8:12], ALU.mult))
            chain(V_.tensor_scalar(sm[:, 16:20], sm[:, 12:16], 1.0 / 19, 1.0 / 17, ALU.mult, ALU.add))
            for k in (15, 13, 11, 9, 7, 5, 3, 1):
                chain(V_.tensor_tensor(sm[:, 20:24], sm[:, 16:20], sm[:, 12:16], ALU.mult))
                chain(V_.tensor_scalar(sm[:, 16:20], sm[:, 20:24], 1.0 / k, None, ALU.add))
            chain(V_.scalar_tensor_tensor(sm[:, 8:12], sm[:, 8:12], 2.0, sm[:, 16:20], ALU.mult, ALU.mult))
            chain(V_.tensor_scalar(sm[:, 12:16], lam, -1.0, 0.0, ALU.mult, ALU.max))
            chain(V_.tensor_tensor(sm[:, 16:20], sm[:, 8:12], sm[:, 12:16], ALU.add))
            chain(V_.tensor_scalar(sm[:, 20:24], sm[:, 16:20], 8.0, None, ALU.mult))
            chain(V_.tensor_scalar(sm[:, 24:28], sm[:, 16:20], -8.0, None, ALU.mult))
            assert n_sp[0] == SP_COUNT, n_sp[0]

            dve.wait_ge(z_evac, 28)
            for c in range(LC):
                w = lambda k: pr[:, G_CW + 4 * c + k:G_CW + 4 * c + k + 1]
                V_.tensor_scalar(xc[:, c, :], lr[:, c, :], w(3), pr[:, G_CB + c:G_CB + c + 1], ALU.mult, ALU.add
                                 ).then_inc(l_cv, 1)
                for s in (1, 2, 3):
                    dve.wait_ge(l_cv, 3 * c + s)
                    m = V_.scalar_tensor_tensor(xc[:, c, s:S], lr[:, c, 0:S - s], w(3 - s), xc[:, c, s:S],
                                                ALU.mult, ALU.add)
                    m.then_inc(l_cv if s < 3 else l_conv, 1)
            for c in range(LC):
                dve.wait_ge(l_sig, 2 * c + 2)
                dve.wait_ge(l_gate, 2 * c + 2)
                V_.tensor_tensor(lri[:, c, :], lri[:, c, :], xc[:, c, :], ALU.mult).then_inc(l_ix, 1)
            for c in range(LC):
                dve.wait_ge(l_exp, c + 1)
                dve.wait_ge(l_ix, c + 1)
                V_.tensor_tensor(xc[:, c, :], lra[:, c, :], lra[:, c, :], ALU.mult).then_inc(l_aa, 1)
                dve.wait_ge(l_aa, c + 1)
                V_.scalar_tensor_tensor(xc[:, c, :], xc[:, c, :], 1.0, lrt[:, c % 2, :], ALU.add, ALU.mult
                                        ).then_inc(l_t2, 1)
            for c in range(LC):
                dve.wait_ge(l_mult, c + 1)
                V_.memset(xc[:, c, 0:1], 1.0).then_inc(l_b, 1)
                dve.wait_ge(l_b, 2 * c + 1)
                V_.tensor_tensor(lri[:, c, :], lri[:, c, :], xc[:, c, :], ALU.mult).then_inc(l_b, 1)
                dve.wait_ge(l_b, 2 * c + 2)
                V_.tensor_tensor_scan(lr[:, c, :], lra[:, c, :], lri[:, c, :], 0.0, ALU.mult, ALU.add
                                      ).then_inc(l_scan, 1)
                dve.wait_ge(l_scan, c + 1)
                V_.tensor_tensor(lr[:, c, :], lr[:, c, :], xg[:, c, :], ALU.mult).then_inc(l_done, 1)

            dve.wait_ge(m_sq, 2)
            V_.tensor_tensor(lacc[:, 0, :], lsq[:, 0, :], lsq[:, 1, :], ALU.add).then_inc(m_acc, 1)
            dve.wait_ge(m_sq, 3)
            dve.wait_ge(m_acc, 1)
            V_.tensor_tensor(lacc[:, 0, :], lacc[:, 0, :], lsq[:, 0, :], ALU.add).then_inc(m_acc, 1)
            dve.wait_ge(m_sq, 5)
            V_.tensor_tensor(lacc[:, 1, :], lsq[:, 1, :], lsq[:, 0, :], ALU.add).then_inc(m_acc, 1)
            for c in range(KVC):
                V_.tensor_scalar(kvlat[:, c, :], kvlat[:, c, :], pr[:, G_KVN + c:G_KVN + c + 1], None, ALU.mult
                                 ).then_inc(m_g, 1)
            for c in range(QRC):
                V_.tensor_scalar(qlat[:, c, :], qlat[:, c, :], pr[:, G_QN + c:G_QN + c + 1], None, ALU.mult
                                 ).then_inc(m_g, 1)
            dve.wait_ge(m_ssq, 1)
            V_.tensor_scalar(msq[:, 0:8], ps[:, 0, 0:8], 1.0 / QR, EPS, ALU.mult, ALU.add)
            V_.tensor_scalar(msq[:, 8:16], ps[:, 0, 8:16], 1.0 / KVR, EPS, ALU.mult, ALU.add).then_inc(m_ms, 1)
            dve.wait_ge(m_sd, 1)
            V_.reciprocal(rsd[:], rsd[:]).then_inc(m_rs, 1)
            dve.wait_ge(m_rope, 1)
            V_.tensor_copy(K[:, :, :, MNOPE:MQK],
                           ps[:, 1, 0:NT * ROPE].rearrange("p (t d) -> p t d", t=NT).unsqueeze(2)
                           .to_broadcast([P, NT, MH, ROPE])).then_inc(m_krope, 1)
            for c in range(KVC):
                dve.wait_ge(m_hi, c + 1)
                V_.tensor_tensor(kvl_lo[:, c, :], kvlat[:, c, :], kvl_hi[:, c, :].bitcast(F32), ALU.subtract
                                 ).then_inc(m_lo, 1)
            dve.wait_ge(m_up, 2 * NT)
            for c in range(QRC):
                dve.wait_ge(m_hi, KVC + c + 1)
                V_.tensor_tensor(ql_lo[:, c, :], qlat[:, c, :], ql_hi[:, c, :].bitcast(F32), ALU.subtract
                                 ).then_inc(m_lo, 1)
            for n in range(2 * NT):
                dve.wait_ge(h_sq, n + 1)
                V_.tensor_reduce(ss[:, 8 * n:8 * n + 8], hsq[:, n % NT], AX, ALU.add).then_inc(h_red, 1)
            dve.wait_ge(h_red, 2 * NT)
            V_.tensor_scalar(ss[:], ss[:], 1.0 / MQK, EPS, ALU.mult, ALU.add).then_inc(h_ms, 1)
            dve.wait_ge(h_sd, 1)
            V_.reciprocal(rs[:], rs[:]).then_inc(h_rs, 1)
            dve.wait_ge(h_rs, 1)
            V_.tensor_scalar(rs[:, 0:64], rs[:, 0:64], float(MQK) ** -0.5, None, ALU.mult).then_inc(h_rs, 1)
            dve.wait_ge(h_rs, 2)
            for t in range(NT):
                V_.tensor_tensor(Q[:, t], Q[:, t], rs[:, 8 * t:8 * t + 8].unsqueeze(2).to_broadcast([P, MH, MQK]),
                                 ALU.mult).then_inc(q_nrm, 1)
            for t in range(NT):
                dve.wait_ge(q_nrm, t + 1)
                V_.tensor_tensor(Q[:, t], Q[:, t],
                                 pr[:, G_GQ:G_GQ + MQK].unsqueeze(1).to_broadcast([P, MH, MQK]),
                                 ALU.mult).then_inc(q_nrm, 1)
            rotate(dve, V_, Q, 0, q_nrm, 2 * NT)

            with dve.Fori(0, MH // 2) as it:
                for u in range(16):
                    h_, i = u // 8, u % 8
                    n = (i + 1) * P
                    s_ps = bank(2 * (u % 2), 2)
                    dve.wait_ge(a_qk, it * 16 + u + 1)
                    V_.tensor_tensor(s_ps[:, i * P:n], s_ps[:, i * P:n], causal, ALU.add).then_inc(a_diag, 1)
                    dve.wait_ge(a_diag, it * 16 + u + 1)
                    if u % 8 == 0:
                        dve.wait_ge(a_exp, it * 16 + u)
                    V_.tensor_reduce(nmx[:, i:i + 1], s_ps[:, 0:n], AX, ALU.max, negate=True).then_inc(a_max, 1)
                    if i == 7:
                        dve.wait_ge(a_exp, it * 16 + u + 1)
                        V_.reciprocal(rinv[:], sums[:]).then_inc(a_ri, 1)
                    if u in (9, 15):
                        dve.wait_ge(a_ri, it * 2 + (1 if u == 9 else 2))
                        dve.wait_ge(a_pv, it * 16 + (8 if u == 9 else 16))
                        h_ = u // 15
                        V_.tensor_tensor(
                            mla_out[:, :, bass.ds((it * 2 + h_) * MV, MV)],
                            bank(6).rearrange("p (t d) -> p t d", t=NT),
                            rinv[:].unsqueeze(2).to_broadcast([P, NT, MV]), ALU.mult).then_inc(a_out, 1)

            for c in range(4):
                dve.wait_ge(x_hi, c + 1)
                V_.tensor_tensor(U_lo[:, c, :], lr[:, c, :], U_hi[:, c, :].bitcast(F32), ALU.subtract).then_inc(x_lo, 1)
            for n in range(8):
                dve.wait_ge(x_hi, 4 + n + 1)
                cols = slice((n % 2) * HALF, (n % 2 + 1) * HALF)
                V_.tensor_tensor(U_lo[:, 4 + n // 2, cols], ps[:, n % 4, :], U_hi[:, 4 + n // 2, cols].bitcast(F32),
                                 ALU.subtract).then_inc(x_lo, 1)

            def add_out(k):
                for n in range(16):
                    dve.wait_ge(o_ready, 16 * k + n + 1)
                    dve.wait_ge(h_in, 16 * (k + 1))
                    cols = slice((n % 2) * HALF, (n % 2 + 1) * HALF)
                    V_.tensor_tensor(H[:, n // 2, cols], H[:, n // 2, cols], ps[:, n % 4 + 4, :], ALU.add
                                     ).then_inc(o_added, 1)

            add_out(0)
            dve.wait_ge(o_added, 16)
            norm(1, G_MLP0)
            mlp_dve(dve, 0)
            if stop == 1:
                dve.wait_ge(dn_free, 4 + 8 * MLP_UNITS)
                dve.sem_inc(out_done, 1)
                return

            dve.wait_ge(dn_free, 4 + 8 * MLP_UNITS)
            norm(2, G_MIX1)
            V_.tensor_scalar(q_gain8, pr[0:DK, G_Q1:G_Q1 + 1], float(DK) ** -0.5, None, ALU.mult)
            for n in range(NT + 2):
                dve.wait_ge(h_sq, n + 1 + HD0)
                dst = ss[:, 16 * n:16 * n + 16] if n < NT else ssk[:, 16 * (n - NT):16 * (n - NT) + 16]
                V_.tensor_reduce(dst, SQ1[:, n % 2, :].rearrange("p (h d) -> p h d", d=DK), AX, ALU.add
                                 ).then_inc(h_red, 1)
            dve.wait_ge(h_red, NT + 2 + HD0)
            V_.tensor_scalar(ss[:], ss[:], 1.0 / DK, EPS, ALU.mult, ALU.add).then_inc(h_ms, 1)
            V_.tensor_scalar(ssk[:], ssk[:], 1.0 / DK, EPS, ALU.mult, ALU.add).then_inc(h_ms, 1)
            dve.wait_ge(t4_in, 128)
            for u in range(4):
                if u >= 2:
                    dve.wait_ge(c_mm, u - 1)
                src = T4[:, u, 0:1]
                src = bass.AP(src.tensor, src.offset, [list(src.ap[0]), [2, 16], [16, NCMP]])
                V_.tensor_tensor(TP[:, u % 2], src,
                                 pr[:, G_POS + 16 * (u // 2):G_POS + 16 * (u // 2 + 1)].unsqueeze(2)
                                 .to_broadcast([P, 16, NCMP]), ALU.add).then_inc(c_tp, 1)
            dve.wait_ge(h_sd, 2 + 1)
            V_.reciprocal(rs[:], rs[:]).then_inc(h_rs, 1)
            V_.reciprocal(rsk[:], rsk[:]).then_inc(h_rs, 1)
            dve.wait_ge(h_rs, 2 + 2)
            for j in range(2):
                V_.tensor_tensor(KV[:, :, 2 * j], KV[:, :, 2 * j],
                                 rsk[:, 16 * j:16 * j + 16].rearrange("p (t g) -> p t g", g=NG).unsqueeze(3)
                                 .to_broadcast([P, NT, NG, DK]), ALU.mult).then_inc(k_sc, 1)
            dve.wait_ge(c_hT, 1)
            V_.tensor_copy(HCT[:].rearrange("p u k n -> p (u k n)"), ps[:, 4, 0:8 * NCMP]).then_inc(c_hTev, 1)
            dve.wait_ge(c_out, 1)
            o5 = ps[0:NCMP, 5, 0:4 * DK].rearrange("p (u d) -> p u d", u=4)
            V_.tensor_copy(CKN[:], o5[:, 0:2]).then_inc(c_sm, 1)
            dve.wait_ge(c_sm, 1)
            V_.tensor_tensor(CTMP[:], CKN[:], CKN[:], ALU.mult).then_inc(c_sm, 1)
            dve.wait_ge(c_sm, 2)
            V_.tensor_reduce(cmx[0:NCMP, 0:2], CTMP[:], AX, ALU.add).then_inc(c_sm, 1)
            dve.wait_ge(c_sm, 3)
            V_.tensor_scalar(cmx[0:NCMP, 2:4], cmx[0:NCMP, 0:2], 1.0 / DK, EPS, ALU.mult, ALU.add).then_inc(c_sm, 1)
            dve.wait_ge(c_sd, 1)
            V_.reciprocal(cmx[0:NCMP, 6:8], cmx[0:NCMP, 4:6]).then_inc(c_sm, 1)
            dve.wait_ge(c_sm, 5)
            V_.tensor_tensor(CKN[:], CKN[:], cmx[0:NCMP, 6:8].unsqueeze(2).to_broadcast([NCMP, NG, DK]), ALU.mult
                             ).then_inc(c_sm, 1)
            V_.tensor_copy(CV[:], o5[:, 2:4]).then_inc(c_sm, 1)
            dve.wait_ge(c_gate, 1)
            V_.tensor_copy(GATE[:].rearrange("p t n -> p (t n)"), ps[:, 7, 0:NT * GATES]).then_inc(c_sm, 1)
            dve.wait_ge(const_in, 48)
            dve.wait_ge(c_sm, 8)

            with dve.Fori(0, NG) as g:
                def gate(h, branch):
                    return GATE[:, :, bass.ds((g * HPG + h) * 3 + branch, 1)]

                def head_out(h):
                    return ZQ[:, :, bass.ds((g * HPG + h) * DK, DK)]

                def finish(h, branch, ri, co, pv, tmp, o):
                    dve.wait_ge(ri, g * 8 + h + 1)
                    V_.tensor_tensor(coef[:].unsqueeze(2), rinv[:].unsqueeze(2), gate(h, branch), ALU.mult).then_inc(co, 1)
                    dve.wait_ge(co, g * 8 + h + 1)
                    dve.wait_ge(pv, g * 64 + h * 8 + 8)
                    V_.tensor_tensor(TMPO[:], bank(6).rearrange("p (t d) -> p t d", t=NT),
                                     coef[:].unsqueeze(2).to_broadcast([P, NT, DK]), ALU.mult).then_inc(tmp, 1)
                    dve.wait_ge(tmp, g * 8 + h + 1)
                    V_.tensor_tensor(head_out(h), head_out(h), TMPO[:], ALU.add).then_inc(o, 1)

                def head_scores(h, par):
                    dve.wait_ge(e_qk, g * 8 + h + 1)
                    dve.wait_ge(e_tp, g * 8 + h)
                    cb = CB[:, bass.ds(h, 1), 0:1]
                    cb = bass.AP(cb.tensor, cb.offset, [list(cb.ap[0]), [8, NT], [1, NCMP]])
                    V_.tensor_tensor(PC[:], bank(7)[:, 0:NT * NCMP].rearrange("p (t n) -> p t n", t=NT), cb, ALU.add
                                     ).then_inc(e_dve, 1)
                    dve.wait_ge(e_dve, g * 24 + h * 3 + 1)
                    V_.tensor_reduce(cmx[:], PC[:], AX, ALU.max).then_inc(e_dve, 1)
                    dve.wait_ge(e_dve, g * 24 + h * 3 + 2)
                    V_.tensor_tensor(PC[:], PC[:], cmx[:].unsqueeze(2).to_broadcast([P, NT, NCMP]), ALU.subtract
                                     ).then_inc(e_dve, 1)

                    def biased(i):
                        u = g * 64 + h * 8 + i
                        nk = (min(i, WB) + 1) * P
                        c0 = RW - nk
                        if i == 0:
                            dve.wait_ge(rw_in[par], g * 64 + (h - par) * 8 + 16)
                        dve.wait_ge(w_qk, u + 1)
                        dve.wait_ge(w_exp, u if i == 0 else u - 1)
                        alone(dve)
                        V_.tensor_tensor_reduce(SW[:, i % 2, 0:nk], bank(2 * (i % 2), 2)[:, 0:nk],
                                                RWB[:, par, c0:RW], -1.0, 3.0e38, ALU.add, ALU.min, nmx[:, i:i + 1]
                                                ).then_inc(w_max, 1)

                    biased(0)
                    biased(1)
                    n0 = (g * HPG + h) * 4
                    dve.wait_ge(e_exp, g * 8 + h + 1)
                    V_.tensor_reduce(cmx[:], PC[:], AX, ALU.add).then_inc(e_acc_c, 1)
                    dve.wait_ge(e_acc_c, n0 + 1)
                    V_.reciprocal(coef[:], cmx[:]).then_inc(e_acc_c, 1)
                    dve.wait_ge(e_acc_c, n0 + 2)
                    V_.tensor_tensor(cmx[:], coef[:], cs[:, C_V0:C_V0 + NT], ALU.mult).then_inc(e_acc_c, 1)
                    dve.wait_ge(e_acc_c, n0 + 3)
                    V_.tensor_tensor(PC[:], PC[:], cmx[:].unsqueeze(2).to_broadcast([P, NT, NCMP]), ALU.mult
                                     ).then_inc(e_acc_c, 1)
                    dve.wait_ge(e_acc_c, n0 + 4)
                    V_.scalar_tensor_tensor(PC[:], PC[:], 1.17549435e-38, PC[:], ALU.is_ge, ALU.mult).then_inc(e_p, 1)
                    dve.wait_ge(e_p, g * 8 + h + 1)
                    dve.wait_ge(e_acc, g * 9 + h + 1)
                    V_.tensor_tensor(PACC[:], PACC[:], PC[:], ALU.add).then_inc(e_acc, 1)
                    for i in range(2, NT):
                        biased(i)
                    dve.wait_ge(e_pv, g * 8 + h + 1)
                    V_.tensor_tensor(head_out(h), bank(7).rearrange("p (t d) -> p t d", t=NT),
                                     gate(h, 0).to_broadcast([P, NT, DK]), ALU.mult).then_inc(e_o, 1)
                    dve.wait_ge(w_exp, g * 64 + h * 8 + 8)
                    V_.reciprocal(rinv[:], sums[:]).then_inc(w_ri, 1)
                    dve.wait_ge(e_o, g * 8 + h + 1)
                    finish(h, 2, w_ri, w_co, w_pv, w_tmp, w_o)

                dve.wait_ge(g_in, g * 16 + 16)
                dve.wait_ge(i_tp, g * 1)
                V_.memset(PACC[:], 0.0).then_inc(e_acc, 1)
                with dve.Fori(0, HPG // 2) as t:
                    head_scores(t * 2, 0)
                    head_scores(t * 2 + 1, 1)

                dve.wait_ge(i_mm, g + 1)
                dve.wait_ge(w_exp, g * 64 + 64)
                n0 = g * (3 + 2 * NT)
                A_ = cs[:, C_ROPE:C_ROPE + 128].rearrange("p (t n) -> p t n", t=NT)
                B_ = cs[:, C_ROPE + 128:C_ROPE + 256].rearrange("p (t n) -> p t n", t=NT)
                V_.tensor_tensor(SCO[:], bank(7)[:, 0:NT * NSEL].rearrange("p (t n) -> p t n", t=NT), A_, ALU.mult
                                 ).then_inc(i_dve, 1)
                dve.wait_ge(i_dve, n0 + 1)
                V_.tensor_tensor(SCO[:], SCO[:], B_, ALU.add).then_inc(i_dve, 1)
                dve.wait_ge(i_dve, n0 + 2)
                alone(dve)
                for t in range(NT):
                    V_.max(M8[:, t, :], SCO[:, t, :]).then_inc(i_dve, 1)
                for t in range(NT):
                    dve.wait_ge(i_dve, n0 + 3 + t)
                    alone(dve)
                    V_.match_replace(REP[:, t, :], M8[:, t, :], SCO[:, t, :], FILL).then_inc(i_dve, 1)
                dve.wait_ge(i_dve, n0 + 2 + 2 * NT)
                V_.tensor_scalar(REP[:], REP[:], FILL, -1.0, ALU.is_equal, ALU.add).then_inc(i_dve, 1)
                dve.wait_ge(i_dve, n0 + 3 + 2 * NT)
                V_.tensor_scalar(REP[:], REP[:], -NEG, None, ALU.mult).then_inc(i_mask, 1)

                def head_selected(h, par, first=False):
                    for i in range(NT):
                        u = g * 64 + h * 8 + i
                        nk = (i + 1) * P
                        if i == 0:
                            dve.wait_ge(rs_in[par], g * 64 + (h - par) * 8 + 16)
                        dve.wait_ge(s_qk, u + 1)
                        dve.wait_ge(s_exp, u if i == 0 else u - 1)
                        alone(dve)
                        V_.tensor_tensor_reduce(SS1[:, i % 2, 0:nk], bank(2 * (i % 2), 2)[:, 0:nk],
                                                RSB[:, par, S - nk:S], -1.0, 3.0e38, ALU.add, ALU.min, nmx[:, i:i + 1]
                                                ).then_inc(s_max, 1)
                        if i == 7:
                            dve.wait_ge(s_exp, u + 1)
                            V_.reciprocal(rinv[:], sums[:]).then_inc(s_ri, 1)
                        if i == 1 and not first:
                            finish(h - 1, 1, s_ri, s_co, s_pv, s_tmp, s_o)

                head_selected(0, 0, True)
                with dve.Fori(0, HPG // 2 - 1) as t:
                    head_selected(t * 2 + 1, 1)
                    head_selected(t * 2 + 2, 0)
                head_selected(HPG - 1, 1)
                finish(HPG - 1, 1, s_ri, s_co, s_pv, s_tmp, s_o)

            for n in range(2 * KC):
                dve.wait_ge(x_hi, n + 1 + XL0)
                cols = slice((n % 2) * HALF, (n % 2 + 1) * HALF)
                V_.tensor_tensor(U_lo[:, n // 2, cols], ps[:, n % 4, :], U_hi[:, n // 2, cols].bitcast(F32),
                                 ALU.subtract).then_inc(x_lo, 1)
            add_out(1)
            dve.wait_ge(o_added, 32)
            norm(3, G_MLP1)
            mlp_dve(dve, 1)
            dve.wait_ge(dn_free, 4 + 16 * MLP_UNITS)
            dve.sem_inc(out_done, 1)


def layouts(inp):
    import math

    import numpy as np

    a = {k: np.asarray(v) for k, v in inp.items()}
    f = np.float32

    def cols(w, n=COLS):
        out = []
        for c in range(0, w.shape[1], n):
            p = np.zeros((P, KC, n), f)
            part = w[:, c:c + n]
            p[:, :, :part.shape[1]] = part.reshape(KC, P, -1).transpose(1, 0, 2)
            out.append(p.reshape(P, PIECE))
        return out

    def flat(w, kc):
        p = np.zeros((P, PIECE), f)
        v = w.reshape(kc, P, -1).transpose(1, 0, 2).reshape(P, -1)
        p[:, :v.shape[1]] = v
        return p

    pieces = cols(a["hy_w_in"][0])
    ukv = a["mla_w_ukv"][0].reshape(KVR, MH, MNOPE + MV)
    ukv = np.concatenate([ukv[:, :, :MNOPE].reshape(KVR, -1), ukv[:, :, MNOPE:].reshape(KVR, -1)], axis=1)
    pieces.append(flat(ukv, KVC))
    uq = a["mla_w_uq"][0]
    pieces += [flat(uq[:, 384 * j:384 * (j + 1)], QRC) for j in range(2)]
    pieces += cols(a["hy_w_out"][0])

    def mlp(layer):
        w1, w2 = a["mlp_w1"][layer], a["mlp_w2"][layer]
        for g in range(FF // COLS):
            pieces.append(cols(w1[:, g * COLS:(g + 1) * COLS])[0])
            pieces.append(flat(w2[g * COLS:(g + 1) * COLS], COLS // P))

    mlp(0)
    w = a["nsa_w_in"][0]
    n0 = NH * DK
    part = [w[:, n0 + 128 * j:n0 + 128 * (j + 1)] for j in range(6)]
    pieces += cols(w[:, :n0]) + cols(np.concatenate(part[0:2], 1)) + cols(np.concatenate(part[2:4], 1))
    pieces += cols(np.concatenate(part[4:6], 1)) + cols(w[:, n0 + 768:]) + cols(a["nsa_w_out"][0])
    mlp(1)
    assert len(pieces) == N_PIECES
    half = ROPE // 2
    freqs = f(10000.0) ** (-np.arange(half, dtype=f) / f(half))
    ang = np.arange(S).astype(f)[:, None] * freqs[None, :]
    tok = lambda x: x.reshape(NT, P, -1).transpose(1, 0, 2).reshape(P, -1)
    cst = np.zeros((P, N_CST), f)
    cst[:, C_ID:C_ID + P] = np.eye(P)
    cst[:, C_CAUS:C_CAUS + P] = np.where(np.arange(P)[None, :] <= np.arange(P)[:, None], 0.0, NEG)
    cst[:, C_ROPE:C_ROPE + 128] = tok(np.cos(ang).astype(f))
    cst[:, C_ROPE + 128:C_ROPE + 256] = tok(np.sin(ang).astype(f))
    cs0 = np.arange(NCMP) * 16
    ss0 = np.arange(NSEL) * 64
    ov = np.clip(np.minimum(cs0[:, None] + 32, ss0[None] + 64) - np.maximum(cs0[:, None], ss0[None]), 0, None) / 32
    cst[:NCMP, C_OV:C_OV + NSEL] = ov
    cst[:, C_V0:C_V0 + NT] = tok((np.arange(S) >= 31).astype(f))[::-1, ::-1]
    q = np.arange(S)
    cur = q // 64
    blk = np.arange(NSEL)
    valid = ss0[None] <= q[:, None]
    forced = (blk[None] == 0) | (blk[None] == cur[:, None]) | (blk[None] == cur[:, None] - 1)
    sel = np.concatenate([np.eye(P, dtype=f), tok((valid & ~forced).astype(f)),
                          tok(np.where(valid & forced, 1e4, np.where(valid, 0.0, -1.0)).astype(f))], 1)[::-1]
    n = np.arange(S)
    nf = np.maximum(n, 1).astype(f)
    bucket = 16 + (np.log(nf / f(16)) / f(math.log(64)) * f(16)).astype(np.int32)
    bucket = np.where(n < 16, n, np.minimum(bucket, 31))

    def rows(dist, top):
        m = np.zeros((33, len(dist)), f)
        ok = (dist >= 0) & (dist < top)
        m[bucket[dist[ok]], np.nonzero(ok)[0]] = 1
        m[32, ~ok] = NEG
        return m

    onehot = np.concatenate([rows(S - 1 - np.arange(ES_N), S), rows(639 - np.arange(EW_N), 512),
                             rows(992 - np.arange(1120), S)], 1)
    blkind = np.zeros((NSEL, NG, S), f)
    blkind[np.arange(S) // 64, :, np.arange(S)] = 1
    relx = np.concatenate([a["rel_bias"], np.ones((1, NH), f)], 0)
    vec = lambda x: x.reshape(-1, P).T
    prm = np.zeros((P, N_PRM), f)
    for g, x in ((G_MIX0, a["norm_mix"][0]), (G_MLP0, a["norm_mlp"][0]), (G_MIX1, a["norm_mix"][1]),
                 (G_MLP1, a["norm_mlp"][1]), (G_CB, a["lru_conv_b"][0]), (G_BA, a["lru_ba"][0].reshape(-1)),
                 (G_BX, a["lru_bx"][0].reshape(-1)), (G_LAM, a["lru_lambda"][0]), (G_QN, a["mla_q_norm"][0]),
                 (G_KVN, a["mla_kv_norm"][0])):
        v = vec(x)
        prm[:, g:g + v.shape[1]] = v
    prm[:, G_CW:G_CW + 16] = a["lru_conv_w"][0].reshape(CONV, LC, P).transpose(2, 1, 0).reshape(P, 16)
    prm[:, G_GQ:G_GQ + MQK] = a["mla_qn_q"][0][None]
    prm[:, G_GK:G_GK + MQK] = a["mla_qn_k"][0][None]
    prm[:DK, G_Q1] = a["nsa_q_norm"][0]
    prm[:DK, G_K1:G_K1 + 3] = a["nsa_k_norm"][0].T
    for j, x in enumerate((a["nsa_cmp_pos_k"][0], a["nsa_cmp_pos_v"][0])):
        prm[:, G_POS + 16 * j:G_POS + 16 * (j + 1)] = x.reshape(16, 2 * DK).T
    gatew = np.zeros((P, 2, LC, P), f)
    for j, x in enumerate((a["lru_wa"][0], a["lru_wx"][0])):
        for b in range(8):
            o = b % 2 * 64
            gatew[o:o + 64, j, b // 2, o:o + 64] = x[b]
    w1c = np.stack([a["nsa_cmp_w1_k"][0], a["nsa_cmp_w1_v"][0]]).reshape(2, 16, P, CMP_HID).transpose(2, 0, 1, 3)
    w2c = np.stack([a["nsa_cmp_w2_k"][0], a["nsa_cmp_w2_v"][0]]).reshape(2, 2, P, DK).transpose(2, 0, 1, 3)
    xT = a["x"][0].T.reshape(KC, P, S).transpose(1, 0, 2)
    arrays = dict(xT=xT, pieces=np.stack(pieces), cst=cst, sel=sel, prm=prm, gatew=gatew, relx=relx, onehot=onehot,
                  w1c=w1c, w2c=w2c, blkind=blkind)
    return {k: np.ascontiguousarray(v, dtype=f) for k, v in arrays.items()}


def kernel(**inputs):
    import numpy as np
    import concourse.bacc as bacc
    from concourse.bass_utils import run_bass_kernel_spmd

    arrays = layouts(inputs)
    nc = bacc.Bacc("TRN2", target_bir_lowering=False, num_devices=1)
    args = [nc.dram_tensor("in_" + k, v.shape, F32, kind="ExternalInput").ap() for k, v in arrays.items()]
    out = nc.dram_tensor("out_h", (P, KC, S), F32, kind="ExternalOutput").ap()
    build_program(nc, *args, out)
    r = run_bass_kernel_spmd(nc, [{"in_" + k: v for k, v in arrays.items()}], core_ids=[0])
    h = r.results[0]["out_h"]
    return np.ascontiguousarray(h.transpose(1, 0, 2).reshape(1, D, S).transpose(0, 2, 1))
```

```python
from contextlib import ExitStack

import concourse.bass as bass
from concourse import mybir

F32 = mybir.dt.float32
F32R = mybir.dt.float32r
ALU = mybir.AluOpType
ACT = mybir.ActivationFunctionType
AX = mybir.AxisListType.X

P = 128
S = 1024
D = 1024
NT = S // P
KC = D // P
HALF = 512
FF = 4096
PIECE = 2048
COLS = PIECE // KC
EPS = 1e-6
NEG = -1e30

LW = 512
LC = LW // P
CONV = 4
QR, KVR, ROPE = 384, 256, 32
QRC, KVC = QR // P, KVR // P
MH, MQK, MNOPE, MV = 8, 96, 64, 64
NH, NG, HPG, DK = 16, 2, 8, 64
NCMP = 63
CMP_HID = 256
NSEL = 16
WB = 4
GATES = 3 * NH
ES_N = S + P - 1
EW_N = WB * P + 2 * P - 1
RW = (WB + 1) * P
CB_N = 119
FILL = -3.0e38

P_IN0 = 0
P_UKV = 7
P_UQ = 8
P_OUT0 = 10
P_MLP0 = 14
P_IN1 = P_MLP0 + 2 * (FF // COLS)
P_KC1 = P_IN1 + 4
P_KV1 = P_IN1 + 5
P_GATE1 = P_IN1 + 7
P_OUT1 = P_IN1 + 8
P_MLP1 = P_OUT1 + 4
N_PIECES = P_MLP1 + 2 * (FF // COLS)

C_ID, C_CAUS, C_ROPE, C_OV, C_V0 = 0, 128, 256, 512, 528
N_CST = 536
C_REV = C_CAUS
G_MIX0, G_MLP0, G_MIX1, G_MLP1 = 0, 8, 16, 24
G_CW, G_CB, G_BA, G_BX, G_LAM = 32, 48, 52, 56, 60
G_QN, G_KVN, G_GQ, G_GK = 64, 67, 69, 165
G_Q1, G_K1, G_POS = 261, 262, 265
G_GQC, G_GKC = 297, 298
N_PRM = 299


def build_program(nc, xT, pieces, cst, sel, prm, gatew, relx, onehot, w1c, w2c, blkind, out):
    ctx = ExitStack()
    with ctx:
        base = (nc.sbuf_base + 63) // 64 * 64
        A0, A_W = 0, 14848
        B0 = A0 + A_W
        W0 = B0 + 16384
        G0 = W0 + 16384
        C0 = G0 + 4096

        def at(name, word, shape, dt=F32):
            return nc.alloc_sbuf_tensor_at(name, shape, dt, offset=base + 4 * word)

        def sem(name):
            return ctx.enter_context(nc.semaphore(name))

        def dram(name, shape):
            return nc.dram_tensor(name, shape, F32, kind="Internal").ap()

        ps = ctx.enter_context(nc.psum_tensor("ps", [P, 8, HALF], F32))

        def bank(b, n=1):
            return ps[:, b:b + n, :].rearrange("p b n -> p (b n)")

        top = [C0]

        def small(name, n, dt=F32):
            t = at(name, top[0], [P, n], dt)
            top[0] += (n + 7) // 8 * 8
            return t

        cs = small("cs", N_CST)
        pr = small("pr", N_PRM)
        ones = small("ones", P)
        msq = small("msq", 16)
        rsd = small("rsd", 16)
        ss = small("ss", 128)
        rs = small("rs", 128)
        ssk = small("ssk", 32)
        rsk = small("rsk", 32)
        nmx = small("nmx", 8)
        sums = small("sums", 16)
        rinv = small("rinv", 8)
        coef = small("coef", 8)
        cmx = small("cmx", 8)
        sm = small("sm", 32)
        assert (top[0]) * 4 + base <= nc.sbuf_usable_end, (top[0] * 4 + base, nc.sbuf_usable_end)
        ident = cs[:, C_ID:C_ID + P]
        causal = cs[:, C_CAUS:C_CAUS + P]
        reverse = cs[:, C_REV:C_REV + P]

        H = at("H", A0, [P, KC, S])
        hid_hi = at("hid_hi", A0 + 8192, [P, 2, 2, HALF], F32R)
        hid_lo = at("hid_lo", A0 + 10240, [P, 2, 2, HALF], F32R)
        relu = at("relu", A0 + 12288, [P, 2, HALF])
        sqr = at("sqr", A0 + 13312, [P, 2, HALF])
        nacc = at("nacc", A0 + 8192, [P, S])
        ndiag = at("ndiag", A0 + 9216, [P, NT, P])
        nuf = at("nuf", A0 + 10240, [P, 2, S])
        nsq = at("nsq", A0 + 12288, [P, 2, S])
        U_hi = at("U_hi", B0, [P, KC, S], F32R)
        U_lo = at("U_lo", B0 + 8192, [P, KC, S], F32R)
        W_hi = at("W_hi", W0, [P, 4, PIECE], F32R)
        W_lo = at("W_lo", W0 + 8192, [P, 4, PIECE], F32R)
        stage = at("stage", G0, [P, 2, PIECE])
        oh = at("oh", B0, [33, ES_N + EW_N + 1120])
        esb = at("esb", B0 + 3200, [NH, ES_N + EW_N])
        cbs = at("cbs", B0 + 5400, [P, NH, CB_N])
        rel = at("rel", B0 + 7400, [33, NH])
        lr = at("lr", A0, [P, LC, S])
        xg = at("xg", A0 + 4096, [P, LC, S])
        krope = at("krope", A0 + 8192, [32, S])
        kvlat = at("kvlat", A0 + 9216, [P, KVC, S])
        qlat = at("qlat", A0 + 11264, [P, QRC, S])
        xc = at("xc", B0, [P, LC, S])
        lra = at("lra", B0 + 4096, [P, LC, S])
        lri = at("lri", B0 + 8192, [P, LC, S])
        lrt = at("lrt", B0 + 12288, [P, 2, S])
        gw = at("gw", B0 + 14336, [P, 2, LC, P])
        lsq = at("lsq", A0 + 4096, [P, 2, S])
        lacc = at("lacc", A0 + 6144, [P, 2, S])
        Q = at("Q", A0 + 4096, [P, NT, MH, MQK])
        mla_out = Q[:].rearrange("p t h d -> p t (h d)")
        K = at("K", B0, [P, NT, MH, MQK])
        V = at("V", B0 + 6144, [P, NT, MH * MV])
        kvl_hi = at("kvl_hi", B0 + 10240, [P, KVC, S], F32R)
        kvl_lo = at("kvl_lo", B0 + 12288, [P, KVC, S], F32R)
        ql_hi = at("ql_hi", B0 + 10240, [P, QRC, S], F32R)
        ql_lo = at("ql_lo", B0 + 13312, [P, QRC, S], F32R)
        hsq = at("hsq", B0 + 10240, [P, NT, MH, MQK])
        ropet = at("ropet", B0 + 10240, [P, 4, NT, MH, 16])
        QT = at("QT", A0 + 10240, [P, 2, S])
        KT = at("KT", A0 + 12288, [P, 2, S])
        stq = at("stq", B0 + 10240, [P, NT, MQK])
        stk = at("stk", B0 + 11008, [P, NT, MQK])
        prob = at("prob", B0 + 11776, [P, 2, S])
        probT = at("probT", B0 + 13824, [P, 2, S])
        ZQ = at("ZQ", A0, [P, NT, NH * DK])
        KV = at("KV", A0 + 8192, [P, NT, 4, NG, DK])
        KCV = at("KCV", A0 + 12288, [P, 2, S])
        GATE = at("GATE", A0 + 14336, [P, NT, GATES])
        T4 = at("T4", B0, [P, 4, S])
        W1C = [at("W1C%d" % k, W0 + 4096 + 8192 * (k % 2) + 2048 * (k // 2), [P, 8, CMP_HID]) for k in range(4)]
        TP = at("TP", B0 + 12288, [P, 2, 16, NCMP])
        HC = at("HC", B0 + 14336, [NCMP, 4, CMP_HID])
        HCT = at("HCT", B0 + 15360, [P, 4, 2, NCMP])
        W2C = at("W2C", B0 + 15872, [P, 2, 2, DK])
        CKN = at("CKN", A0 + 12288, [NCMP, NG, DK])
        CKT = at("CKT", A0 + 12416, [P, NG, NCMP])
        CV = at("CV", A0 + 12544, [NCMP, NG, DK])
        KST = at("KST", B0, [P, NG, S])
        KWT = at("KWT", B0 + 2048, [P, NG, S])
        QTG = at("QTG", B0 + 4096, [DK, HPG, S])
        QA = at("QA", W0 + 9216, [P, 2, S])
        PW = at("PW", B0 + 12288, [P, 2, RW])
        PTW = at("PTW", B0 + 13568, [P, 2, RW])
        PTC = at("PTC", B0 + 14848, [NCMP, S])
        MT16 = at("MT16", B0 + 14848, [NSEL, S])
        P1 = at("P1", W0 + 11264, [P, 2, S])
        PT1 = at("PT1", W0 + 13312, [P, 2, S])
        STQ = at("STQ", A0 + 12800, [P, NT, DK])
        TMPO = at("TMPO", A0 + 13312, [P, NT, DK])
        PACC = at("PACC", A0 + 13824, [P, NT, NCMP])
        SW = at("SW", W0, [P, 2, RW])
        RWB = at("RWB", W0 + 1280, [P, 2, RW])
        CB = at("CB", W0 + 2560, [P, HPG, CB_N])
        PC = at("PC", W0 + 3520, [P, NT, NCMP])
        SS1 = at("SS1", W0 + 4096, [P, 2, S])
        RSB = at("RSB", W0 + 6144, [P, 2, S])
        SCO = at("SCO", W0 + 8192, [P, NT, NSEL])
        REP = at("REP", W0 + 8320, [P, NT, NSEL])
        M8 = at("M8", W0 + 8448, [P, NT, 8])
        SQ1 = at("SQ1", W0, [P, 2, S])
        CTMP = at("CTMP", W0 + 8704, [NCMP, NG, DK])
        q_gain8 = sm[0:DK, 28:29]

        es_d = dram("es_d", [NH, ES_N])
        ew_d = dram("ew_d", [NH, EW_N])
        cb_d = dram("cb_d", [NG, P, HPG, CB_N])
        h_d = dram("h_d", [P, KC, S])

        loaded = [sem("piece_loaded0"), sem("piece_loaded1")]
        split_hi = sem("piece_hi")
        ready = sem("piece_ready")
        used = sem("piece_used")
        const_in = sem("const_in")
        x_in = sem("x_in")
        gw_in = sem("gw_in")
        oh_in = sem("oh_in")
        ones_ok = sem("ones_ok")
        waited = sem("register_waited")
        zeroed = sem("rows_zeroed")
        b_ready, b_evac, cb_ok, b_out = sem("bias_ready"), sem("bias_evac"), sem("cmp_bias"), sem("bias_out")
        n_sq, n_acc, n_ssq, n_ms, n_sd, n_rs, n_dg, n_bc, n_uf, n_hi, n_lo = (
            sem("norm_" + x) for x in "sq acc ssq ms sd rs dg bc uf hi lo".split())
        z_ready, z_evac = sem("z_ready"), sem("z_evac")
        sp_dve, sp_act = sem("softplus_dve"), sem("softplus_act")
        l_cv, l_conv, l_gate, l_sig, l_tanh, l_exp, l_ix, l_aa, l_t2, l_mult, l_b, l_scan, l_done = (
            sem("lru_" + x) for x in "cv conv gate sig tanh exp ix aa t2 mult b scan done".split())
        m_sq, m_acc, m_ssq, m_ms, m_sd, m_rs, m_g, m_hi, m_lo = (
            sem("lat_" + x) for x in "sq acc ssq ms sd rs gain hi lo".split())
        m_rope, m_krope, m_up, m_upev = sem("krope_T"), sem("krope_in_K"), sem("up_ready"), sem("up_evac")
        h_sq, h_red, h_ms, h_sd, h_rs, q_nrm, k_nrm = (
            sem("head_" + x) for x in "sq red ms sd rs q k".split())
        a_st, a_tr, a_trev, a_qk, a_max, a_exp, a_tp, a_tpev, a_pv, a_ri, a_out = (
            sem("mla_" + x) for x in "staged tr trev qk max exp tp tpev pv rinv out".split())
        a_diag = sem("mla_diag")
        x_tr, x_hi, x_lo = sem("mix_T"), sem("mix_hi"), sem("mix_lo")
        o_ready, o_added = sem("oproj_ready"), sem("oproj_added")
        h_in, h_spill = sem("h_reload"), sem("h_spilled")
        up_ready, up_free, relu_ok, sq_ok, sq_free, hh, hl, dn_ready, dn_free = (
            sem("mlp_" + x) for x in
            "up_ready up_free relu sq sq_free hid_hi hid_lo down_ready down_free".split())
        out_done = sem("out_done")
        w_in, t4_in, ki_in = sem("cmp_w_in"), sem("cmp_T4_in"), sem("block_rows_in")
        c_tp, c_mm, c_gelu, c_hT, c_hTev, c_out, c_sm, c_sd, c_ckT, c_ck, c_gate = (
            sem("cmp_" + x) for x in "TP mm gelu hT hTev out small sd ckT ck gate".split())
        k_sc, k_tr, k_trev = (sem("nsa_k_" + x) for x in "scaled tr trev".split())
        g_in, rw_in, rs_in, mk_in = sem("cb_in"), [sem("rw_in0"), sem("rw_in1")], [sem("rs_in0"), sem("rs_in1")], sem("mask_in")
        t_st, t_tr, t_ev, t_kept, t_back = (sem("q_" + x) for x in "staged T Tev kept back".split())
        e_qk, e_dve, e_exp, e_p, e_acc, e_tp, e_tpev, e_pv, e_o = (
            sem("c_" + x) for x in "qk dve exp p acc tp tpev pv o".split())
        w_qk, w_max, w_exp, w_tp, w_tpev, w_pv, w_ri, w_o = (
            sem("w_" + x) for x in "qk max exp tp tpev pv ri o".split())
        s_qk, s_max, s_exp, s_tp, s_tpev, s_pv, s_ri, s_o = (
            sem("s_" + x) for x in "qk max exp tp tpev pv ri o".split())
        f_co, f_tmp = sem("finish_coef"), sem("finish_gated")
        i_tp, i_tpev, i_mm, i_dve, i_mask, i_mtr, i_mtrev = (
            sem("imp_" + x) for x in "tp tpev mm dve mask mtr mtrev".split())
        e_norm = sem("c_norm")

        block = ctx.enter_context(nc.Block())

        MLP_UNITS = 2 * (FF // COLS)

        def word(i):
            return i % 4

        def alone(eng):
            eng.sem_inc(waited, 1)

        def rotate(eng, api, X, slot, done, n):
            cos = cs[:, C_ROPE:C_ROPE + 128].rearrange("p (t d) -> p t d", t=NT).unsqueeze(2).to_broadcast([P, NT, MH, 16])
            sin = cs[:, C_ROPE + 128:C_ROPE + 256].rearrange("p (t d) -> p t d", t=NT).unsqueeze(2).to_broadcast([P, NT, MH, 16])
            x1, x2 = X[:, :, :, 64:80], X[:, :, :, 80:96]
            t1, t2 = ropet[:, slot], ropet[:, slot + 1]
            eng.wait_ge(done, n)
            api.tensor_tensor(t1, x1, sin, ALU.mult).then_inc(done, 1)
            api.tensor_tensor(t2, x2, sin, ALU.mult).then_inc(done, 1)
            eng.wait_ge(done, n + 2)
            api.tensor_tensor(x1, x1, cos, ALU.mult).then_inc(done, 1)
            api.tensor_tensor(x2, x2, cos, ALU.mult).then_inc(done, 1)
            eng.wait_ge(done, n + 4)
            api.tensor_tensor(x1, x1, t2, ALU.subtract).then_inc(done, 1)
            api.tensor_tensor(x2, x2, t1, ALU.add).then_inc(done, 1)

        KT_POOL = 3

        def scale_keys(api, t):
            return api.tensor_tensor(K[:, t], K[:, t], rs[:, 64 + 8 * t:72 + 8 * t].unsqueeze(2).to_broadcast([P, MH, MQK]),
                                     ALU.mult)

        def gain_rope(api, X, g):
            x = X[:].rearrange("p t h d -> p (t h) d")[:, :, MNOPE:MQK]
            return api.tensor_tensor(x, x, pr[:, g + MNOPE:g + MQK].unsqueeze(1).to_broadcast([P, NT * MH, ROPE]), ALU.mult)

        def turned_pair(t, c):
            return mla_out[:, t, c * P:(c + 1) * P]

        def mlp_pe(pe, first_units, mm3, piece_read, piece_read_now, p0, layer):
            u0 = MLP_UNITS * layer

            def up(n, q):
                s, g = q % 2, q // 2
                if s == 0:
                    pe.wait_ge(ready, n_piece(n, q) + 1)
                for j in range(2):
                    pe.wait_ge(up_free, (n + u0) * 2 + j + 1)
                    b = 2 * s + j
                    for kc in range(KC):
                        w = slice(kc * COLS + j * P, kc * COLS + (j + 1) * P)
                        m = mm3(ps[:, b, :], W_hi[:, word(p0 + 2 * g), w], W_lo[:, word(p0 + 2 * g), w],
                                U_hi[:, kc, s * HALF:(s + 1) * HALF], U_lo[:, kc, s * HALF:(s + 1) * HALF],
                                kc == 0, kc == KC - 1)
                    m.then_inc(up_ready, 1)
                if s == 1:
                    piece_read()

            def n_piece(n, q):
                return p0 + (n - q) + 2 * (q // 2)

            def down(n, q):
                s, g = q % 2, q // 2
                if s == 0:
                    pe.wait_ge(ready, n_piece(n, q) + 2)
                pe.wait_ge(hl, (n + u0) * 2 + 2)
                for dc in range(KC):
                    pe.wait_ge(dn_free, (n + u0) * 8 + dc + 1)
                    for j in range(2):
                        w = slice(j * 1024 + dc * P, j * 1024 + (dc + 1) * P)
                        m = mm3(ps[:, 4 + dc % 4, :], W_hi[:, word(p0 + 2 * g + 1), w], W_lo[:, word(p0 + 2 * g + 1), w],
                                hid_hi[:, s, j, :], hid_lo[:, s, j, :], j == 0, j == 1)
                    m.then_inc(dn_ready, 1)
                if s == 1 and q == 1:
                    piece_read()
                elif s == 1:
                    piece_read_now(dn_ready, (n + u0) * 8 + 9)

            def up_bank(b):
                s, j = b // 2, b % 2

                def operands(kc):
                    w = slice(kc * COLS + j * P, kc * COLS + (j + 1) * P)
                    return (ps[:, b, :], W_hi[:, word(p0), w], W_lo[:, word(p0), w],
                            U_hi[:, kc, s * HALF:(s + 1) * HALF], U_lo[:, kc, s * HALF:(s + 1) * HALF])
                return operands

            pe.wait_ge(ready, p0 + 1)
            pe.wait_ge(up_free, 2 * u0 + 4)
            first_units(2 * layer + 1, [up_bank(b) for b in range(4)], up_ready)
            piece_read()
            down(0, 0)
            for q in range(1, 4):
                up(q + 1, (q + 1) % 4)
                down(q, q)
            n_it = MLP_UNITS // 4
            with pe.Fori(1, n_it - 1) as t:
                for q in range(4):
                    up(t * 4 + (q + 1), (q + 1) % 4)
                    down(t * 4 + q, q)
            for q in range(4):
                n = (n_it - 1) * 4 + q
                if q < 3:
                    up(n + 1, q + 1)
                down(n, q)

        def mlp_act(act, layer):
            A = nc.scalar.activation
            u0 = MLP_UNITS * layer

            def hidden(n, q):
                for j in range(2):
                    act.wait_ge(up_ready, (n + u0) * 2 + j + 1)
                    A(relu[:, j, :], ps[:, 2 * (q % 2) + j, :], ACT.Relu).then_inc(up_free, 1)
                    act.wait_ge(sq_free, (n + u0) * 2 + j + 1)
                    act.wait_ge(up_free, (n + u0) * 2 + j + 5)
                    A(sqr[:, j, :], relu[:, j, :], ACT.Square).then_inc(sq_ok, 1)

            hidden(0, 0)
            n_it = MLP_UNITS // 4
            with act.Fori(0, n_it - 1) as t:
                for q in range(4):
                    hidden(t * 4 + (q + 1), (q + 1) % 4)
            for q in range(3):
                hidden((n_it - 1) * 4 + q + 1, q + 1)

        def mlp_dve(dve, add_squares, layer):
            V_ = nc.vector
            u0 = MLP_UNITS * layer

            def hidden(n, q, first=False):
                for j in range(2):
                    dve.wait_ge(sq_ok, (n + u0) * 2 + j + 1)
                    if not first:
                        dve.wait_ge(dn_ready, (n + u0) * 8 - 7)
                    V_.tensor_copy(hid_hi[:, q % 2, j, :], sqr[:, j, :]).then_inc(hh, 1)
                    dve.wait_ge(hh, (n + u0) * 2 + j + 1)
                    V_.tensor_tensor(hid_lo[:, q % 2, j, :], sqr[:, j, :], hid_hi[:, q % 2, j, :].bitcast(F32),
                                     ALU.subtract).then_inc(hl, 1)
                dve.wait_ge(hl, (n + u0) * 2 + 2)
                dve.sem_inc(sq_free, 2)

            def add(n, q, last=False):
                cols = slice((q % 2) * HALF, (q % 2 + 1) * HALF)
                for dc in range(KC):
                    dve.wait_ge(dn_ready, (n + u0) * 8 + dc + 2)
                    dve.wait_ge(dn_free, (n + u0) * 8 + dc + 4)
                    V_.tensor_tensor(H[:, dc, cols], H[:, dc, cols], ps[:, 4 + dc % 4, :], ALU.add
                                     ).then_inc(dn_free, 1)
                    if last and layer == 0:
                        add_squares(2, dc - 1)

            hidden(0, 0, True)
            n_it = MLP_UNITS // 4
            with dve.Fori(0, n_it - 1) as t:
                for q in range(4):
                    hidden(t * 4 + (q + 1), (q + 1) % 4)
                    add(t * 4 + q, q)
            for q in range(4):
                n = (n_it - 1) * 4 + q
                if q < 3:
                    hidden(n + 1, q + 1)
                add(n, q, q == 3)


        SP_COUNT = 27
        Z0 = 28
        Z1_UNITS = 60
        X0, XL0 = 8, 12
        HD0 = 2 * NT

        @block.sync
        def _(sp):
            def load(p, k):
                nc.sync.dma_start(stage[:, k % 2, :], pieces[p, :, :]).then_inc(loaded[k % 2], 16)

            load(0, 0)
            load(1, 1)
            with sp.Fori(0, (P_MLP0 - 2) // 4) as t:
                for j in range(4):
                    sp.wait_ge(ready, t * 4 + (j + 1))
                    load(t * 4 + (j + 2), j)
            with sp.Fori(0, (P_OUT1 - P_MLP0) // 4) as t:
                for j in range(4):
                    sp.wait_ge(ready, t * 4 + (P_MLP0 + j - 1))
                    load(t * 4 + (P_MLP0 + j), j)
            nc.sync.dma_start(cs[:, C_REV:C_ROPE + 256], sel[:, :]).then_inc(const_in, 16)
            for k in range(4):
                sp.wait_ge(used, P_KC1 + 1 + k // 2)
                nc.sync.dma_start(W1C[k][:], w1c[:, k // 2, 8 * (k % 2):8 * (k % 2) + 8, :]).then_inc(w_in, 16)
            for p in range(P_OUT1, P_OUT1 + 2):
                sp.wait_ge(ready, p - 1)
                load(p, p)
            sp.wait_ge(z_evac, Z1_UNITS + Z0)
            nc.sync.dma_start(W2C[:], w2c[:, :, :, :]).then_inc(w_in, 16)
            for kv in range(2):
                for g in range(NG):
                    rows = slice(DK * g, DK * (g + 1))
                    nc.sync.dma_start(T4[0:DK, 2 * kv + g, :], KCV[rows, kv, :]).then_inc(t4_in, 16)
                    nc.sync.dma_start(T4[DK:P, 2 * kv + g, 0:S - 1], KCV[rows, kv, 1:S]).then_inc(t4_in, 16)
            sp.wait_ge(zeroed, 6)
            nc.sync.dma_start(KST[DK:DK + NSEL, :, :], blkind[:, :, :]).then_inc(ki_in, 16)
            sp.wait_ge(h_red, NT + 2 + HD0)
            for g in range(NG):
                if g:
                    sp.wait_ge(e_dve, g * 24)
                nc.sync.dma_start(CB[:], cb_d[g]).then_inc(g_in, 16)
                for h in range(HPG):
                    if g * HPG + h >= 2:
                        sp.wait_ge(w_max, g * 64 + 8 * (h - 1) + 1)
                    src = ew_d[g * HPG + h:g * HPG + h + 1, :]
                    src = bass.AP(src.tensor, src.offset, [[1, P], [1, RW]])
                    nc.sync.dma_start(RWB[:, h % 2, :], src).then_inc(rw_in[h % 2], 16)
                sp.wait_ge(i_mtrev, g + 1)
                for k in range(2):
                    nc.sync.dma_start(QA[DK:DK + NSEL, k, :], MT16[:]).then_inc(mk_in, 16)
                for h in range(HPG):
                    if g * HPG + h >= 2:
                        sp.wait_ge(s_max, g * 64 + 8 * (h - 1) + 1)
                    src = es_d[g * HPG + h:g * HPG + h + 1, :]
                    src = bass.AP(src.tensor, src.offset, [[1, P], [1, S]])
                    nc.sync.dma_start(RSB[:, h % 2, :], src).then_inc(rs_in[h % 2], 16)
            for p in range(P_OUT1 + 2, P_MLP1):
                sp.wait_ge(ready, p - 1)
                load(p, p)
            with sp.Fori(0, (N_PIECES - P_MLP1) // 4) as t:
                for j in range(4):
                    sp.wait_ge(ready, t * 4 + (P_MLP1 + j - 1))
                    load(t * 4 + (P_MLP1 + j), j)

        @block.gpsimd
        def _(pool):
            nc.gpsimd.memset(ones[:], 1.0).then_inc(ones_ok, 1)
            pool.sem_inc(t_kept, 1)

            def split(t, p0, j):
                k = p0 + j
                pool.wait_ge(loaded[k % 2], (t * 4 + k - k % 2) * 8 + 16)
                if not (isinstance(t, int) and 4 * t + k < 4):
                    pool.wait_ge(used, t * 4 + (k - 3))
                alone(pool)
                nc.gpsimd.tensor_copy(W_hi[:, k % 4, :], stage[:, k % 2, :]).then_inc(split_hi, 1)
                pool.wait_ge(split_hi, t * 4 + (k + 1))
                nc.gpsimd.tensor_tensor(W_lo[:, k % 4, :], stage[:, k % 2, :],
                                        W_hi[:, k % 4, :].bitcast(F32), ALU.subtract).then_inc(ready, 1)

            for j in range(4):
                split(0, 0, j)
            with pool.Fori(1, 2) as t:
                for j in range(4):
                    split(t, 0, j)
            for j in range(3):
                split(0, 8, j)

            for c in range(LC):
                pool.wait_ge(l_exp, c + 1)
                pool.wait_ge(l_ix, c + 1)
                nc.gpsimd.tensor_tensor(xc[:, c, :], lra[:, c, :], lra[:, c, :], ALU.mult).then_inc(l_aa, 1)
            for c in range(LC):
                pool.wait_ge(l_scan, c + 1)
                nc.gpsimd.tensor_tensor(lr[:, c, :], lr[:, c, :], xg[:, c, :], ALU.mult).then_inc(l_done, 1)

            for p in range(11, P_MLP0):
                split(0, p, 0)

            pool.wait_ge(h_rs, 2)
            for t in range(KT_POOL):
                scale_keys(nc.gpsimd, t).then_inc(k_nrm, 1)
            pool.wait_ge(k_nrm, NT)
            gain_rope(nc.gpsimd, K, G_GK).then_inc(k_nrm, 1)
            rotate(pool, nc.gpsimd, K, 2, k_nrm, NT + 1)

            pool.wait_ge(m_lo, KVC + QRC)
            pool.wait_ge(m_up, 4 * NT)
            pool.wait_ge(k_nrm, NT + 7)
            for rows in (QT, KT):
                nc.gpsimd.memset(rows[MQK:P], 0.0).then_inc(zeroed, 1)
            pool.wait_ge(zeroed, 2)

            with pool.Fori(0, (P_OUT1 - P_MLP0) // 4) as t:
                for j in range(4):
                    split(t, P_MLP0, j)
            pool.wait_ge(h_rs, 2 + 2)
            rs_t = rs[:].rearrange("p (t h) -> p t h", t=NT)
            pool.wait_ge(c_tp, 4)
            for rows in (KST, KWT, QA, CKT):
                nc.gpsimd.memset(rows[DK:P], 0.0).then_inc(zeroed, 1)
            pool.wait_ge(zeroed, 6)
            with pool.Fori(0, NG) as g:
                def stage_q(h):
                    pool.wait_ge(t_tr, g * 16 + h * 2 + 1)
                    head = g * HPG + h
                    nc.gpsimd.tensor_tensor(STQ[:], ZQ[:, :, bass.ds(head * DK, DK)],
                                            rs_t[:, :, bass.ds(head, 1)].to_broadcast([P, NT, DK]), ALU.mult
                                            ).then_inc(t_st, 1)

                def keep_q(h, par):
                    pool.wait_ge(t_ev, g * 16 + h * 2 + 3)
                    alone(pool)
                    nc.gpsimd.tensor_copy(QTG[:, bass.ds(h, 1), :].rearrange("p o n -> p (o n)"), QA[0:DK, par, :]
                                          ).then_inc(t_kept, 1)

                stage_q(0)
                with pool.Fori(0, HPG // 2 - 1) as t:
                    stage_q(t * 2 + 1)
                    keep_q(t * 2, 0)
                    stage_q(t * 2 + 2)
                    keep_q(t * 2 + 1, 1)
                stage_q(HPG - 1)
                keep_q(HPG - 2, 0)
                keep_q(HPG - 1, 1)

                def return_q(h, par):
                    alone(pool)
                    nc.gpsimd.tensor_copy(QA[0:DK, par, :], QTG[:, bass.ds(h, 1), :].rearrange("p o n -> p (o n)")
                                          ).then_inc(t_back, 1)

                pool.wait_ge(w_qk, g * 64 + 64)
                pool.wait_ge(t_kept, g * 8 + 9)
                return_q(0, 0)
                return_q(1, 1)
                with pool.Fori(1, HPG // 2) as t:
                    for k in range(2):
                        pool.wait_ge(s_qk, g * 64 + (t * 2 + (k - 1)) * 8)
                        return_q(t * 2 + k, k)
            pool.wait_ge(s_o, NH + 1)
            pool.wait_ge(s_qk, 8 * NH)
            pool.wait_ge(s_pv, 8 * NH + 1)
            with pool.Fori(0, (N_PIECES - P_OUT1) // 4) as t:
                for j in range(4):
                    split(t, P_OUT1, j)

        @block.tensor
        def _(pe):
            mm = nc.tensor.matmul
            for ahead in (a_tr, a_pv, dn_ready, t_tr, w_tp, w_pv, e_pv, s_tp, s_pv, e_tp, i_tp):
                pe.sem_inc(ahead, 1)

            owed = [0]

            def piece_read():
                assert not owed[0]
                owed[0] = 1

            def piece_read_now(last, value):
                pe.wait_ge(last, value)
                pe.sem_inc(used, 1)

            def weigh(i, n, kb, last, p, v, down=False):
                k = 1 if i == (0 if down else NT - 1) else 2
                lo = (i + 1 - k if down else i) * n
                return mm(ps[:, 6, lo:lo + k * n].rearrange("p (k d) -> p k d", k=k), p,
                          v.to_broadcast([P, k, n]), start=kb == 0, stop=last)

            def mm3(o, a_hi, a_lo, b_hi, b_lo, first, last):
                m = mm(o, a_hi, b_hi, start=first, stop=False)
                if owed[0]:
                    m.then_inc(used, 1)
                    owed[0] = 0
                mm(o, a_hi, b_lo, start=False, stop=False)
                return mm(o, a_lo, b_hi, start=False, stop=last)

            def norm(k):
                pe.wait_ge(n_acc, 7 * (k + 1))
                if k == 0:
                    pe.wait_ge(ones_ok, 1)
                    pe.wait_ge(cb_ok, 2)
                for t in range(NT):
                    m = mm(ps[:, 5, t:t + 1], nacc[:, t * P:(t + 1) * P], ones[:, 0:1], start=True, stop=True)
                m.then_inc(n_ssq, 1)
                pe.wait_ge(n_dg, NT * (k + 1))
                for t in range(NT):
                    m = mm(ps[:, 6 + t // 4, t % 4 * P:t % 4 * P + P], ones[:], ndiag[:, t, :], start=True, stop=True)
                m.then_inc(n_bc, 1)

            def first_units(k, units, then):
                for kc in range(KC):
                    pe.wait_ge(n_lo, KC * k + kc + 1)
                    for unit in units:
                        o, a_hi, a_lo, b_hi, b_lo = unit(kc)
                        m = mm3(o, a_hi, a_lo, b_hi, b_lo, kc == 0, kc == KC - 1)
                        if kc == KC - 1:
                            m.then_inc(then, 1)

            def project_cols(k, p, c, b, m=P):
                for half in range(2):
                    yield half, b(half), [
                        (W_hi[:, word(p), kc * COLS + c * P:kc * COLS + c * P + m],
                         W_lo[:, word(p), kc * COLS + c * P:kc * COLS + c * P + m],
                         U_hi[:, kc, half * HALF:(half + 1) * HALF],
                         U_lo[:, kc, half * HALF:(half + 1) * HALF]) for kc in range(KC)]

            pe.wait_ge(oh_in, 32)
            n_tab = ES_N + EW_N
            for j in range(4):
                c1 = min(n_tab, (j + 1) * HALF)
                mm(ps[0:NH, j, 0:c1 - j * HALF], rel[:], oh[:, j * HALF:c1], start=True, stop=True).then_inc(b_ready, 1)
            for r in range(63):
                m = mm(ps[:, 4 + r // 32, (r % 32) * NH:(r % 32 + 1) * NH],
                       oh[:, n_tab + 16 * r:n_tab + 16 * r + P], rel[:], start=True, stop=True)
                if r in (31, 62):
                    m.then_inc(b_ready, 1)

            norm(0)
            pe.wait_ge(ready, P_IN0 + 1)
            pe.wait_ge(b_evac, 4)

            def z0_unit(n):
                cols = slice(n % 2 * HALF, (n % 2 + 1) * HALF)

                def operands(kc):
                    w = slice(kc * COLS + n // 2 * P, kc * COLS + (n // 2 + 1) * P)
                    return (ps[:, n, :], W_hi[:, word(P_IN0), w], W_lo[:, word(P_IN0), w],
                            U_hi[:, kc, cols], U_lo[:, kc, cols])
                return operands

            first_units(0, [z0_unit(n) for n in range(4)], z_ready)
            piece_read()
            for c in range(2, 14):
                p = P_IN0 + c // 2
                if c % 2 == 0:
                    pe.wait_ge(ready, p + 1)
                m_ = P if c < 13 else ROPE
                for half, b, ks in project_cols(0, p, c % 2, lambda h: (2 * c + h) % 8, m_):
                    if 2 * c + half >= 8:
                        pe.wait_ge(z_evac, 2 * c + half - 7)
                    for kc, (wh, wl, uh, ul) in enumerate(ks):
                        m = mm3(ps[0:m_, b, :], wh, wl, uh, ul, kc == 0, kc == KC - 1)
                    m.then_inc(z_ready, 1)
                if c % 2 == 1 and c < 13:
                    piece_read()
            piece_read_now(z_ready, 28)

            pe.wait_ge(gw_in, 16)
            pe.wait_ge(z_evac, 28)
            for c in range(LC):
                pe.wait_ge(l_conv, c + 1)
                if c >= 2:
                    pe.wait_ge(l_sig, 2 * (c - 1))
                for g in range(2):
                    for half in range(2):
                        m = mm(ps[:, 4 * (c % 2) + 2 * g + half, :], gw[:, g, c, :],
                               xc[:, c, half * HALF:(half + 1) * HALF], start=True, stop=True)
                    m.then_inc(l_gate, 1)

            pe.wait_ge(m_acc, 3)
            pe.wait_ge(l_sig, 2 * LC)
            for j in range(2):
                for t in range(NT):
                    m = mm(ps[:, 0, 8 * j + t:8 * j + t + 1], lacc[:, j, t * P:(t + 1) * P], ones[:, 0:1],
                           start=True, stop=True)
            m.then_inc(m_ssq, 1)
            for t in range(NT):
                m = nc.tensor.transpose(ps[:, 1, t * ROPE:(t + 1) * ROPE], krope[:, t * P:(t + 1) * P],
                                        ident[0:ROPE, 0:ROPE])
            m.then_inc(m_rope, 1)
            pe.wait_ge(ready, P_UKV + 1)
            pe.wait_ge(m_lo, KVC)
            pe.wait_ge(m_krope, 1)
            pe.wait_ge(m_ms, 1)
            for t in range(NT):
                for j in range(2):
                    n = 2 * t + j
                    if n >= 8:
                        pe.wait_ge(m_upev, n - 7)
                    for kc in range(KVC):
                        cols = slice(kc * 1024 + j * HALF, kc * 1024 + (j + 1) * HALF)
                        m = mm3(bank(n % 8), kvl_hi[:, kc, t * P:(t + 1) * P], kvl_lo[:, kc, t * P:(t + 1) * P],
                                W_hi[:, word(P_UKV), cols], W_lo[:, word(P_UKV), cols], kc == 0, kc == KVC - 1)
                    m.then_inc(m_up, 1)
            piece_read_now(m_up, 2 * NT)
            pe.wait_ge(m_lo, KVC + QRC)
            for j in range(2):
                pe.wait_ge(ready, P_UQ + j + 1)
                for t in range(NT):
                    n = 2 * NT + NT * j + t
                    pe.wait_ge(m_upev, n - 7)
                    for kc in range(QRC):
                        cols = slice(kc * 384, (kc + 1) * 384)
                        m = mm3(ps[:, n % 8, 0:384], ql_hi[:, kc, t * P:(t + 1) * P], ql_lo[:, kc, t * P:(t + 1) * P],
                                W_hi[:, word(P_UQ + j), cols], W_lo[:, word(P_UQ + j), cols],
                                kc == 0, kc == QRC - 1)
                    m.then_inc(m_up, 1)
                piece_read_now(m_up, 2 * NT + NT * (j + 1))

            pe.wait_ge(m_upev, 4 * NT)
            pe.wait_ge(zeroed, 2)
            with pe.Fori(0, MH // 2) as it:
                for hh_ in range(2):
                    for j in range(2):
                        pe.wait_ge(a_st, it * 4 + 2 * hh_ + j + 1)
                        if hh_:
                            pe.wait_ge(a_trev, it * 4 + j + 2)
                        else:
                            pe.wait_ge(a_exp, it * 16 + 1)
                        src = stk if j else stq
                        for t in range(NT):
                            m = nc.tensor.transpose(ps[0:MQK, 2 * j + t // 4, t % 4 * P:t % 4 * P + P], src[:, t, :], ident)
                        m.then_inc(a_tr, 1)

                def scores(u):
                    h_, i = u // 8, u % 8
                    if u >= 2:
                        pe.wait_ge(a_exp, it * 16 + u)
                    else:
                        pe.wait_ge(a_trev, it * 4 + 5)
                    n = (i + 1) * P
                    for c in range(0, n, HALF):
                        w = min(HALF, n - c)
                        m = mm(ps[:, 2 * (u % 2) + c // HALF, 0:w], QT[:, h_, i * P:(i + 1) * P],
                               KT[:, h_, c:c + w], start=True, stop=True)
                    m.then_inc(a_qk, 1)

                scores(0)
                scores(1)
                for u in range(16):
                    h_, i = u // 8, u % 8
                    pe.wait_ge(a_exp, it * 16 + u + 2)
                    pe.wait_ge(a_tpev, it * 16 + u + 1)
                    for kb in range(i + 1):
                        m = nc.tensor.transpose(ps[:, 4 + kb // 4, kb % 4 * P:kb % 4 * P + P],
                                                prob[:, u % 2, kb * P:(kb + 1) * P], ident)
                    m.then_inc(a_tp, 1)
                    if u + 2 < 16:
                        scores(u + 2)
                    pe.wait_ge(a_tpev, it * 16 + u + 2)
                    if i == 0:
                        pe.wait_ge(a_out, it * 2 + h_ + 1)
                    for kb in range(i + 1):
                        m = weigh(i, MV, kb, kb == i, probT[:, u % 2, kb * P:(kb + 1) * P],
                                  V[:, kb, bass.ds((it * 2 + h_) * MV, MV)].unsqueeze(1))
                    m.then_inc(a_pv, 1)

            pe.wait_ge(a_out, MH + 1)
            for c in range(4):
                for half in range(2):
                    n = 2 * c + half
                    if n >= 4:
                        pe.wait_ge(x_lo, 4 + n - 3)
                    for t in range(4):
                        m = nc.tensor.transpose(ps[:, n % 4, t * P:(t + 1) * P],
                                                turned_pair(4 * half + t, c), ident)
                    m.then_inc(x_tr, 1)

            def out_proj(p0, k):
                for c in range(KC):
                    p = p0 + c // 2
                    if c % 2 == 0:
                        pe.wait_ge(ready, p + 1)
                    for half, b, ks in project_cols(0, p, c % 2, lambda h: (2 * c + h) % 4 + 4):
                        n = 16 * k + 2 * c + half
                        if n >= 4:
                            pe.wait_ge(o_added, n - 3)
                        for kc, (wh, wl, uh, ul) in enumerate(ks):
                            m = mm3(ps[:, b, :], wh, wl, uh, ul, kc == 0, kc == KC - 1)
                        m.then_inc(o_ready, 1)
                    if c % 2 == 1 and c < KC - 1:
                        piece_read()
                piece_read_now(o_ready, 16 * (k + 1))

            pe.wait_ge(x_lo, 12)
            out_proj(P_OUT0, 0)
            norm(1)
            mlp_pe(pe, first_units, mm3, piece_read, piece_read_now, P_MLP0, 0)

            norm(2)
            pe.wait_ge(ready, P_IN1 + 1)

            def z1_unit(t):
                def operands(kc):
                    w = slice(kc * COLS, (kc + 1) * COLS)
                    return (ps[:, t, 0:COLS], U_hi[:, kc, t * P:(t + 1) * P], U_lo[:, kc, t * P:(t + 1) * P],
                            W_hi[:, word(P_IN1), w], W_lo[:, word(P_IN1), w])
                return operands

            first_units(2, [z1_unit(t) for t in range(4)], z_ready)
            n = 4
            for p in range(P_IN1, P_OUT1):
                pe.wait_ge(ready, p + 1)
                if p == P_KC1:
                    for c in range(2):
                        for half, b, ks in project_cols(0, p, c, lambda h: (n + h) % 8):
                            pe.wait_ge(z_evac, n + half - 7 + Z0)
                            for kc, (wh, wl, uh, ul) in enumerate(ks):
                                m = mm3(ps[:, b, :], wh, wl, uh, ul, kc == 0, kc == KC - 1)
                            m.then_inc(z_ready, 1)
                        n += 2
                else:
                    w = GATES if p == P_GATE1 else COLS
                    for t in range(4 if p == P_IN1 else 0, NT):
                        if n >= 8:
                            pe.wait_ge(z_evac, n - 7 + Z0)
                        for kc in range(KC):
                            m = mm3(ps[:, n % 8, 0:w], U_hi[:, kc, t * P:(t + 1) * P], U_lo[:, kc, t * P:(t + 1) * P],
                                    W_hi[:, word(p), kc * COLS:kc * COLS + w], W_lo[:, word(p), kc * COLS:kc * COLS + w],
                                    kc == 0, kc == KC - 1)
                        m.then_inc(z_ready, 1)
                        n += 1
                if p < P_OUT1 - 1:
                    piece_read()
            assert n == Z1_UNITS
            piece_read_now(z_ready, Z0 + n)

            pe.wait_ge(w_in, 80)
            pe.wait_ge(z_evac, Z1_UNITS + Z0)
            for u in range(4):
                pe.wait_ge(c_tp, u + 1)
                for c in range(16):
                    m = mm(ps[0:NCMP, u, 0:CMP_HID], TP[:, u % 2, c, :], W1C[2 * (u // 2) + c // 8][:, c % 8, :], start=c == 0, stop=c == 15)
                m.then_inc(c_mm, 1)
            for u in range(4):
                pe.wait_ge(c_gelu, u + 1)
                for k in range(2):
                    j = 2 * u + k
                    m = nc.tensor.transpose(ps[:, 4, j * NCMP:(j + 1) * NCMP], HC[:, u, k * P:(k + 1) * P],
                                            ident[0:NCMP, 0:NCMP])
            m.then_inc(c_hT, 1)
            pe.wait_ge(c_hTev, 1)
            for u in range(4):
                for k in range(2):
                    m = mm(ps[0:NCMP, 5, u * DK:(u + 1) * DK], HCT[:, u, k, :], W2C[:, u // 2, k, :],
                           start=k == 0, stop=k == 1)
            m.then_inc(c_out, 1)
            pe.wait_ge(const_in, 48)
            mm(ps[:, 7, 0:NT * GATES], reverse, GATE[:].rearrange("p t n -> p (t n)"), start=True, stop=True
               ).then_inc(c_gate, 1)
            for n in range(8):
                j, g, half = n // 4, n // 2 % 2, n % 2
                pe.wait_ge(k_sc, j + 1)
                if n >= 4:
                    pe.wait_ge(k_trev, n - 3)
                for t in range(4):
                    m = nc.tensor.transpose(ps[0:DK, n % 4, t * P:(t + 1) * P], KV[:, 4 * half + t, 2 * j, g, :], ident)
                m.then_inc(k_tr, 1)
            pe.wait_ge(c_sm, 6)
            for g in range(NG):
                m = nc.tensor.transpose(ps[0:DK, 6, g * NCMP:(g + 1) * NCMP], CKN[:, g, :], ident[0:NCMP, 0:NCMP])
            m.then_inc(c_ckT, 1)

            pe.wait_ge(c_ck, 1)
            pe.wait_ge(k_trev, 8)
            pe.wait_ge(ki_in, 16)
            pe.wait_ge(c_sm, 8)
            pe.wait_ge(zeroed, 6)
            with pe.Fori(0, NG) as g:
                pe.wait_ge(s_o, g * 8 + 1)

                def turn_q(h, half):
                    if half == 0:
                        pe.wait_ge(t_st, g * 8 + h + 1)
                        pe.wait_ge(e_o, g * 8 + h + 1)
                    pe.wait_ge(t_ev, g * 16 + h * 2 + half + 1)
                    for t in range(4):
                        m = mm(ps[0:DK, 7, t * P:(t + 1) * P], STQ[:, 4 * half + t, :], reverse, start=True, stop=True)
                    m.then_inc(t_tr, 1)

                def turn_p(i, src, nb, exp, tp, tpev, value):
                    pe.wait_ge(exp, value + 2)
                    pe.wait_ge(tpev, value + 1)
                    for kb in range(nb):
                        m = nc.tensor.transpose(ps[:, 4 + kb // 4, kb % 4 * P:kb % 4 * P + P],
                                                src[:, i % 2, kb * P:(kb + 1) * P], ident)
                    m.then_inc(tp, 1)

                def head_scores(h, par, last):
                    def window(i):
                        u = g * 64 + h * 8 + i
                        pe.wait_ge(w_max, (u if i == 0 else u - 1) + 1)
                        alone(pe)
                        k0, nk = max(i - WB, 0) * P, (min(i, WB) + 1) * P
                        for c in range(0, nk, HALF):
                            w = min(HALF, nk - c)
                            m = mm(ps[:, 2 * (i % 2) + c // HALF, 0:w], QA[:, par, i * P:(i + 1) * P],
                                   KWT[:, bass.ds(g, 1), k0 + c:k0 + c + w].rearrange("p o n -> p (o n)"),
                                   start=True, stop=True)
                        m.then_inc(w_qk, 1)

                    pe.wait_ge(t_ev, g * 16 + h * 2 + 2)
                    window(0)
                    window(1)
                    pe.wait_ge(t_ev, g * 16 + h * 2 + 3)
                    alone(pe)
                    for i in range(NT):
                        j = NT - 1 - i
                        m = mm(ps[:, 7, j * NCMP:(j + 1) * NCMP], QA[:, par, i * P:(i + 1) * P],
                               CKT[:, bass.ds(g, 1), :].rearrange("p o n -> p (o n)"), start=True, stop=True)
                    m.then_inc(e_qk, 1)
                    for i in range(NT):
                        nb, k0 = min(i, WB) + 1, max(i - WB, 0)
                        if i == 5:
                            pe.wait_ge(e_tpev, g * 8 + h + 1)
                        turn_p(i, PW, nb, w_exp, w_tp, w_tpev, g * 64 + h * 8 + i)
                        if i + 2 < NT:
                            window(i + 2)
                        elif not last:
                            turn_q(h + 1, i - 6)
                        pe.wait_ge(w_tpev, g * 64 + h * 8 + i + 2)
                        if i == 4:
                            pe.wait_ge(e_p, g * 8 + h + 1)
                            alone(pe)
                            for t in range(NT):
                                m = nc.tensor.transpose(ps[0:NCMP, 4 + t // 4, t % 4 * P:t % 4 * P + P], PC[:, NT - 1 - t, :], ident)
                            m.then_inc(e_tp, 1)
                        if i == 0:
                            pe.wait_ge(w_o, g * 8 + h + 1)
                        for kb in range(nb):
                            m = weigh(i, DK, kb, kb == nb - 1, PTW[:, i % 2, kb * P:(kb + 1) * P],
                                      KV[:, k0 + kb, 3, bass.ds(g, 1), :])
                        m.then_inc(w_pv, 1)
                        if i == 5:
                            alone(pe)
                            for t in range(NT):
                                m = mm(ps[:, 7, t * DK:(t + 1) * DK], PTC[:, t * P:(t + 1) * P],
                                       CV[:, bass.ds(g, 1), :].rearrange("p o n -> p (o n)"), start=True, stop=True)
                            m.then_inc(e_pv, 1)

                turn_q(0, 0)
                turn_q(0, 1)
                with pe.Fori(0, HPG // 2 - 1) as t:
                    head_scores(t * 2, 0, False)
                    head_scores(t * 2 + 1, 1, False)
                head_scores(HPG - 2, 0, False)
                head_scores(HPG - 1, 1, True)

                pe.wait_ge(e_acc, g * 9 + 9)
                pe.wait_ge(w_tpev, g * 64 + 65)
                alone(pe)
                for t in range(NT):
                    m = nc.tensor.transpose(ps[0:NCMP, 4 + t // 4, t % 4 * P:t % 4 * P + P], PACC[:, NT - 1 - t, :], ident)
                m.then_inc(i_tp, 1)
                pe.wait_ge(i_tpev, g + 1)
                pe.wait_ge(e_o, g * 8 + 9)
                for t in range(NT):
                    m = mm(ps[:, 7, t * NSEL:(t + 1) * NSEL], PTC[:, t * P:(t + 1) * P], cs[0:NCMP, C_OV:C_OV + NSEL],
                           start=True, stop=True)
                m.then_inc(i_mm, 1)
                pe.wait_ge(i_mask, g + 1)
                for t in range(NT):
                    m = nc.tensor.transpose(ps[0:NSEL, 4 + t // 4, t % 4 * P:t % 4 * P + P], REP[:, t, :], ident)
                m.then_inc(i_mtr, 1)

                pe.wait_ge(mk_in, g * 32 + 32)

                def selected(h, par, k, first=False):
                    i = NT - 1 - k
                    if k == 0:
                        pe.wait_ge(t_back, g * 8 + h + 1)
                    pe.wait_ge(s_max, (g * 64 if first else g * 64 + h * 8 + k - 1) + 1)
                    alone(pe)
                    nk = (i + 1) * P
                    for c in range(0, nk, HALF):
                        w = min(HALF, nk - c)
                        m = mm(ps[:, 2 * (i % 2) + c // HALF, 0:w], QA[:, par, i * P:(i + 1) * P],
                               KST[:, bass.ds(g, 1), c:c + w].rearrange("p o n -> p (o n)"), start=True, stop=True)
                    m.then_inc(s_qk, 1)

                def head_selected(h, par, first=False, last=False):
                    for k in range(NT):
                        i = NT - 1 - k
                        turn_p(i, P1, i + 1, s_exp, s_tp, s_tpev, g * 64 + h * 8 + k)
                        if k + 2 < NT:
                            selected(h, par, k + 2)
                        elif not last:
                            selected(h + 1, 1 - par, k + 2 - NT)
                        pe.wait_ge(s_tpev, g * 64 + h * 8 + k + 2)
                        if k == 0 and first:
                            pe.wait_ge(w_o, g * 8 + 9)
                        elif k == 0:
                            pe.wait_ge(s_o, g * 8 + h + 1)
                        for kb in range(i + 1):
                            m = weigh(i, DK, kb, kb == i, PT1[:, i % 2, kb * P:(kb + 1) * P],
                                      KV[:, kb, 1, bass.ds(g, 1), :], down=True)
                        m.then_inc(s_pv, 1)

                selected(0, 0, 0, True)
                selected(0, 0, 1, True)
                pe.wait_ge(i_mtrev, g + 1)
                head_selected(0, 0, first=True)
                with pe.Fori(0, HPG // 2 - 1) as t:
                    head_selected(t * 2 + 1, 1)
                    head_selected(t * 2 + 2, 0)
                head_selected(HPG - 1, 1, last=True)

            pe.wait_ge(s_o, NH + 1)
            for n in range(2 * KC):
                if n >= 4:
                    pe.wait_ge(x_lo, n - 3 + XL0)
                for t in range(4):
                    m = mm(ps[:, n % 4, t * P:(t + 1) * P],
                           ZQ[:, 4 * (n % 2) + t, n // 2 * P:(n // 2 + 1) * P], reverse, start=True, stop=True)
                m.then_inc(x_tr, 1)
            pe.wait_ge(x_lo, 2 * KC + XL0)
            out_proj(P_OUT1, 1)
            norm(3)
            mlp_pe(pe, first_units, mm3, piece_read, piece_read_now, P_MLP1, 1)

        @block.scalar
        def _(act):
            A = nc.scalar.activation
            for ahead in (a_trev, a_exp, a_tpev, t_ev, w_tpev, w_exp, s_tpev, s_exp):
                act.sem_inc(ahead, 1)
            act.sem_inc(up_free, 4)
            act.dma_start(cs[:], cst[:, :]).then_inc(const_in, 16)
            act.dma_start(pr[:], prm[:, :]).then_inc(const_in, 16)
            act.dma_start(oh[:], onehot[:, :]).then_inc(oh_in, 16)
            act.dma_start(rel[:], relx[:, :]).then_inc(oh_in, 16)
            act.dma_start(H[:], xT[:, :, :]).then_inc(x_in, 16)

            def norm(k):
                for c in range(KC):
                    if k == 0 and c == 0:
                        act.wait_ge(x_in, 16)
                    if k == 2:
                        act.wait_ge(dn_free, 4 + 8 * (MLP_UNITS - 1) + c + 1)
                    elif k:
                        act.wait_ge(o_added, 16 * (k // 2) + 2 * c + 2)
                    if c >= 2:
                        act.wait_ge(n_acc, 7 * k + c - 1)
                    A(nsq[:, c % 2, :], H[:, c, :], ACT.Square).then_inc(n_sq, 1)
                if k == 0:
                    act.wait_ge(cb_ok, 2)
                    for g in range(NG):
                        act.dma_start(cb_d[g], cbs[:, HPG * g:HPG * (g + 1), :]).then_inc(b_out, 16)
                if k == 2:
                    act.wait_ge(dn_free, 4 + 8 * MLP_UNITS)
                    act.dma_start(h_d[:, :, :], H[:]).then_inc(h_spill, 16)
                act.wait_ge(n_ms, k + 1)
                A(msq[:, 8:16], msq[:, 0:8], ACT.Sqrt).then_inc(n_sd, 1)
                if k == 0:
                    act.wait_ge(b_out, 64)
                for c in range(KC):
                    act.wait_ge(n_uf, KC * k + c + 1)
                    A(U_hi[:, c, :], nuf[:, c % 2, :], ACT.Copy).then_inc(n_hi, 1)

            for j in range(4):
                act.wait_ge(b_ready, j + 1)
                c1 = min(ES_N + EW_N, (j + 1) * HALF)
                A(esb[:, j * HALF:c1], ps[0:NH, j, 0:c1 - j * HALF], ACT.Copy).then_inc(b_evac, 1)
            act.wait_ge(b_evac, 4)
            act.dma_start(es_d[:, :], esb[:, 0:ES_N]).then_inc(b_out, 16)
            act.dma_start(ew_d[:, :], esb[:, ES_N:ES_N + EW_N]).then_inc(b_out, 16)
            norm(0)

            act.wait_ge(sp_dve, 1)
            A(sm[:, 4:8], sm[:, 0:4], ACT.Exp, scale=-1.0).then_inc(sp_act, 1)
            for c in range(14):
                for half in range(2):
                    n = 2 * c + half
                    act.wait_ge(z_ready, n + 1)
                    cols = slice(half * HALF, (half + 1) * HALF)
                    src = ps[:, n % 8, :]
                    if c < 4:
                        A(lr[:, c, cols], src, ACT.Copy).then_inc(z_evac, 1)
                    elif c < 8:
                        A(xg[:, c - 4, cols], src, ACT.Gelu_apprx_tanh).then_inc(z_evac, 1)
                    elif c < 11:
                        A(qlat[:, c - 8, cols], src, ACT.Copy).then_inc(z_evac, 1)
                    elif c < 13:
                        A(kvlat[:, c - 11, cols], src, ACT.Copy).then_inc(z_evac, 1)
                    else:
                        A(krope[:, cols], ps[0:ROPE, n % 8, :], ACT.Copy).then_inc(z_evac, 1)
            act.wait_ge(z_evac, 28)
            act.dma_start(gw[:], gatew[:, :, :, :]).then_inc(gw_in, 16)
            for c in range(LC):
                for g, dst in ((0, lra), (1, lri)):
                    act.wait_ge(l_gate, 2 * c + g + 1)
                    o = G_BA if g == 0 else G_BX
                    A(dst[:, c, :], bank(4 * (c % 2) + 2 * g, 2), ACT.Sigmoid, bias=pr[:, o + c:o + c + 1]
                      ).then_inc(l_sig, 1)
            act.wait_ge(sp_dve, SP_COUNT)
            for c in range(LC):
                act.wait_ge(l_sig, 2 * c + 1)
                if c >= 2:
                    act.wait_ge(l_t2, c - 1)
                A(lrt[:, c % 2, :], lra[:, c, :], ACT.Tanh, scale=sm[:, 20 + c:21 + c]).then_inc(l_tanh, 1)
                act.wait_ge(l_tanh, c + 1)
                A(lra[:, c, :], lra[:, c, :], ACT.Exp, scale=sm[:, 24 + c:25 + c]).then_inc(l_exp, 1)
            for c in range(LC):
                act.wait_ge(l_t2, c + 1)
                A(xc[:, c, :], xc[:, c, :], ACT.Sqrt).then_inc(l_mult, 1)
            act.wait_ge(l_done, LC)
            for n, src in enumerate([qlat[:, 0], qlat[:, 1], qlat[:, 2], kvlat[:, 0], kvlat[:, 1]]):
                if n == 2:
                    act.wait_ge(m_acc, 1)
                if n == 4:
                    act.wait_ge(m_acc, 2)
                A(lsq[:, n % 2, :], src, ACT.Square).then_inc(m_sq, 1)
            act.wait_ge(m_ms, 1)
            A(rsd[:], msq[:], ACT.Sqrt).then_inc(m_sd, 1)
            for c in range(KVC):
                act.wait_ge(m_g, c + 1)
                A(kvl_hi[:, c, :], kvlat[:, c, :], ACT.Copy).then_inc(m_hi, 1)
            act.wait_ge(m_rs, 1)
            for t in range(NT):
                for j in range(2):
                    act.wait_ge(m_up, 2 * t + j + 1)
                    b = (2 * t + j) % 8
                    if j == 0:
                        A(K[:, t, :, 0:MNOPE], bank(b).rearrange("p (h d) -> p h d", h=MH), ACT.Copy,
                          scale=rsd[:, 8 + t:9 + t]).then_inc(m_upev, 1)
                    else:
                        A(V[:, t, :], bank(b), ACT.Copy, scale=rsd[:, 8 + t:9 + t]).then_inc(m_upev, 1)
            for c in range(QRC):
                act.wait_ge(m_g, KVC + c + 1)
                A(ql_hi[:, c, :], qlat[:, c, :], ACT.Copy).then_inc(m_hi, 1)
            for j in range(2):
                for t in range(NT):
                    n = 2 * NT + NT * j + t
                    act.wait_ge(m_up, n + 1)
                    A(Q[:, t, 4 * j:4 * j + 4, :], ps[:, n % 8, 0:384].rearrange("p (h d) -> p h d", h=4), ACT.Copy,
                      scale=rsd[:, t:t + 1]).then_inc(m_upev, 1)
            act.wait_ge(m_upev, 4 * NT)
            act.wait_ge(m_krope, 1)
            for n in range(2 * NT):
                if n >= NT:
                    act.wait_ge(h_red, n - NT + 1)
                X = Q if n < NT else K
                A(hsq[:, n % NT], X[:, n % NT], ACT.Square).then_inc(h_sq, 1)
            act.wait_ge(h_ms, 1)
            A(rs[:], ss[:], ACT.Sqrt).then_inc(h_sd, 1)

            with act.Fori(0, MH // 2) as it:
                for hh_ in range(2):
                    for j in range(2):
                        act.wait_ge(a_tr, it * 4 + 2 * hh_ + j + 2)
                        A((KT if j else QT)[0:MQK, hh_, :], bank(2 * j, 2)[0:MQK, :], ACT.Copy,
                          scale=pr[0:MQK, G_GQC + j:G_GQC + j + 1]).then_inc(a_trev, 1)

                def turned(u):
                    n = (u % 8 + 1) * P
                    act.wait_ge(a_tp, it * 16 + u + 1)
                    if u >= 2:
                        act.wait_ge(a_pv, it * 16 + (u - 1) + 1)
                    A(probT[:, u % 2, 0:n], bank(4, 2)[:, 0:n], ACT.Copy).then_inc(a_tpev, 1)

                for u in range(16):
                    n = (u % 8 + 1) * P
                    act.wait_ge(a_max, it * 16 + u + 1)
                    if u >= 2:
                        act.wait_ge(a_tp, it * 16 + (u - 1))
                    if u == 0:
                        act.wait_ge(a_ri, it * 2 + 1)
                    A(prob[:, u % 2, 0:n], bank(2 * (u % 2), 2)[:, 0:n], ACT.Exp, bias=nmx[:, u % 8:u % 8 + 1],
                      accum_out=sums[:, u:u + 1]).then_inc(a_exp, 1)
                    if u >= 1:
                        turned(u - 1)
                turned(15)

            act.wait_ge(a_pv, 8 * MH + 1)
            for c in range(4):
                A(U_hi[:, c, :], lr[:, c, :], ACT.Copy).then_inc(x_hi, 1)
            for n in range(8):
                act.wait_ge(x_tr, n + 1)
                A(U_hi[:, 4 + n // 2, (n % 2) * HALF:(n % 2 + 1) * HALF], ps[:, n % 4, :], ACT.Copy).then_inc(x_hi, 1)
            act.wait_ge(x_lo, 12)
            act.wait_ge(x_tr, 8)
            act.dma_start(H[:], xT[:, :, :]).then_inc(h_in, 16)
            norm(1)
            mlp_act(act, 0)
            norm(2)
            act.wait_ge(h_spill, 16)
            n = 0
            for p in range(P_IN1, P_OUT1):
                for t in range(4 if p == P_KC1 else NT):
                    act.wait_ge(z_ready, n + 1 + Z0)
                    src = ps[:, n % 8, 0:COLS]
                    if p < P_KC1:
                        A(ZQ[:, t, (p - P_IN1) * COLS:(p - P_IN1 + 1) * COLS], src, ACT.Copy).then_inc(z_evac, 1)
                    elif p == P_KC1:
                        A(KCV[:, t // 2, t % 2 * HALF:(t % 2 + 1) * HALF], ps[:, n % 8, :], ACT.Copy).then_inc(z_evac, 1)
                    elif p < P_GATE1:
                        j = 2 * (p - P_KV1)
                        A(KV[:, t, j:j + 2].rearrange("p j g d -> p (j g d)"), src, ACT.Copy).then_inc(z_evac, 1)
                    else:
                        A(GATE[:, t, :], ps[:, n % 8, 0:GATES], ACT.Sigmoid).then_inc(z_evac, 1)
                    n += 1
            act.wait_ge(z_evac, Z1_UNITS + Z0)
            for t in range(NT):
                if t >= 2:
                    act.wait_ge(h_red, t - 1 + HD0)
                A(SQ1[:, t % 2, :], ZQ[:, t, :], ACT.Square).then_inc(h_sq, 1)
            for j in range(2):
                act.wait_ge(h_red, NT + j - 1 + HD0)
                A(SQ1[:, j, :].rearrange("p (t n) -> p t n", t=NT), KV[:, :, 2 * j].rearrange("p t g d -> p t (g d)"),
                  ACT.Square).then_inc(h_sq, 1)
            act.wait_ge(h_ms, 2 + 1)
            A(rs[:], ss[:], ACT.Sqrt).then_inc(h_sd, 1)
            A(rsk[:], ssk[:], ACT.Sqrt).then_inc(h_sd, 1)
            for u in range(4):
                act.wait_ge(c_mm, u + 1)
                A(HC[:, u, :], ps[0:NCMP, u, 0:CMP_HID], ACT.Gelu_apprx_tanh).then_inc(c_gelu, 1)
            act.wait_ge(c_sm, 4)
            A(cmx[0:NCMP, 4:6], cmx[0:NCMP, 2:4], ACT.Sqrt).then_inc(c_sd, 1)
            act.wait_ge(c_tp, 4)
            for n in range(8):
                j, g, half = n // 4, n // 2 % 2, n % 2
                act.wait_ge(k_tr, n + 1)
                dst = KST if j == 0 else KWT
                A(dst[0:DK, g, half * HALF:(half + 1) * HALF], ps[0:DK, n % 4, :], ACT.Copy,
                  scale=pr[0:DK, G_K1 + 1 + j:G_K1 + 2 + j]).then_inc(k_trev, 1)
            act.wait_ge(c_ckT, 1)
            A(CKT[0:DK], ps[0:DK, 6, 0:NG * NCMP].rearrange("p (g n) -> p g n", g=NG), ACT.Copy,
              scale=pr[0:DK, G_K1:G_K1 + 1]).then_inc(c_ck, 1)

            with act.Fori(0, NG) as g:
                def turn_q(h, par, half):
                    act.wait_ge(t_tr, g * 16 + h * 2 + half + 2)
                    act.wait_ge(t_kept, (g * 8 + (h if isinstance(h, int) and h < 1 else h - 1)) + 1)
                    A(QA[0:DK, par, half * HALF:(half + 1) * HALF], ps[0:DK, 7, :], ACT.Copy, scale=q_gain8
                      ).then_inc(t_ev, 1)

                turn_q(0, 0, 0)
                turn_q(0, 0, 1)

                def head_scores(h, par, last):
                    def expo(i):
                        u = g * 64 + h * 8 + i
                        nk = (min(i, WB) + 1) * P
                        act.wait_ge(w_max, u + 2)
                        if i == 0:
                            act.wait_ge(w_ri, g * 8 + h + 1)
                        else:
                            act.wait_ge(w_tp, u)
                        A(PW[:, i % 2, 0:nk], SW[:, i % 2, 0:nk], ACT.Exp, bias=nmx[:, i:i + 1], scale=-1.0,
                          accum_out=sums[:, 8 * par + i:8 * par + i + 1]).then_inc(w_exp, 1)

                    expo(0)
                    for i in range(NT):
                        if i + 1 < NT:
                            expo(i + 1)
                        nk = (min(i, WB) + 1) * P
                        act.wait_ge(w_tp, g * 64 + h * 8 + i + 2)
                        act.wait_ge(w_pv, g * 64 + h * 8 + i + 1)
                        A(PTW[:, i % 2, 0:nk], bank(4, 2)[:, 0:nk], ACT.Copy).then_inc(w_tpev, 1)
                        if i == 1:
                            act.wait_ge(e_dve, g * 24 + h * 3 + 3)
                            A(PC[:], PC[:], ACT.Exp).then_inc(e_exp, 1)
                        if i == 4:
                            act.wait_ge(e_tp, g * 8 + h + 2)
                            act.wait_ge(e_pv, g * 8 + h + 1)
                            A(PTC[:], bank(4, 2)[0:NCMP, :], ACT.Copy).then_inc(e_tpev, 1)
                        if i >= 6 and not last:
                            turn_q(h + 1, 1 - par, i - 6)

                with act.Fori(0, HPG // 2 - 1) as t:
                    head_scores(t * 2, 0, False)
                    head_scores(t * 2 + 1, 1, False)
                head_scores(HPG - 2, 0, False)
                head_scores(HPG - 1, 1, True)
                act.wait_ge(i_tp, g + 2)
                act.wait_ge(e_pv, g * 8 + 9)
                A(PTC[:], bank(4, 2)[0:NCMP, :], ACT.Copy).then_inc(i_tpev, 1)
                act.wait_ge(i_mtr, g + 1)
                A(MT16[:], bank(4, 2)[0:NSEL, :], ACT.Copy).then_inc(i_mtrev, 1)

                def expo_s(h, par, k, first=False):
                    i = NT - 1 - k
                    nk = (i + 1) * P
                    act.wait_ge(s_max, g * 64 + h * 8 + k + 2)
                    if first:
                        act.wait_ge(w_ri, g * 8 + 10)
                    else:
                        act.wait_ge(s_tp, g * 64 + h * 8 + k)
                        if k == 0:
                            act.wait_ge(s_ri, g * 8 + h + 1)
                    A(P1[:, i % 2, 0:nk], SS1[:, i % 2, 0:nk], ACT.Exp, bias=nmx[:, i:i + 1], scale=-1.0,
                      accum_out=sums[:, 8 * par + i:8 * par + i + 1]).then_inc(s_exp, 1)

                def head_selected(h, par, last):
                    for k in range(NT):
                        i = NT - 1 - k
                        if k + 1 < NT:
                            expo_s(h, par, k + 1)
                        elif not last:
                            expo_s(h + 1, 1 - par, 0)
                        nk = (i + 1) * P
                        act.wait_ge(s_tp, g * 64 + h * 8 + k + 2)
                        act.wait_ge(s_pv, g * 64 + h * 8 + k + 1)
                        A(PT1[:, i % 2, 0:nk], bank(4, 2)[:, 0:nk], ACT.Copy).then_inc(s_tpev, 1)

                act.wait_ge(mk_in, g * 32 + 32)
                expo_s(0, 0, 0, True)
                with act.Fori(0, HPG // 2 - 1) as t:
                    head_selected(t * 2, 0, False)
                    head_selected(t * 2 + 1, 1, False)
                head_selected(HPG - 2, 0, False)
                head_selected(HPG - 1, 1, True)

            act.wait_ge(s_pv, 129)
            for n in range(2 * KC):
                act.wait_ge(x_tr, n + 1 + X0)
                A(U_hi[:, n // 2, (n % 2) * HALF:(n % 2 + 1) * HALF], ps[:, n % 4, :], ACT.Copy).then_inc(x_hi, 1)
            act.dma_start(H[:], h_d[:, :, :]).then_inc(h_in, 16)
            norm(3)
            mlp_act(act, 1)
            for half in range(2):
                for dc in range(KC):
                    act.wait_ge(dn_free, 4 + 8 * (2 * MLP_UNITS - 2 + half) + dc + 1)
                    cols = slice(half * HALF, (half + 1) * HALF)
                    act.dma_start(out[:, dc, cols], H[:, dc, cols]).then_inc(out_done, 16)
            act.wait_ge(out_done, 16 * 2 * KC)


        @block.vector
        def _(dve):
            V_ = nc.vector
            for ahead in (a_out, a_ri, s_o, e_o, w_max, w_o, s_max, w_ri, w_ri, s_ri, s_ri):
                dve.sem_inc(ahead, 1)

            dve.sem_inc(sq_free, 2)
            dve.sem_inc(dn_free, 4)

            def add_squares(k, c):
                if c < 1:
                    return
                dve.wait_ge(n_sq, KC * k + c + 1)
                if c == 1:
                    V_.tensor_tensor(nacc[:], nsq[:, 0, :], nsq[:, 1, :], ALU.add).then_inc(n_acc, 1)
                else:
                    dve.wait_ge(n_acc, 7 * k + c - 1)
                    V_.tensor_tensor(nacc[:], nacc[:], nsq[:, c % 2, :], ALU.add).then_inc(n_acc, 1)

            def norm(k, g0):
                if k:
                    add_squares(k, KC - 1)
                dve.wait_ge(n_ssq, k + 1)
                V_.tensor_scalar(msq[:, 0:8], ps[:, 5, 0:8], 1.0 / D, EPS, ALU.mult, ALU.add).then_inc(n_ms, 1)
                dve.wait_ge(n_sd, k + 1)
                V_.reciprocal(rsd[:, 0:8], msq[:, 8:16]).then_inc(n_rs, 1)
                dve.wait_ge(n_rs, k + 1)
                for t in range(NT):
                    V_.tensor_scalar(ndiag[:, t, :], ident, rsd[:, t:t + 1], None, ALU.mult).then_inc(n_dg, 1)
                dve.wait_ge(n_bc, k + 1)

                def low(c):
                    dve.wait_ge(n_hi, KC * k + c + 1)
                    V_.tensor_tensor(U_lo[:, c, :], nuf[:, c % 2, :], U_hi[:, c, :].bitcast(F32), ALU.subtract
                                     ).then_inc(n_lo, 1)

                for c in range(KC):
                    if c >= 2:
                        dve.wait_ge(n_lo, KC * k + c - 1)
                    V_.scalar_tensor_tensor(nuf[:, c % 2, :], H[:, c, :], pr[:, g0 + c:g0 + c + 1], bank(6, 2),
                                            ALU.mult, ALU.mult).then_inc(n_uf, 1)
                    if c >= 1:
                        low(c - 1)
                low(KC - 1)

            V_.memset(cbs[:, :, 63:CB_N], NEG).then_inc(cb_ok, 1)
            for c in range(1, KC):
                add_squares(0, c)
            dve.wait_ge(b_ready, 6)
            cb_v = cbs[:, :, 0:63].rearrange("p h r -> p r h")
            V_.tensor_copy(cb_v, bank(4, 2)[:, 0:63 * NH].rearrange("p (r h) -> p r h", h=NH)).then_inc(cb_ok, 1)
            dve.wait_ge(const_in, 32)
            norm(0, G_MIX0)

            n_sp = [0]

            def chain(ins):
                ins.then_inc(sp_dve, 1)
                n_sp[0] += 1
                dve.wait_ge(sp_dve, n_sp[0])

            lam = pr[:, G_LAM:G_LAM + 4]
            chain(V_.scalar_tensor_tensor(sm[:, 0:4], lam, -1.0, lam, ALU.mult, ALU.max))
            dve.wait_ge(sp_act, 1)
            e = sm[:, 4:8]
            chain(V_.tensor_scalar(sm[:, 8:12], e, 2.0, None, ALU.add))
            chain(V_.reciprocal(sm[:, 12:16], sm[:, 8:12]))
            chain(V_.tensor_tensor(sm[:, 8:12], e, sm[:, 12:16], ALU.mult))
            chain(V_.tensor_tensor(sm[:, 12:16], sm[:, 8:12], sm[:, 8:12], ALU.mult))
            chain(V_.tensor_scalar(sm[:, 16:20], sm[:, 12:16], 1.0 / 19, 1.0 / 17, ALU.mult, ALU.add))
            for k in (15, 13, 11, 9, 7, 5, 3, 1):
                chain(V_.tensor_tensor(sm[:, 20:24], sm[:, 16:20], sm[:, 12:16], ALU.mult))
                chain(V_.tensor_scalar(sm[:, 16:20], sm[:, 20:24], 1.0 / k, None, ALU.add))
            chain(V_.scalar_tensor_tensor(sm[:, 8:12], sm[:, 8:12], 2.0, sm[:, 16:20], ALU.mult, ALU.mult))
            chain(V_.tensor_scalar(sm[:, 12:16], lam, -1.0, 0.0, ALU.mult, ALU.max))
            chain(V_.tensor_tensor(sm[:, 16:20], sm[:, 8:12], sm[:, 12:16], ALU.add))
            chain(V_.tensor_scalar(sm[:, 20:24], sm[:, 16:20], 8.0, None, ALU.mult))
            chain(V_.tensor_scalar(sm[:, 24:28], sm[:, 16:20], -8.0, None, ALU.mult))
            assert n_sp[0] == SP_COUNT, n_sp[0]

            dve.wait_ge(z_evac, 28)
            for c in range(LC):
                w = lambda k: pr[:, G_CW + 4 * c + k:G_CW + 4 * c + k + 1]
                V_.tensor_scalar(xc[:, c, :], lr[:, c, :], w(3), pr[:, G_CB + c:G_CB + c + 1], ALU.mult, ALU.add
                                 ).then_inc(l_cv, 1)
                for s in (1, 2, 3):
                    dve.wait_ge(l_cv, 3 * c + s)
                    m = V_.scalar_tensor_tensor(xc[:, c, s:S], lr[:, c, 0:S - s], w(3 - s), xc[:, c, s:S],
                                                ALU.mult, ALU.add)
                    m.then_inc(l_cv if s < 3 else l_conv, 1)
            for c in range(LC):
                dve.wait_ge(l_sig, 2 * c + 2)
                dve.wait_ge(l_gate, 2 * c + 2)
                V_.tensor_tensor(lri[:, c, :], lri[:, c, :], xc[:, c, :], ALU.mult).then_inc(l_ix, 1)
            for c in range(LC):
                dve.wait_ge(l_aa, c + 1)
                V_.scalar_tensor_tensor(xc[:, c, :], xc[:, c, :], 1.0, lrt[:, c % 2, :], ALU.add, ALU.mult
                                        ).then_inc(l_t2, 1)
            for c in range(LC):
                dve.wait_ge(l_mult, c + 1)
                V_.memset(xc[:, c, 0:1], 1.0).then_inc(l_b, 1)
                dve.wait_ge(l_b, 2 * c + 1)
                V_.tensor_tensor(lri[:, c, :], lri[:, c, :], xc[:, c, :], ALU.mult).then_inc(l_b, 1)
                dve.wait_ge(l_b, 2 * c + 2)
                V_.tensor_tensor_scan(lr[:, c, :], lra[:, c, :], lri[:, c, :], 0.0, ALU.mult, ALU.add
                                      ).then_inc(l_scan, 1)

            dve.wait_ge(m_sq, 2)
            V_.tensor_tensor(lacc[:, 0, :], lsq[:, 0, :], lsq[:, 1, :], ALU.add).then_inc(m_acc, 1)
            dve.wait_ge(m_sq, 3)
            dve.wait_ge(m_acc, 1)
            V_.tensor_tensor(lacc[:, 0, :], lacc[:, 0, :], lsq[:, 0, :], ALU.add).then_inc(m_acc, 1)
            dve.wait_ge(m_sq, 5)
            V_.tensor_tensor(lacc[:, 1, :], lsq[:, 1, :], lsq[:, 0, :], ALU.add).then_inc(m_acc, 1)
            for c in range(KVC):
                V_.tensor_scalar(kvlat[:, c, :], kvlat[:, c, :], pr[:, G_KVN + c:G_KVN + c + 1], None, ALU.mult
                                 ).then_inc(m_g, 1)
            for c in range(QRC):
                V_.tensor_scalar(qlat[:, c, :], qlat[:, c, :], pr[:, G_QN + c:G_QN + c + 1], None, ALU.mult
                                 ).then_inc(m_g, 1)
            dve.wait_ge(m_ssq, 1)
            V_.tensor_scalar(msq[:, 0:8], ps[:, 0, 0:8], 1.0 / QR, EPS, ALU.mult, ALU.add)
            V_.tensor_scalar(msq[:, 8:16], ps[:, 0, 8:16], 1.0 / KVR, EPS, ALU.mult, ALU.add).then_inc(m_ms, 1)
            dve.wait_ge(m_sd, 1)
            V_.reciprocal(rsd[:], rsd[:]).then_inc(m_rs, 1)
            dve.wait_ge(m_rope, 1)
            V_.tensor_copy(K[:, :, :, MNOPE:MQK],
                           ps[:, 1, 0:NT * ROPE].rearrange("p (t d) -> p t d", t=NT).unsqueeze(2)
                           .to_broadcast([P, NT, MH, ROPE])).then_inc(m_krope, 1)
            for c in range(KVC):
                dve.wait_ge(m_hi, c + 1)
                V_.tensor_tensor(kvl_lo[:, c, :], kvlat[:, c, :], kvl_hi[:, c, :].bitcast(F32), ALU.subtract
                                 ).then_inc(m_lo, 1)
            dve.wait_ge(m_up, 2 * NT)
            for c in range(QRC):
                dve.wait_ge(m_hi, KVC + c + 1)
                V_.tensor_tensor(ql_lo[:, c, :], qlat[:, c, :], ql_hi[:, c, :].bitcast(F32), ALU.subtract
                                 ).then_inc(m_lo, 1)
            for n in range(2 * NT):
                dve.wait_ge(h_sq, n + 1)
                V_.tensor_reduce(ss[:, 8 * n:8 * n + 8], hsq[:, n % NT], AX, ALU.add).then_inc(h_red, 1)
            dve.wait_ge(h_red, 2 * NT)
            V_.tensor_scalar(ss[:], ss[:], 1.0 / MQK, EPS, ALU.mult, ALU.add).then_inc(h_ms, 1)
            dve.wait_ge(h_sd, 1)
            V_.reciprocal(rs[:], rs[:]).then_inc(h_rs, 1)
            dve.wait_ge(h_rs, 1)
            V_.tensor_scalar(rs[:, 0:64], rs[:, 0:64], float(MQK) ** -0.5, None, ALU.mult).then_inc(h_rs, 1)
            dve.wait_ge(h_rs, 2)
            for t in range(KT_POOL, NT):
                scale_keys(V_, t).then_inc(k_nrm, 1)
            for t in range(NT):
                V_.tensor_tensor(Q[:, t], Q[:, t], rs[:, 8 * t:8 * t + 8].unsqueeze(2).to_broadcast([P, MH, MQK]),
                                 ALU.mult).then_inc(q_nrm, 1)
            dve.wait_ge(q_nrm, NT)
            gain_rope(V_, Q, G_GQ).then_inc(q_nrm, 1)
            rotate(dve, V_, Q, 0, q_nrm, NT + 1)

            dve.wait_ge(k_nrm, NT + 7)
            dve.wait_ge(q_nrm, NT + 7)
            with dve.Fori(0, MH // 2) as it:
                for h_ in range(2):
                    for j, (src, dst) in enumerate(((Q, stq), (K, stk))):
                        dve.wait_ge(a_tr, it * 4 + 2 * h_ + j)
                        V_.tensor_copy(dst[:], src[:, :, bass.ds(it * 2 + h_, 1), :].rearrange("p t o d -> p t (o d)")
                                       ).then_inc(a_st, 1)
                for u in range(16):
                    h_, i = u // 8, u % 8
                    n = (i + 1) * P
                    s_ps = bank(2 * (u % 2), 2)
                    dve.wait_ge(a_qk, it * 16 + u + 1)
                    V_.tensor_tensor(s_ps[:, i * P:n], s_ps[:, i * P:n], causal, ALU.add).then_inc(a_diag, 1)
                    dve.wait_ge(a_diag, it * 16 + u + 1)
                    V_.tensor_reduce(nmx[:, i:i + 1], s_ps[:, 0:n], AX, ALU.max, negate=True).then_inc(a_max, 1)
                    if u in (9, 15):
                        dve.wait_ge(a_exp, it * 16 + (9 if u == 9 else 17))
                        V_.reciprocal(rinv[:], sums[:, 8 * (u // 15):8 * (u // 15) + 8]).then_inc(a_ri, 1)
                        dve.wait_ge(a_ri, (it * 2 + (1 if u == 9 else 2)) + 1)
                        dve.wait_ge(a_pv, (it * 16 + (8 if u == 9 else 16)) + 1)
                        h_ = u // 15
                        V_.tensor_tensor(
                            mla_out[:, :, bass.ds((it * 2 + h_) * MV, MV)],
                            bank(6).rearrange("p (t d) -> p t d", t=NT),
                            rinv[:].unsqueeze(2).to_broadcast([P, NT, MV]), ALU.mult).then_inc(a_out, 1)

            for c in range(4):
                dve.wait_ge(x_hi, c + 1)
                V_.tensor_tensor(U_lo[:, c, :], lr[:, c, :], U_hi[:, c, :].bitcast(F32), ALU.subtract).then_inc(x_lo, 1)
            for n in range(8):
                dve.wait_ge(x_hi, 4 + n + 1)
                cols = slice((n % 2) * HALF, (n % 2 + 1) * HALF)
                V_.tensor_tensor(U_lo[:, 4 + n // 2, cols], ps[:, n % 4, :], U_hi[:, 4 + n // 2, cols].bitcast(F32),
                                 ALU.subtract).then_inc(x_lo, 1)

            def add_out(k):
                for n in range(16):
                    dve.wait_ge(o_ready, 16 * k + n + 1)
                    dve.wait_ge(h_in, 16 * (k + 1))
                    cols = slice((n % 2) * HALF, (n % 2 + 1) * HALF)
                    V_.tensor_tensor(H[:, n // 2, cols], H[:, n // 2, cols], ps[:, n % 4 + 4, :], ALU.add
                                     ).then_inc(o_added, 1)
                    if n % 2:
                        add_squares(2 * k + 1, n // 2 - 1)

            add_out(0)
            norm(1, G_MLP0)
            mlp_dve(dve, add_squares, 0)
            norm(2, G_MIX1)
            V_.tensor_scalar(q_gain8, pr[0:DK, G_Q1:G_Q1 + 1], float(DK) ** -0.5, None, ALU.mult)
            def compress_in(u):
                if u == 0:
                    dve.wait_ge(t4_in, 128)
                if u >= 2:
                    dve.wait_ge(c_mm, u - 1)
                src = T4[:, u, 0:1]
                src = bass.AP(src.tensor, src.offset, [list(src.ap[0]), [2, 16], [16, NCMP]])
                V_.tensor_tensor(TP[:, u % 2], src,
                                 pr[:, G_POS + 16 * (u // 2):G_POS + 16 * (u // 2 + 1)].unsqueeze(2)
                                 .to_broadcast([P, 16, NCMP]), ALU.add).then_inc(c_tp, 1)

            for n in range(NT + 2):
                if n == 4:
                    compress_in(0)
                    compress_in(1)
                dve.wait_ge(h_sq, n + 1 + HD0)
                dst = ss[:, 16 * n:16 * n + 16] if n < NT else ssk[:, 16 * (n - NT):16 * (n - NT) + 16]
                V_.tensor_reduce(dst, SQ1[:, n % 2, :].rearrange("p (h d) -> p h d", d=DK), AX, ALU.add
                                 ).then_inc(h_red, 1)
            dve.wait_ge(h_red, NT + 2 + HD0)
            V_.tensor_scalar(ss[:], ss[:], 1.0 / DK, EPS, ALU.mult, ALU.add).then_inc(h_ms, 1)
            V_.tensor_scalar(ssk[:], ssk[:], 1.0 / DK, EPS, ALU.mult, ALU.add).then_inc(h_ms, 1)
            compress_in(2)
            compress_in(3)
            dve.wait_ge(h_sd, 2 + 1)
            V_.reciprocal(rs[:], rs[:]).then_inc(h_rs, 1)
            V_.reciprocal(rsk[:], rsk[:]).then_inc(h_rs, 1)
            dve.wait_ge(h_rs, 2 + 2)
            for j in range(2):
                V_.tensor_tensor(KV[:, :, 2 * j], KV[:, :, 2 * j],
                                 rsk[:, 16 * j:16 * j + 16].rearrange("p (t g) -> p t g", g=NG).unsqueeze(3)
                                 .to_broadcast([P, NT, NG, DK]), ALU.mult).then_inc(k_sc, 1)
            dve.wait_ge(c_hT, 1)
            V_.tensor_copy(HCT[:].rearrange("p u k n -> p (u k n)"), ps[:, 4, 0:8 * NCMP]).then_inc(c_hTev, 1)
            dve.wait_ge(c_out, 1)
            o5 = ps[0:NCMP, 5, 0:4 * DK].rearrange("p (u d) -> p u d", u=4)
            V_.tensor_copy(CKN[:], o5[:, 0:2]).then_inc(c_sm, 1)
            dve.wait_ge(c_sm, 1)
            V_.tensor_tensor(CTMP[:], CKN[:], CKN[:], ALU.mult).then_inc(c_sm, 1)
            dve.wait_ge(c_sm, 2)
            V_.tensor_reduce(cmx[0:NCMP, 0:2], CTMP[:], AX, ALU.add).then_inc(c_sm, 1)
            dve.wait_ge(c_sm, 3)
            V_.tensor_scalar(cmx[0:NCMP, 2:4], cmx[0:NCMP, 0:2], 1.0 / DK, EPS, ALU.mult, ALU.add).then_inc(c_sm, 1)
            dve.wait_ge(c_sd, 1)
            V_.reciprocal(cmx[0:NCMP, 6:8], cmx[0:NCMP, 4:6]).then_inc(c_sm, 1)
            dve.wait_ge(c_sm, 5)
            V_.tensor_tensor(CKN[:], CKN[:], cmx[0:NCMP, 6:8].unsqueeze(2).to_broadcast([NCMP, NG, DK]), ALU.mult
                             ).then_inc(c_sm, 1)
            V_.tensor_copy(CV[:], o5[:, 2:4]).then_inc(c_sm, 1)
            dve.wait_ge(c_gate, 1)
            V_.tensor_copy(GATE[:].rearrange("p t n -> p (t n)"), ps[:, 7, 0:NT * GATES]).then_inc(c_sm, 1)
            dve.wait_ge(const_in, 48)
            dve.wait_ge(c_sm, 8)

            with dve.Fori(0, NG) as g:
                def gate(h, branch):
                    return GATE[:, :, bass.ds((g * HPG + h) * 3 + branch, 1)]

                def head_out(h):
                    return ZQ[:, :, bass.ds((g * HPG + h) * DK, DK)]

                def finish(h, par, branch, exp, ri, pv, o):
                    n = g * 16 + h + (1 if branch == 2 else 9)
                    dve.wait_ge(exp, g * 64 + h * 8 + 9)
                    V_.reciprocal(rinv[:], sums[:, 8 * par:8 * par + 8]).then_inc(ri, 1)
                    dve.wait_ge(ri, g * 8 + h + 3)
                    if branch == 2:
                        dve.wait_ge(e_o, g * 8 + h + 2)
                    V_.tensor_tensor(coef[:].unsqueeze(2), rinv[:].unsqueeze(2), gate(h, branch), ALU.mult).then_inc(f_co, 1)
                    dve.wait_ge(f_co, n)
                    dve.wait_ge(pv, g * 64 + h * 8 + 9)
                    V_.tensor_tensor(TMPO[:], bank(6).rearrange("p (t d) -> p t d", t=NT),
                                     coef[:].unsqueeze(2).to_broadcast([P, NT, DK]), ALU.mult).then_inc(f_tmp, 1)
                    dve.wait_ge(f_tmp, n)
                    V_.tensor_tensor(head_out(h), head_out(h), TMPO[:], ALU.add).then_inc(o, 1)

                def head_scores(h, par, first=False):
                    def biased(i):
                        u = g * 64 + h * 8 + i
                        nk = (min(i, WB) + 1) * P
                        c0 = RW - nk
                        if i == 0:
                            dve.wait_ge(rw_in[par], g * 64 + (h - par) * 8 + 16)
                        dve.wait_ge(w_qk, u + 1)
                        dve.wait_ge(w_exp, u + 1 if i == 0 and first else u)
                        alone(dve)
                        V_.tensor_tensor_reduce(SW[:, i % 2, 0:nk], bank(2 * (i % 2), 2)[:, 0:nk],
                                                RWB[:, par, c0:RW], -1.0, 3.0e38, ALU.add, ALU.min, nmx[:, i:i + 1]
                                                ).then_inc(w_max, 1)

                    biased(0)
                    biased(1)
                    if not first:
                        finish(h - 1, 1 - par, 2, w_exp, w_ri, w_pv, w_o)
                    biased(2)
                    dve.wait_ge(e_qk, g * 8 + h + 1)
                    dve.wait_ge(e_tp, g * 8 + h + 1)
                    cb = CB[:, bass.ds(h, 1), 0:1]
                    cb = bass.AP(cb.tensor, cb.offset, [list(cb.ap[0]), [8, NT], [1, NCMP]])
                    V_.tensor_tensor(PC[:], bank(7)[:, 0:NT * NCMP].rearrange("p (t n) -> p t n", t=NT), cb, ALU.add
                                     ).then_inc(e_dve, 1)
                    dve.wait_ge(e_dve, g * 24 + h * 3 + 1)
                    V_.tensor_reduce(cmx[:], PC[:], AX, ALU.max).then_inc(e_dve, 1)
                    dve.wait_ge(e_dve, g * 24 + h * 3 + 2)
                    V_.tensor_tensor(PC[:], PC[:], cmx[:].unsqueeze(2).to_broadcast([P, NT, NCMP]), ALU.subtract
                                     ).then_inc(e_dve, 1)
                    biased(3)
                    n0 = (g * HPG + h) * 4
                    dve.wait_ge(e_exp, g * 8 + h + 1)
                    V_.tensor_reduce(cmx[:], PC[:], AX, ALU.add).then_inc(e_norm, 1)
                    dve.wait_ge(e_norm, n0 + 1)
                    V_.reciprocal(coef[:], cmx[:]).then_inc(e_norm, 1)
                    dve.wait_ge(e_norm, n0 + 2)
                    V_.tensor_tensor(cmx[:], coef[:], cs[:, C_V0:C_V0 + NT], ALU.mult).then_inc(e_norm, 1)
                    dve.wait_ge(e_norm, n0 + 3)
                    V_.tensor_tensor(PC[:], PC[:], cmx[:].unsqueeze(2).to_broadcast([P, NT, NCMP]), ALU.mult
                                     ).then_inc(e_norm, 1)
                    dve.wait_ge(e_norm, n0 + 4)
                    V_.scalar_tensor_tensor(PC[:], PC[:], 1.17549435e-38, PC[:], ALU.is_ge, ALU.mult).then_inc(e_p, 1)
                    dve.wait_ge(e_p, g * 8 + h + 1)
                    biased(4)
                    dve.wait_ge(e_acc, g * 9 + h + 1)
                    V_.tensor_tensor(PACC[:], PACC[:], PC[:], ALU.add).then_inc(e_acc, 1)
                    for i in range(5, NT):
                        if i == 7:
                            dve.wait_ge(e_pv, g * 8 + h + 2)
                            V_.tensor_tensor(head_out(h), bank(7).rearrange("p (t d) -> p t d", t=NT),
                                             gate(h, 0).to_broadcast([P, NT, DK]), ALU.mult).then_inc(e_o, 1)
                        biased(i)

                dve.wait_ge(g_in, g * 16 + 16)
                dve.wait_ge(i_tp, g * 1 + 1)
                V_.memset(PACC[:], 0.0).then_inc(e_acc, 1)
                head_scores(0, 0, True)
                with dve.Fori(0, HPG // 2 - 1) as t:
                    head_scores(t * 2 + 1, 1)
                    head_scores(t * 2 + 2, 0)
                head_scores(HPG - 1, 1)
                finish(HPG - 1, 1, 2, w_exp, w_ri, w_pv, w_o)

                dve.wait_ge(i_mm, g + 1)
                dve.wait_ge(w_exp, g * 64 + 65)
                n0 = g * (3 + 2 * NT)
                A_ = cs[:, C_ROPE:C_ROPE + 128].rearrange("p (t n) -> p t n", t=NT)
                B_ = cs[:, C_ROPE + 128:C_ROPE + 256].rearrange("p (t n) -> p t n", t=NT)
                V_.tensor_tensor(SCO[:], bank(7)[:, 0:NT * NSEL].rearrange("p (t n) -> p t n", t=NT), A_, ALU.mult
                                 ).then_inc(i_dve, 1)
                dve.wait_ge(i_dve, n0 + 1)
                V_.tensor_tensor(SCO[:], SCO[:], B_, ALU.add).then_inc(i_dve, 1)
                dve.wait_ge(i_dve, n0 + 2)
                alone(dve)
                for t in range(NT):
                    V_.max(M8[:, t, :], SCO[:, t, :]).then_inc(i_dve, 1)
                for t in range(NT):
                    dve.wait_ge(i_dve, n0 + 3 + t)
                    alone(dve)
                    V_.match_replace(REP[:, t, :], M8[:, t, :], SCO[:, t, :], FILL).then_inc(i_dve, 1)
                dve.wait_ge(i_dve, n0 + 2 + 2 * NT)
                V_.tensor_scalar(REP[:], REP[:], FILL, -1.0, ALU.is_equal, ALU.add).then_inc(i_dve, 1)
                dve.wait_ge(i_dve, n0 + 3 + 2 * NT)
                V_.tensor_scalar(REP[:], REP[:], -NEG, None, ALU.mult).then_inc(i_mask, 1)

                def head_selected(h, par, first=False):
                    for k in range(NT):
                        i = NT - 1 - k
                        u = g * 64 + h * 8 + k
                        nk = (i + 1) * P
                        if k == 0:
                            dve.wait_ge(rs_in[par], g * 64 + (h - par) * 8 + 16)
                        dve.wait_ge(s_qk, u + 1)
                        dve.wait_ge(s_exp, u + 1 if k == 0 and first else u)
                        alone(dve)
                        V_.tensor_tensor_reduce(SS1[:, i % 2, 0:nk], bank(2 * (i % 2), 2)[:, 0:nk],
                                                RSB[:, par, S - nk:S], -1.0, 3.0e38, ALU.add, ALU.min, nmx[:, i:i + 1]
                                                ).then_inc(s_max, 1)
                        if k == 1 and not first:
                            finish(h - 1, 1 - par, 1, s_exp, s_ri, s_pv, s_o)

                head_selected(0, 0, True)
                with dve.Fori(0, HPG // 2 - 1) as t:
                    head_selected(t * 2 + 1, 1)
                    head_selected(t * 2 + 2, 0)
                head_selected(HPG - 1, 1)
                finish(HPG - 1, 1, 1, s_exp, s_ri, s_pv, s_o)

            for n in range(2 * KC):
                dve.wait_ge(x_hi, n + 1 + XL0)
                cols = slice((n % 2) * HALF, (n % 2 + 1) * HALF)
                V_.tensor_tensor(U_lo[:, n // 2, cols], ps[:, n % 4, :], U_hi[:, n // 2, cols].bitcast(F32),
                                 ALU.subtract).then_inc(x_lo, 1)
            add_out(1)
            norm(3, G_MLP1)
            mlp_dve(dve, add_squares, 1)


def layouts(inp):
    import math

    import numpy as np

    a = {k: np.asarray(v) for k, v in inp.items()}
    f = np.float32

    def cols(w, n=COLS):
        out = []
        for c in range(0, w.shape[1], n):
            p = np.zeros((P, KC, n), f)
            part = w[:, c:c + n]
            p[:, :, :part.shape[1]] = part.reshape(KC, P, -1).transpose(1, 0, 2)
            out.append(p.reshape(P, PIECE))
        return out

    def flat(w, kc):
        p = np.zeros((P, PIECE), f)
        v = w.reshape(kc, P, -1).transpose(1, 0, 2).reshape(P, -1)
        p[:, :v.shape[1]] = v
        return p

    pieces = cols(a["hy_w_in"][0])
    ukv = a["mla_w_ukv"][0].reshape(KVR, MH, MNOPE + MV)
    ukv = np.concatenate([ukv[:, :, :MNOPE].reshape(KVR, -1), ukv[:, :, MNOPE:].reshape(KVR, -1)], axis=1)
    pieces.append(flat(ukv, KVC))
    uq = a["mla_w_uq"][0]
    pieces += [flat(uq[:, 384 * j:384 * (j + 1)], QRC) for j in range(2)]
    pieces += cols(a["hy_w_out"][0])

    def mlp(layer):
        w1, w2 = a["mlp_w1"][layer], a["mlp_w2"][layer]
        for g in range(FF // COLS):
            pieces.append(cols(w1[:, g * COLS:(g + 1) * COLS])[0])
            pieces.append(flat(w2[g * COLS:(g + 1) * COLS], COLS // P))

    mlp(0)
    w = a["nsa_w_in"][0]
    n0 = NH * DK
    part = [w[:, n0 + 128 * j:n0 + 128 * (j + 1)] for j in range(6)]
    pieces += cols(w[:, :n0]) + cols(np.concatenate(part[0:2], 1)) + cols(np.concatenate(part[2:4], 1))
    pieces += cols(np.concatenate(part[4:6], 1)) + cols(w[:, n0 + 768:]) + cols(a["nsa_w_out"][0])
    mlp(1)
    assert len(pieces) == N_PIECES
    half = ROPE // 2
    freqs = f(10000.0) ** (-np.arange(half, dtype=f) / f(half))
    ang = np.arange(S).astype(f)[:, None] * freqs[None, :]
    tok = lambda x: x.reshape(NT, P, -1).transpose(1, 0, 2).reshape(P, -1)
    cst = np.zeros((P, N_CST), f)
    cst[:, C_ID:C_ID + P] = np.eye(P)
    cst[:, C_CAUS:C_CAUS + P] = np.where(np.arange(P)[None, :] <= np.arange(P)[:, None], 0.0, NEG)
    cst[:, C_ROPE:C_ROPE + 128] = tok(np.cos(ang).astype(f))
    cst[:, C_ROPE + 128:C_ROPE + 256] = tok(np.sin(ang).astype(f))
    cs0 = np.arange(NCMP) * 16
    ss0 = np.arange(NSEL) * 64
    ov = np.clip(np.minimum(cs0[:, None] + 32, ss0[None] + 64) - np.maximum(cs0[:, None], ss0[None]), 0, None) / 32
    cst[:NCMP, C_OV:C_OV + NSEL] = ov
    cst[:, C_V0:C_V0 + NT] = tok((np.arange(S) >= 31).astype(f))[::-1, ::-1]
    q = np.arange(S)
    cur = q // 64
    blk = np.arange(NSEL)
    valid = ss0[None] <= q[:, None]
    forced = (blk[None] == 0) | (blk[None] == cur[:, None]) | (blk[None] == cur[:, None] - 1)
    sel = np.concatenate([np.eye(P, dtype=f), tok((valid & ~forced).astype(f)),
                          tok(np.where(valid & forced, 1e4, np.where(valid, 0.0, -1.0)).astype(f))], 1)[::-1]
    n = np.arange(S)
    nf = np.maximum(n, 1).astype(f)
    bucket = 16 + (np.log(nf / f(16)) / f(math.log(64)) * f(16)).astype(np.int32)
    bucket = np.where(n < 16, n, np.minimum(bucket, 31))

    def rows(dist, top):
        m = np.zeros((33, len(dist)), f)
        ok = (dist >= 0) & (dist < top)
        m[bucket[dist[ok]], np.nonzero(ok)[0]] = 1
        m[32, ~ok] = NEG
        return m

    onehot = np.concatenate([rows(S - 1 - np.arange(ES_N), S), rows(639 - np.arange(EW_N), 512),
                             rows(992 - np.arange(1120), S)], 1)
    blkind = np.zeros((NSEL, NG, S), f)
    blkind[np.arange(S) // 64, :, np.arange(S)] = 1
    relx = np.concatenate([a["rel_bias"], np.ones((1, NH), f)], 0)
    vec = lambda x: x.reshape(-1, P).T
    prm = np.zeros((P, N_PRM), f)
    for g, x in ((G_MIX0, a["norm_mix"][0]), (G_MLP0, a["norm_mlp"][0]), (G_MIX1, a["norm_mix"][1]),
                 (G_MLP1, a["norm_mlp"][1]), (G_CB, a["lru_conv_b"][0]), (G_BA, a["lru_ba"][0].reshape(-1)),
                 (G_BX, a["lru_bx"][0].reshape(-1)), (G_LAM, a["lru_lambda"][0]), (G_QN, a["mla_q_norm"][0]),
                 (G_KVN, a["mla_kv_norm"][0])):
        v = vec(x)
        prm[:, g:g + v.shape[1]] = v
    prm[:, G_CW:G_CW + 16] = a["lru_conv_w"][0].reshape(CONV, LC, P).transpose(2, 1, 0).reshape(P, 16)
    prm[:, G_GQ:G_GQ + MQK] = a["mla_qn_q"][0][None]
    prm[:, G_GK:G_GK + MQK] = a["mla_qn_k"][0][None]
    for g, x in ((G_GQC, a["mla_qn_q"][0]), (G_GKC, a["mla_qn_k"][0])):
        prm[:MQK, g] = np.concatenate([x[:MNOPE], np.ones(ROPE, f)])
    prm[:DK, G_Q1] = a["nsa_q_norm"][0]
    prm[:DK, G_K1:G_K1 + 3] = a["nsa_k_norm"][0].T
    for j, x in enumerate((a["nsa_cmp_pos_k"][0], a["nsa_cmp_pos_v"][0])):
        prm[:, G_POS + 16 * j:G_POS + 16 * (j + 1)] = x.reshape(16, 2 * DK).T
    gatew = np.zeros((P, 2, LC, P), f)
    for j, x in enumerate((a["lru_wa"][0], a["lru_wx"][0])):
        for b in range(8):
            o = b % 2 * 64
            gatew[o:o + 64, j, b // 2, o:o + 64] = x[b]
    w1c = np.stack([a["nsa_cmp_w1_k"][0], a["nsa_cmp_w1_v"][0]]).reshape(2, 16, P, CMP_HID).transpose(2, 0, 1, 3)
    w2c = np.stack([a["nsa_cmp_w2_k"][0], a["nsa_cmp_w2_v"][0]]).reshape(2, 2, P, DK).transpose(2, 0, 1, 3)
    xT = a["x"][0].T.reshape(KC, P, S).transpose(1, 0, 2)
    arrays = dict(xT=xT, pieces=np.stack(pieces), cst=cst, sel=sel, prm=prm, gatew=gatew, relx=relx, onehot=onehot,
                  w1c=w1c, w2c=w2c, blkind=blkind)
    return {k: np.ascontiguousarray(v, dtype=f) for k, v in arrays.items()}


def kernel(**inputs):
    import numpy as np
    import concourse.bacc as bacc
    from concourse.bass_utils import run_bass_kernel_spmd

    arrays = layouts(inputs)
    nc = bacc.Bacc("TRN2", target_bir_lowering=False, num_devices=1)
    args = [nc.dram_tensor("in_" + k, v.shape, F32, kind="ExternalInput").ap() for k, v in arrays.items()]
    out = nc.dram_tensor("out_h", (P, KC, S), F32, kind="ExternalOutput").ap()
    build_program(nc, *args, out)
    r = run_bass_kernel_spmd(nc, [{"in_" + k: v for k, v in arrays.items()}], core_ids=[0])
    h = r.results[0]["out_h"]
    return np.ascontiguousarray(h.transpose(1, 0, 2).reshape(1, D, S).transpose(0, 2, 1))
```
